# Optimizing a Trainium2 kernel written in Bass

```python
import jax
import jax.numpy as jnp
from jax import lax
import numpy as np

D_MODEL = 1024
BATCH = 1
SEQ = 1024
DEPTH = 2

CTX_LEN = 256
GRID_W = 64
NORM_EPS = 1e-6
N_MOD = 6

MIX_WIDTH = D_MODEL
SC_WIDTH = MIX_WIDTH // 2
SC_CONV = 3
SC_PAD_LEFT = 1
GLA_HEADS = 4
GLA_VALUE = MIX_WIDTH // 2
GLA_DV = GLA_VALUE // GLA_HEADS
GLA_DK = GLA_DV // 2
GLA_KEY = GLA_HEADS * GLA_DK
GLA_RANK = 16
GLA_TAU = 16.0
GLA_CHUNK = 64
EVEN_SIZES = (SC_WIDTH, SC_WIDTH, SC_WIDTH, GLA_KEY, GLA_VALUE)
EVEN_KV_SIZES = (GLA_KEY, GLA_VALUE, GLA_RANK, GLA_RANK)
EVEN_KV_START = 3 * SC_WIDTH + GLA_KEY + GLA_VALUE
EVEN_IN = EVEN_KV_START + GLA_KEY + GLA_VALUE + 2 * GLA_RANK
EVEN_OUT = SC_WIDTH + GLA_VALUE
LRU_WIDTH = MIX_WIDTH // 2
LRU_HEADS = 4
LRU_HEAD_DIM = LRU_WIDTH // LRU_HEADS
LRU_CONV = 4
LRU_PAD_LEFT = 2
LRU_C = 8.0
SG_WIDTH = MIX_WIDTH // 2
SG_GROUPS = 4
SG_GROUP_DIM = SG_WIDTH // SG_GROUPS
SG_CHUNK = 128
ODD_SIZES = (LRU_WIDTH, LRU_WIDTH, SG_WIDTH, SG_WIDTH)
ODD_IN = 2 * LRU_WIDTH + 2 * SG_WIDTH
ODD_OUT = LRU_WIDTH + SG_WIDTH
N_EXPERTS = 16
EXPERT_HIDDEN = D_MODEL
EC_CAPACITY = 2

kernel_name = 'hybrid_diffusion_conv_gla_rglru_sgmlp_ec'

def _split(z, sizes):
    return jnp.split(z, [int(s) for s in np.cumsum(sizes)[:-1]], axis=-1)

def rmsnorm(x, g):
    xf = x.astype(jnp.float32)
    y = xf * lax.rsqrt(jnp.mean(xf * xf, axis=-1, keepdims=True) + NORM_EPS)
    return (y * g.astype(jnp.float32)).astype(x.dtype)

def layernorm(x, g):
    xf = x.astype(jnp.float32)
    xc = xf - jnp.mean(xf, axis=-1, keepdims=True)
    y = xc * lax.rsqrt(jnp.mean(xc * xc, axis=-1, keepdims=True) + NORM_EPS)
    return (y * g.astype(jnp.float32)).astype(x.dtype)

def modulate(h, shift, scale):
    return h * (1 + scale) + shift

def dwconv(x, w, b, pad_left):
    width = w.shape[0]
    length = x.shape[-2]
    pad = [(0, 0)] * (x.ndim - 2) + [(pad_left, width - 1 - pad_left), (0, 0)]
    xp = jnp.pad(x, pad)
    y = b
    for j in range(width):
        y = y + w[j] * xp[..., j:j + length, :]
    return y

def _heads(t, n):
    bsz, length, _ = t.shape
    return t.reshape(bsz, length, n, -1).transpose(0, 2, 1, 3)

def gla_chunk_scan(q, k, v, la, s0):
    bsz, heads, length, _ = k.shape
    n = length // GLA_CHUNK

    def blocks(t):
        return t.reshape(bsz, heads, n, GLA_CHUNK, t.shape[-1])

    k, v, la = blocks(k), blocks(v), blocks(la)
    b = jnp.cumsum(la, axis=3)
    b_last = b[:, :, :, -1:, :]
    ds = jnp.einsum('bhncd,bhnce->nbhde', k * jnp.exp(b_last - b), v)
    decay = jnp.moveaxis(jnp.exp(b_last[:, :, :, 0, :]), 2, 0)
    with_out = q is not None

    def step(s, inp):
        dec, d = inp
        return dec[..., None] * s + d, (s if with_out else None)

    s_last, s_in = lax.scan(step, s0, (decay, ds))
    if not with_out:
        return None, s_last
    q_d = blocks(q) * jnp.exp(b)
    att = jnp.einsum('bhnid,bhnjd->bhnij', q_d, k * jnp.exp(-b))
    att = jnp.where(jnp.tril(jnp.ones((GLA_CHUNK, GLA_CHUNK), bool)), att, 0.0)
    o = jnp.einsum('bhnij,bhnje->bhnie', att, v) + jnp.einsum('bhncd,nbhde->bhnce', q_d, s_in)
    return o.reshape(bsz, heads, length, v.shape[-1]), s_last

def gla_bidir(q, k, v, la_f, la_b, s0_f, s0_b):
    def flip(t):
        return None if t is None else jnp.flip(t, axis=2)

    o_f, s_f = gla_chunk_scan(q, k, v, la_f, s0_f)
    o_b, s_b = gla_chunk_scan(flip(q), flip(k), flip(v), flip(la_b), s0_b)
    o = None if q is None else o_f + jnp.flip(o_b, axis=2)
    return o, s_f, s_b

def gla_readout(o, g, norm_g):
    bsz, heads, length, dv = o.shape
    o = o * lax.rsqrt(jnp.mean(o * o, axis=-1, keepdims=True) + NORM_EPS)
    o = o.transpose(0, 2, 1, 3).reshape(bsz, length, heads * dv)
    return (o * norm_g.astype(jnp.float32) * jax.nn.silu(g.astype(jnp.float32))).astype(g.dtype)

def _lin_combine(earlier, later):
    a1, b1 = earlier
    a2, b2 = later
    return a1 * a2, a2 * b1 + b2

def linear_scan(a, b, h0, reverse):
    if reverse:
        a, b = jnp.flip(a, axis=1), jnp.flip(b, axis=1)
    b = b.at[:, 0].add(a[:, 0] * h0)
    _, h = lax.associative_scan(_lin_combine, (a, b), axis=1)
    h_last = h[:, -1]
    if reverse:
        h = jnp.flip(h, axis=1)
    return h, h_last

def _blockdiag(x, w, b):
    bsz, length, _ = x.shape
    y = jnp.einsum('bthi,hij->bthj', x.reshape(bsz, length, LRU_HEADS, LRU_HEAD_DIM), w.astype(jnp.float32))
    return y.reshape(bsz, length, LRU_WIDTH) + b.astype(jnp.float32)

def even_mixer(h_lat, h_ctx, w_in, conv_w, conv_b, decay_up, decay_b, norm_g, w_out, need_ctx_out):
    f32 = jnp.float32
    bsz, seq, _ = h_lat.shape
    rows = seq // GRID_W
    scale = GLA_DK ** -0.5

    def kv_decay(zkv):
        k, v, lr_f, lr_b = _split(zkv, EVEN_KV_SIZES)
        la_f = jax.nn.log_sigmoid(lr_f.astype(f32) @ decay_up[0].astype(f32) + decay_b[0].astype(f32)) / GLA_TAU
        la_b = jax.nn.log_sigmoid(lr_b.astype(f32) @ decay_up[1].astype(f32) + decay_b[1].astype(f32)) / GLA_TAU
        return (_heads(k.astype(f32), GLA_HEADS), _heads(v.astype(f32), GLA_HEADS),
                _heads(la_f, GLA_HEADS), _heads(la_b, GLA_HEADS))

    zero = jnp.zeros((bsz, GLA_HEADS, GLA_DK, GLA_DV), f32)
    if need_ctx_out:
        zc = h_ctx @ w_in
        bg_c, cg_c, xa_c, q_c, g_c = _split(zc[..., :EVEN_KV_START], EVEN_SIZES)
        kv_c = kv_decay(zc[..., EVEN_KV_START:])
        qh_c = _heads(q_c.astype(f32), GLA_HEADS) * scale
    else:
        kv_c = kv_decay(h_ctx @ w_in[:, EVEN_KV_START:])
        qh_c = None
    o_c, s_f, s_b = gla_bidir(qh_c, *kv_c, zero, zero)

    z = h_lat @ w_in
    bg, cg, xa, q, g = _split(z[..., :EVEN_KV_START], EVEN_SIZES)
    o, _, _ = gla_bidir(_heads(q.astype(f32), GLA_HEADS) * scale, *kv_decay(z[..., EVEN_KV_START:]), s_f, s_b)
    conv = dwconv((cg * xa).reshape(bsz, rows, GRID_W, SC_WIDTH), conv_w, conv_b, SC_PAD_LEFT)
    conv = conv.reshape(bsz, seq, SC_WIDTH)
    y_lat = jnp.concatenate([bg * conv, gla_readout(o, g, norm_g)], axis=-1) @ w_out
    y_ctx = None
    if need_ctx_out:
        conv_c = dwconv(cg_c * xa_c, conv_w, conv_b, SC_PAD_LEFT)
        y_ctx = jnp.concatenate([bg_c * conv_c, gla_readout(o_c, g_c, norm_g)], axis=-1) @ w_out
    return y_lat, y_ctx

def odd_mixer(h_lat, h_ctx, w_in, conv_w, conv_b, gate_a_w, gate_a_b, gate_x_w, gate_x_b, lam,
              sg_norm_g, sg_w, sg_b, w_out, need_ctx_out):
    f32 = jnp.float32
    bsz = h_lat.shape[0]

    def lru_coeffs(xc, d):
        xf = xc.astype(f32)
        r = jax.nn.sigmoid(_blockdiag(xf, gate_a_w[d], gate_a_b[d]))
        i = jax.nn.sigmoid(_blockdiag(xf, gate_x_w[d], gate_x_b[d]))
        log_a = -LRU_C * r * jax.nn.softplus(-lam[d].astype(f32))
        return jnp.exp(log_a), jnp.sqrt(-jnp.expm1(2.0 * log_a)) * (i * xf)

    def spatial_gate(u, v):
        b, length, _ = u.shape
        n = length // SG_CHUNK
        vb = layernorm(jax.nn.gelu(v), sg_norm_g).reshape(b, n, SG_CHUNK, SG_GROUPS, SG_GROUP_DIM)
        mixed = jnp.einsum('gij,bnjgc->bnigc', sg_w, vb) + sg_b.T[:, :, None]
        return jax.nn.gelu(u) * mixed.reshape(b, length, SG_WIDTH)

    if need_ctx_out:
        xb_c, gb_c, u_c, v_c = _split(h_ctx @ w_in, ODD_SIZES)
    else:
        xb_c = h_ctx @ w_in[:, :LRU_WIDTH]
    xc_c = dwconv(xb_c, conv_w, conv_b, LRU_PAD_LEFT)
    xb, gb, u, v = _split(h_lat @ w_in, ODD_SIZES)
    xc = dwconv(xb, conv_w, conv_b, LRU_PAD_LEFT)
    zero = jnp.zeros((bsz, LRU_WIDTH), f32)
    h_lat_dirs, h_ctx_dirs = [], []
    for d, reverse in enumerate((False, True)):
        h_c, h_c_last = linear_scan(*lru_coeffs(xc_c, d), zero, reverse)
        h_l, _ = linear_scan(*lru_coeffs(xc, d), h_c_last, reverse)
        h_lat_dirs.append(h_l)
        h_ctx_dirs.append(h_c)
    y_rec = (h_lat_dirs[0] + h_lat_dirs[1]).astype(gb.dtype) * jax.nn.gelu(gb)
    y_lat = jnp.concatenate([y_rec, spatial_gate(u, v)], axis=-1) @ w_out
    y_ctx = None
    if need_ctx_out:
        y_rec_c = (h_ctx_dirs[0] + h_ctx_dirs[1]).astype(gb_c.dtype) * jax.nn.gelu(gb_c)
        y_ctx = jnp.concatenate([y_rec_c, spatial_gate(u_c, v_c)], axis=-1) @ w_out
    return y_lat, y_ctx

def ec_moe(h, w_router, w_gate, w_up, w_down):
    bsz, length, dim = h.shape
    cap = EC_CAPACITY * length // N_EXPERTS
    aff = jax.nn.softmax((h @ w_router).astype(jnp.float32), axis=-1)
    g, idx = lax.top_k(jnp.swapaxes(aff, 1, 2), cap)
    xg = jax.vmap(lambda hb, ib: hb[ib])(h, idx)
    hid = jax.nn.silu(jnp.einsum('becd,edf->becf', xg, w_gate)) * jnp.einsum('becd,edf->becf', xg, w_up)
    out = jnp.einsum('becf,efd->becd', hid, w_down) * g.astype(h.dtype)[..., None]
    return jax.vmap(lambda ib, ob: jnp.zeros((length, dim), ob.dtype).at[ib.reshape(-1)].add(ob.reshape(-1, dim)))(idx, out)

def setup_inputs(seed: int = 0) -> dict:
    key = jax.random.key(seed)
    keys = [k for k in jax.random.split(key, 48)]

    def nrm(shape, scale):
        return jax.random.normal(keys.pop(), shape, jnp.float32) * scale

    d = D_MODEL
    ne, no = (DEPTH + 1) // 2, DEPTH // 2
    u = jax.random.uniform(keys.pop(), (no, 2, LRU_WIDTH), jnp.float32, 0.9, 0.999)
    a = u ** (1.0 / LRU_C)
    lam = jnp.log(a) - jnp.log1p(-a)
    return {
        'x': nrm((BATCH, SEQ, d), 1.0),
        'c': nrm((BATCH, d), 1.0),
        'ctx': nrm((BATCH, CTX_LEN, d), 1.0),
        'c_ctx': nrm((d,), 1.0),
        'ada_w': nrm((DEPTH, d, N_MOD * d), 0.5 * d ** -0.5),
        'ada_b': nrm((DEPTH, N_MOD * d), 0.02),
        'norm_mix_g': 1.0 + nrm((DEPTH, d), 0.02),
        'norm_ffn_g': 1.0 + nrm((DEPTH, d), 0.02),
        'norm_final_g': 1.0 + nrm((d,), 0.02),
        'ev_w_in': nrm((ne, d, EVEN_IN), d ** -0.5),
        'ev_conv_w': nrm((ne, SC_CONV, SC_WIDTH), SC_CONV ** -0.5),
        'ev_conv_b': nrm((ne, SC_WIDTH), 0.02),
        'ev_decay_up': nrm((ne, 2, GLA_RANK, GLA_KEY), GLA_RANK ** -0.5),
        'ev_decay_b': 1.0 + nrm((ne, 2, GLA_KEY), 0.5),
        'ev_norm_g': 1.0 + nrm((ne, GLA_VALUE), 0.02),
        'ev_w_out': nrm((ne, EVEN_OUT, d), EVEN_OUT ** -0.5),
        'od_w_in': nrm((no, d, ODD_IN), d ** -0.5),
        'od_conv_w': nrm((no, LRU_CONV, LRU_WIDTH), LRU_CONV ** -0.5),
        'od_conv_b': nrm((no, LRU_WIDTH), 0.02),
        'od_gate_a_w': nrm((no, 2, LRU_HEADS, LRU_HEAD_DIM, LRU_HEAD_DIM), LRU_HEAD_DIM ** -0.5),
        'od_gate_a_b': nrm((no, 2, LRU_WIDTH), 0.02),
        'od_gate_x_w': nrm((no, 2, LRU_HEADS, LRU_HEAD_DIM, LRU_HEAD_DIM), LRU_HEAD_DIM ** -0.5),
        'od_gate_x_b': nrm((no, 2, LRU_WIDTH), 0.02),
        'od_lambda': lam,
        'od_sg_norm_g': 1.0 + nrm((no, SG_WIDTH), 0.02),
        'od_sg_w': nrm((no, SG_GROUPS, SG_CHUNK, SG_CHUNK), SG_CHUNK ** -0.5),
        'od_sg_b': 1.0 + nrm((no, SG_GROUPS, SG_CHUNK), 0.1),
        'od_w_out': nrm((no, ODD_OUT, d), ODD_OUT ** -0.5),
        'moe_router': nrm((DEPTH, d, N_EXPERTS), d ** -0.5),
        'moe_w_gate': nrm((DEPTH, N_EXPERTS, d, EXPERT_HIDDEN), d ** -0.5),
        'moe_w_up': nrm((DEPTH, N_EXPERTS, d, EXPERT_HIDDEN), d ** -0.5),
        'moe_w_down': nrm((DEPTH, N_EXPERTS, EXPERT_HIDDEN, d), EXPERT_HIDDEN ** -0.5),
    }

def reference(x, c, ctx, c_ctx, ada_w, ada_b, norm_mix_g, norm_ffn_g, norm_final_g,
              ev_w_in, ev_conv_w, ev_conv_b, ev_decay_up, ev_decay_b, ev_norm_g, ev_w_out,
              od_w_in, od_conv_w, od_conv_b, od_gate_a_w, od_gate_a_b, od_gate_x_w, od_gate_x_b,
              od_lambda, od_sg_norm_g, od_sg_w, od_sg_b, od_w_out,
              moe_router, moe_w_gate, moe_w_up, moe_w_down):
    x_lat, x_ctx = x, ctx
    s_lat = jax.nn.silu(c)
    s_ctx = jax.nn.silu(c_ctx)
    for l in range(DEPTH):
        last = l == DEPTH - 1
        mod = jnp.split((s_lat @ ada_w[l] + ada_b[l])[:, None, :], N_MOD, axis=-1)
        mod_c = jnp.split(s_ctx @ ada_w[l] + ada_b[l], N_MOD, axis=-1)
        h_lat = modulate(rmsnorm(x_lat, norm_mix_g[l]), mod[0], mod[1])
        h_ctx = modulate(rmsnorm(x_ctx, norm_mix_g[l]), mod_c[0], mod_c[1])
        i = l // 2
        if l % 2 == 0:
            y_lat, y_ctx = even_mixer(h_lat, h_ctx, ev_w_in[i], ev_conv_w[i], ev_conv_b[i], ev_decay_up[i],
                                      ev_decay_b[i], ev_norm_g[i], ev_w_out[i], not last)
        else:
            y_lat, y_ctx = odd_mixer(h_lat, h_ctx, od_w_in[i], od_conv_w[i], od_conv_b[i], od_gate_a_w[i],
                                     od_gate_a_b[i], od_gate_x_w[i], od_gate_x_b[i], od_lambda[i],
                                     od_sg_norm_g[i], od_sg_w[i], od_sg_b[i], od_w_out[i], not last)
        x_lat = x_lat + mod[2] * y_lat
        h_lat = modulate(rmsnorm(x_lat, norm_ffn_g[l]), mod[3], mod[4])
        x_lat = x_lat + mod[5] * ec_moe(h_lat, moe_router[l], moe_w_gate[l], moe_w_up[l], moe_w_down[l])
        if not last:
            x_ctx = x_ctx + mod_c[2] * y_ctx
            h_ctx = modulate(rmsnorm(x_ctx, norm_ffn_g[l]), mod_c[3], mod_c[4])
            x_ctx = x_ctx + mod_c[5] * ec_moe(h_ctx, moe_router[l], moe_w_gate[l], moe_w_up[l], moe_w_down[l])
    return rmsnorm(x_lat, norm_final_g)


_drawn_inputs = setup_inputs


def setup_inputs(seed=0):
    import zlib

    import numpy as np

    out = dict(_drawn_inputs(seed))
    spreads = {}
    factors = {'norm_mix_g': 3.745,
     'norm_ffn_g': 7.032,
     'norm_final_g': 23.503,
     'ev_conv_b': 8.0,
     'ev_norm_g': 8.0,
     'od_gate_a_b': 188.912,
     'od_gate_x_b': 155.094,
     'od_sg_norm_g': 48.883,
     'od_sg_b': 25.415,
     'od_conv_b': 4.881}
    for name, (base, spread) in spreads.items():
        noise = np.random.default_rng([zlib.crc32(name.encode()), seed]).standard_normal(out[name].shape)
        drawn = base * np.exp(spread * noise) if base else spread * noise
        out[name] = jnp.asarray(drawn.astype(out[name].dtype))
    for name, factor in factors.items():
        out[name] = (out[name] * factor).astype(out[name].dtype)
    return out
```

```python
from contextlib import ExitStack

import concourse.bass as bass
from concourse import mybir

F32 = mybir.dt.float32
U32 = mybir.dt.uint32
ALU = mybir.AluOpType
ACT = mybir.ActivationFunctionType
AXX = mybir.AxisListType.X

P = 128
D = 1024
KC = D // P
TL = 8
TC = 2
NT = TL + TC
T = NT * P
LAT = TL * P
CTX = TC * P
BANK = 512
EPS = 1e-6

HEADS = 4
DK = 64
CHUNK = 64
NCH = T // CHUNK
TAU = 16.0
GRID = 64
RANK = 16
LRU_C = 8.0

NE = 16
CAPL = 2 * LAT // NE
CAPC = 2 * CTX // NE
UNIT = 2048
WS = 3
EU = 12

E_BG, E_CG, E_XA, E_Q, E_G, E_K, E_V, E_LR = 0, 512, 1024, 1536, 1792, 2304, 2560, 3072
O_XB, O_GB, O_U, O_V = 0, 512, 1024, 1536

VEC = {}
_row = 0
for _name, _n in (("c", 8), ("c_ctx", 8), ("mix_g", 16), ("ffn_g", 16), ("ev_conv_w", 12), ("ev_conv_b", 4),
                  ("decay_b", 4), ("ev_norm_g", 4), ("od_conv_w", 16), ("od_conv_b", 4), ("gate_a_b", 8),
                  ("gate_x_b", 8), ("lam", 8), ("sg_norm_g", 4)):
    VEC[_name] = _row
    _row += _n
NVEC = _row


def build(nc, I, out):
    ctx = ExitStack()
    with ctx:
        def sem(name):
            return ctx.enter_context(nc.semaphore(name))

        def sb(name, words, dt=F32):
            return ctx.enter_context(nc.sbuf_tensor(name, [P, words], dt))

        ident = sb("ident", P)
        ones = sb("ones", P)
        vcol = sb("vcol", P)
        adab = sb("adab", 96)
        silc = sb("silc", 16)
        modc = sb("modc", 192)
        scg = sb("scg", 64)
        bc = sb("bc", 4 * D)
        maskf = bc[:, 0:P]
        maskb = bc[:, P:2 * P]
        chunk0 = bc[:, 256:256 + T]
        lrT = bc[:, 1536:1536 + T]
        decup = bc[:, 2816:3328]
        wlr = bc[:, 3328:3328 + KC * 2 * RANK]
        rowtmp = bc[:, 3584:4096]
        diag = sb("diag", 2 * P)
        st = sb("st", 64)
        router = sb("router", KC * NE)
        dec = sb("dec", 4 * NCH)
        lruc = sb("lruc", 24)
        epsc = sb("epsc", 1)
        vst = sb("vst", 6 * TL)
        vmv = sb("vmv", 2 * TL)
        vsd = sb("vsd", 2 * TL)
        tkf = diag[:, 0:P]
        gcolT = sb("gcolT", 48)
        icolT = sb("icolT", 48, U32)
        gidx = sb("gidx", 4, U32)
        sm = sb("sm", 4 * NE)

        R_H = sb("R_H", KC * T)
        R_C = sb("R_C", KC * T)
        vrow, adab_row = R_C[:, 0:P], R_C[:, P:2 * P]
        R_M = sb("R_M", 15360)
        R_W = sb("R_W", 11264)

        hT = R_H[:, :].rearrange("p (k t) -> p k t", k=KC)
        cat = R_C[:, :].rearrange("p (k t) -> p k t", k=KC)
        vtok = R_M[:, 0:NT * 512].rearrange("p (t n) -> p t n", t=NT)
        kT = R_M[:, 5120:7680].rearrange("p (c t) -> p c t", c=2)
        qT = R_M[:, 7680:10240].rearrange("p (c t) -> p c t", c=2)
        BX = R_M[:, 10240:15360].rearrange("p (c t) -> p c t", c=4)
        ring = [R_W[:, UNIT * s:UNIT * (s + 1)] for s in range(WS)]
        TMP = [R_W[:, 6144 + T * i:6144 + T * (i + 1)] for i in range(4)]
        wout = R_W[:, 0:8192].rearrange("p (k n) -> p k n", k=KC)
        XB = [R_W[:, 8192 + D * i:8192 + D * (i + 1)] for i in range(2)]
        XN = R_W[:, 10240:11264]
        ktok = R_H[:, 0:2560].rearrange("p (t r d) -> p t r d", t=NT, r=2)
        SIN = R_H[:, 2560:7680].rearrange("p (r c e) -> p r c e", r=2, c=NCH)
        attS = R_H[:, 7680:9728].rearrange("p (b r n) -> p b r n", b=2, r=2)
        TST = R_H[:, 9728:10240].rearrange("p (r b e) -> p r b e", r=2, b=2)
        SQ = [R_W[:, 8192 + 512 * i:8192 + 512 * (i + 1)] for i in range(2)]
        RS = [R_W[:, 9216 + 512 * i:9216 + 512 * (i + 1)] for i in range(2)]
        XC = R_M[:, 0:5120].rearrange("p (c t) -> p c t", c=4)
        HL = R_M[:, 5120:9216].rearrange("p (c t) -> p c t", c=4)
        vln = R_M[:, 9216:13312].rearrange("p (t n) -> p t n", t=TL)
        sgw = R_M[:, 13312:13824].rearrange("p (g n) -> p g n", g=4)
        sgwT = R_M[:, 13824:14336].rearrange("p (g n) -> p g n", g=4)
        sgb = R_M[:, 14848:15360].rearrange("p (g n) -> p g n", g=4)
        cat1 = R_C[:, 0:8192].rearrange("p (k t) -> p k t", k=KC)
        gatew = R_C[:, 8192:10240].rearrange("p (m j) -> p m j", m=16)
        affT = R_M[:, 14336:15360]
        eslot = [R_M[:, UNIT * s:UNIT * (s + 1)] for s in range(7)] + \
                [R_H[:, UNIT * s:UNIT * (s + 1)] for s in range(5)]
        xT = [R_C[:, 1280 * i:1280 * (i + 1)].rearrange("p (k c) -> p k c", k=KC) for i in range(2)]
        hidT = R_C[:, 2560:3840].rearrange("p (k c) -> p k c", k=KC)
        xg = R_C[:, 3840:4864]
        xgc = R_C[:, 4864:5888]
        tmc = R_C[:, 5888:6400]
        silx = R_C[:, 6400:6912]
        hidc = R_C[:, 6912:7424]
        outc = R_C[:, 7424:8448]
        tkv = R_C[:, 9472:9600]
        tki = R_C[:, 9600:9728].bitcast(U32)
        tmo = R_C[:, 8448:9472]
        sil, hid, eout = XB[0], XB[1], XN

        ps = ctx.enter_context(nc.psum_tensor("ps", [P, 8, BANK], F32))

        def wide(s, n):
            return ps[:, 3 * s:3 * s + 3, :].rearrange("p b n -> p (b n)")[:, 0:n]

        xres = nc.dram_tensor("xres", [T, D], F32).ap()
        xnd = nc.dram_tensor("xnd", [T, D], F32).ap()

        x_rows = I["x"].rearrange("b t d -> (b t) d")
        c_rows = I["ctx"].rearrange("b t d -> (b t) d")

        def tok_tile(src_lat, src_ctx, t):
            return src_lat[t * P:(t + 1) * P, :] if t < TL else src_ctx[(t - TL) * P:(t - TL + 1) * P, :]

        ev_in = I["ev_w_in"].rearrange("l (k p) n -> (l p) k n", p=P)
        od_in = I["od_w_in"].rearrange("l (k p) n -> (l p) k n", p=P)

        def ada_unit(l, g, k):
            return ("ada", l, g, k), I["ada_w"][l, k * P:(k + 1) * P, g * 2048:(g + 1) * 2048]

        def col_unit(name, src, col):
            return (name,), src[:, :, col:col + 256]

        stream = [ada_unit(0, 0, k) for k in range(KC)]
        stream += [col_unit("k", ev_in, E_K), col_unit("v0", ev_in, E_V), col_unit("v1", ev_in, E_V + 256)]
        rest_ada = [ada_unit(l, g, k) for l, g in ((0, 1), (0, 2), (1, 0), (1, 1), (1, 2)) for k in range(KC)]
        gaps = [("q", E_Q), ("g0", E_G), ("g1", E_G + 256)] + \
               [(f"{n}{h}", c + 256 * h) for h in range(2) for n, c in (("cg", E_CG), ("xa", E_XA), ("bg", E_BG))]
        for i, (name, col) in enumerate(gaps):
            stream.append(col_unit(name, ev_in, col))
            stream += rest_ada[len(rest_ada) * i // len(gaps):len(rest_ada) * (i + 1) // len(gaps)]
        n_even = len(stream)
        slot_of = [i % WS for i in range(n_even)]
        for name, col, slot in (("xb0", O_XB, 2), ("xb1", O_XB + 256, 0), ("w0", O_V, 0), ("w1", O_V + 256, 1),
                                ("gb0", O_GB, 2), ("gb1", O_GB + 256, 2), ("u0", O_U, 0), ("u1", O_U + 256, 1)):
            stream.append(col_unit(name, od_in, col))
            slot_of.append(slot)
        index = {key: i for i, (key, _) in enumerate(stream)}
        n_in_slot = [slot_of[:i + 1].count(slot_of[i]) for i in range(len(stream))]
        before = [max([j for j in range(i) if slot_of[j] == slot_of[i]], default=None) for i in range(len(stream))]
        assert slot_of[index[("v0",)]] + 1 == slot_of[index[("v1",)]]

        even_jobs = [("lr", 0, T, "act"), ("k", 0, T, "act"), ("k", 1, T, "act")] + \
                    [("dec", i, T, "dve") for i in range(4)] + \
                    [("q", 0, T, "act"), ("q", 1, T, "act")] + [("g", i, T, "act") for i in range(4)]
        for h in range(2):
            even_jobs += [("cg", 2 * h, T, "act"), ("cg", 2 * h + 1, T, "act"), ("xa", 2 * h, T, "dve"),
                          ("xa", 2 * h + 1, T, "dve"), ("bg", 2 * h, T, "dve"), ("bg", 2 * h + 1, T, "dve")]
        odd_order = [("xb", c) for c in range(4)]
        fill = [[("v", 0), ("v", 1), ("v", 2)], [("v", 3), ("v", 4), ("v", 5)], [("v", 6), ("v", 7), ("gb", 0)],
                [("gb", 1)], [("gb", 2)], [("gb", 3), ("u", 0)], [("u", 1), ("u", 2)], [("u", 3)]]
        for it in range(8):
            odd_order += [("ga", it), ("gx", it)] + fill[it]
        odd_jobs = [(k, i, T if k in ("xb", "ga", "gx") else LAT, "act") for k, i in odd_order if k != "v"]

        jobs = even_jobs + odd_jobs
        n_even_jobs = len(even_jobs)
        emptied = {"act": [0], "dve": [0]}
        for j in jobs:
            for e in emptied:
                emptied[e].append(emptied[e][-1] + (j[3] == e))
        job_at = {j[:2] + (i >= n_even_jobs,): i for i, j in enumerate(jobs)}

        norm0 = {"mix0": 0, "ffn0": NT, "mix1": 2 * NT, "ffn1": 3 * NT, "final": 3 * NT + TL}

        def sems(names):
            return [sem(n) for n in names.split()]

        s_const, s_zero, s_small = sems("s_const s_zero s_small")
        s_load = [sem(f"s_load{i}") for i in range(WS)]
        s_used, s_vt, s_vc, s_silc = sems("s_used s_vt s_vc s_silc")
        s_adar, s_adat, s_adac, s_scg = sems("s_adar s_adat s_adac s_scg")
        s_diag, s_bcp, s_bc = sems("s_diag s_bcp s_bc")
        s_dv, s_ac, s_po = sems("s_dv s_ac s_po")
        s_xl = sems("s_xl0 s_xl1")
        s_ss, s_sq, s_xn, s_tp, s_hd, s_ha = sems("s_ss s_sq s_xn s_tp s_hd s_ha")
        s_job, s_ja, s_jd, s_vm, s_ve = sems("s_job s_ja s_jd s_vm s_ve")
        s_dx, s_dl, s_eb, s_qk = sems("s_dx s_dl s_eb s_qk")
        s_kt, s_kc, s_up, s_tst, s_sin = sems("s_kt s_kc s_up s_tst s_sin")
        s_at, s_am, s_o, s_osq, s_ms, s_rs, s_of = sems("s_at s_am s_o s_osq s_ms s_rs s_of")
        s_wo = sems("s_wo0 s_wo1")
        s_y, s_x1 = sems("s_y s_x1")
        s_dsc, s_cv, s_sw, s_cat, s_sge, s_lru = sems("s_dsc s_cv s_sw s_cat s_sge s_lru")
        s_el = [sem(f"s_el{i}") for i in range(EU)]
        s_gu, s_uu, s_du, s_gd, s_gdc, s_gi, s_gic, s_si, s_sic = sems("s_gu s_uu s_du s_gd s_gdc s_gi s_gic s_si s_sic")
        s_tx, s_txd, s_txa, s_sil, s_hid, s_hidc = sems("s_tx s_txd s_txa s_sil s_hid s_hidc")
        s_c1, s_c2, s_c3, s_c4, s_c5, s_c6, s_c7 = sems("s_c1 s_c2 s_c3 s_c4 s_c5 s_c6 s_c7")
        s_th, s_thd, s_tha, s_eo, s_eoc, s_sc, s_scc = sems("s_th s_thd s_tha s_eo s_eoc s_sc s_scc")
        s_gw, s_sgt, s_sgc, s_xc, s_vg, s_vn, s_vs, s_vq = sems("s_gw s_sgt s_sgc s_xc s_vg s_vn s_vs s_vq")
        s_sg, s_lc, s_le, s_lv, s_lq, s_l1, s_l2 = sems("s_sg s_lc s_le s_lv s_lq s_l1 s_l2")
        s_gf, s_fin = sems("s_gf s_fin")
        s_xst, s_nst = sems("s_xst0 s_xst1"), sem("s_nst")
        s_lg, s_mx, s_ex, s_af, s_aft, s_afc = sems("s_lg s_mx s_ex s_af s_aft s_afc")
        s_tk, s_tkt, s_idx, s_rt = sems("s_tk s_tkt s_idx s_rt")

        class Chain:

            def __init__(self, eng, s):
                self.eng, self.s, self.n = eng, s, 0

            def mark(self, ins):
                self.n += 1
                ins.then_inc(self.s, 1)
                return self.n

            def do(self, ins):
                self.eng.wait_ge(self.s, self.mark(ins))

        N_CONST = 5
        small = [("c", I["c"], 8), ("c_ctx", I["c_ctx"], 8), ("mix_g", I["norm_mix_g"], 16),
                 ("ffn_g", I["norm_ffn_g"], 16), ("ev_conv_w", I["ev_conv_w"], 12), ("ev_conv_b", I["ev_conv_b"], 4),
                 ("decay_b", I["ev_decay_b"], 4), ("ev_norm_g", I["ev_norm_g"], 4),
                 ("od_conv_w", I["od_conv_w"], 16), ("od_conv_b", I["od_conv_b"], 4),
                 ("gate_a_b", I["od_gate_a_b"], 8), ("gate_x_b", I["od_gate_x_b"], 8), ("lam", I["od_lambda"], 8),
                 ("sg_norm_g", I["od_sg_norm_g"], 4)]
        N_SMALL = len(small) + 1
        DONE_SMALL = 16 * N_SMALL

        def flat(ap):
            names = "abcd"[:len(ap.shape)]
            return ap if len(names) == 1 else ap.rearrange(" ".join(names) + " -> (" + " ".join(names) + ")")

        xl_count, xst_count = {}, {}
        for n in range(norm0["final"] + TL):
            xl_count[n] = n // 2 + 1
        stored = [n for n in range(norm0["final"] + TL)
                  if norm0["ffn0"] <= n < norm0["mix1"] or n >= norm0["ffn1"]]
        for n in stored:
            xst_count[n] = sum(1 for m in stored if m <= n and m % 2 == n % 2)

        block = ctx.enter_context(nc.Block())

        used_when, n_ada = [], 0
        unit_jobs = {}
        for i, (key, _) in enumerate(stream):
            if key[0] == "ada":
                n_ada += 1
                used_when.append((s_used, n_ada))
            elif key[0] in ("v0", "v1"):
                used_when.append((s_vm, NT))
            elif key[0] in ("w0", "w1"):
                used_when.append((s_vm, NT + TL))
            else:
                kind, half = ("k", 0) if key[0] in "kq" else (key[0][:-1], int(key[0][-1]))
                kind = key[0] if key[0] in "kq" else kind
                unit_jobs[i] = [job_at[(kind, 2 * half + h, i >= n_even)] for h in range(2)]
                used_when.append((s_job, unit_jobs[i][1] + 1))

        SPLIT = [(0, BANK), (BANK, BANK), (2 * BANK, T - 2 * BANK)]

        def unit_in(pe, i):
            pe.wait_ge(s_load[slot_of[i]], 16 * n_in_slot[i])

        def ada(pe, i):
            _, l, g, k = stream[i][0]
            if k == 0 and 3 * l + g > 0:
                pe.wait_ge(s_adar, 3 * l + g)
            unit_in(pe, i)
            for q in range(4):
                ins = pe.matmul(ps[32 * q:32 * q + 2, 6, :], silc[:, 2 * k:2 * k + 2],
                                ring[slot_of[i]][:, q * BANK:(q + 1) * BANK], start=(k == 0), stop=(k == KC - 1))
            ins.then_inc(s_used, 1)

        def ada_rows(pe, a):
            pe.wait_ge(s_adar, a + 1)
            pe.wait_ge(s_vc, 2) if a == 0 else pe.wait_ge(s_adac, a)
            for j in range(4):
                ins = pe.transpose(ps[:, 7, j * P:(j + 1) * P], rowtmp[:, j * P:(j + 1) * P], ident[:, :])
            ins.then_inc(s_adat, 1)

        def norm_transposes(pe, n, bank, last):
            pe.wait_ge(s_xn, n + 1)
            if last is not None:
                pe.wait_ge(s_hd, last + 1)
                pe.wait_ge(s_ha, last + 1)
            for k in range(KC):
                ins = pe.transpose(ps[:, bank + k // 4, (k % 4) * P:(k % 4 + 1) * P], XN[:, k * P:(k + 1) * P],
                                   ident[:, :])
            ins.then_inc(s_tp, 1)

        def banks_free(pe, j):
            if j >= 2:
                if emptied["act"][j - 1]:
                    pe.wait_ge(s_ja, emptied["act"][j - 1])
                if emptied["dve"][j - 1]:
                    pe.wait_ge(s_jd, emptied["dve"][j - 1])

        def job(pe, j, i, half):
            n = jobs[j][2]
            banks_free(pe, j)
            unit_in(pe, i)
            w = ring[slot_of[i]].rearrange("p (k n) -> p k n", k=KC)
            for c0, cn in SPLIT:
                if c0 >= n:
                    break
                for k in range(KC):
                    ins = pe.matmul(wide(j % 2, n)[:, c0:c0 + cn], w[:, k, half * P:(half + 1) * P],
                                    hT[:, k, c0:c0 + cn], start=(k == 0), stop=(k == KC - 1))
            ins.then_inc(s_job, 1)

        def v_tile(pe, t, unit):
            v2 = R_W[:, UNIT * slot_of[unit]:UNIT * slot_of[unit] + 2 * UNIT].rearrange(
                "p (u k n) -> p k u n", u=2, k=KC)
            out_ = ps[:, 6 + t % 2, :].rearrange("p (u n) -> p u n", u=2)
            for k in range(KC):
                ins = pe.matmul(out_, hT[:, k, t * P:(t + 1) * P], v2[:, k, :, :],
                                start=(k == 0), stop=(k == KC - 1))
            ins.then_inc(s_vm, 1)

        def pe_start(pe):
            pe.wait_ge(s_const, N_CONST)
            pe.wait_ge(s_small, DONE_SMALL)
            pe.transpose(ps[:, 7, 0:NVEC], vrow[0:NVEC, :], ident[0:NVEC, 0:NVEC])
            pe.transpose(ps[:, 7, P:P + 96], adab_row[0:96, :], ident[0:96, 0:96]).then_inc(s_vt, 1)
            pe.wait_ge(s_silc, 2)
            for i in range(8):
                ada(pe, i)
            ada_rows(pe, 0)
            for t in range(NT):
                norm_transposes(pe, t, 2 * (t % 2), t - 2 if t >= 2 else None)

        def pe_even(pe):
            pe.wait_ge(s_sw, 48)
            pe.wait_ge(s_hd, NT)
            pe.wait_ge(s_ha, NT)
            for c0, cn in SPLIT:
                for k in range(KC):
                    ins = pe.matmul(wide(0, T)[0:32, c0:c0 + cn], wlr[:, k * 32:(k + 1) * 32], hT[:, k, c0:c0 + cn],
                                    start=(k == 0), stop=(k == KC - 1))
            ins.then_inc(s_job, 1)
            j = 1
            for half in range(2):
                job(pe, j, index[("k",)], half)
                j += 1
            for pd in range(4):
                banks_free(pe, j)
                for c0, cn in SPLIT:
                    ins = pe.matmul(wide(j % 2, T)[:, c0:c0 + cn], decup[0:32, pd * P:(pd + 1) * P],
                                    lrT[0:32, c0:c0 + cn], start=True, stop=True)
                ins.then_inc(s_job, 1)
                j += 1
            unit_in(pe, index[("v0",)])
            unit_in(pe, index[("v1",)])
            pe.wait_ge(s_adar, 1)
            pe.wait_ge(s_adac, 1)
            for t in range(NT):
                if t >= 2:
                    pe.wait_ge(s_ve, t - 1)
                v_tile(pe, t, index[("v0",)])
            for i in range(index[("q",)], n_even):
                key = stream[i][0]
                if key[0] == "ada":
                    if key[1:] == (0, 1, 0):
                        pe.wait_ge(s_ve, NT)
                    ada(pe, i)
                    if key[3] == KC - 1:
                        ada_rows(pe, 3 * key[1] + key[2])
                else:
                    for half in range(2):
                        job(pe, j, i, half)
                        j += 1
            assert j == n_even_jobs

        order = [[16, 17, 18, 19] + list(range(16)), [19, 18, 17, 16] + list(range(15, -1, -1))]

        def pe_gla(pe):
            for p in range(2):
                pe.wait_ge(s_qk, p + 1)
                for g in range(5):
                    n = 5 * p + g
                    if p == 0 and g == 0:
                        pe.wait_ge(s_ja, emptied["act"][n_even_jobs])
                        pe.wait_ge(s_jd, emptied["dve"][n_even_jobs])
                    if n >= 2:
                        pe.wait_ge(s_kc, n - 1)
                    for q in range(4):
                        t, r = 2 * g + q // 2, q % 2
                        ins = pe.transpose(ps[:, n % 2, q * P:(q + 1) * P], BX[:, 2 * r + p, t * P:(t + 1) * P],
                                           ident[:, :])
                    ins.then_inc(s_kt, 1)
                pe.wait_ge(s_kc, 5 * (p + 1))
                for b in range(NCH // 4):
                    if b >= 2:
                        pe.wait_ge(s_tst, 2 * NCH * p + 8 * (b - 1))
                    for s in range(4 * b, 4 * b + 4):
                        for r in range(2):
                            c = order[r][s]
                            h0, t = 64 * (c % 2), c // 2
                            for hh in range(2):
                                ins = pe.matmul(ps[64 * hh:64 * hh + 64, 2 * (b % 2) + c % 2, (s % 4) * P:(s % 4 + 1) * P],
                                                ktok[h0:h0 + 64, t, r, 64 * hh:64 * hh + 64],
                                                vtok[h0:h0 + 64, t, (2 * p + hh) * P:(2 * p + hh + 1) * P],
                                                start=True, stop=True)
                    ins.then_inc(s_up, 1)
                pe.wait_ge(s_sin, 2 * (NCH - 1) * (p + 1))
                pe.wait_ge(s_tst, 2 * NCH * (p + 1))
                for g in range(5):
                    n = 5 * p + g
                    if n >= 1:
                        pe.wait_ge(s_am, n)
                    for hh in range(2):
                        for r in range(2):
                            for tt in range(2):
                                t = 2 * g + tt
                                qd = (qT if r == 0 else kT)[64 * hh:64 * hh + 64, p, t * P:(t + 1) * P]
                                ins = pe.matmul(ps[:, 4 + hh, (2 * r + tt) * P:(2 * r + tt + 1) * P],
                                                BX[64 * hh:64 * hh + 64, 2 * r + p, t * P:(t + 1) * P], qd,
                                                start=True, stop=True)
                    ins.then_inc(s_at, 1)
                    pe.wait_ge(s_am, n + 1)
                    if n >= 1:
                        pe.wait_ge(s_of, n)
                    for hh in range(2):
                        for tt in range(2):
                            t = 2 * g + tt
                            o = ps[:, 6 + hh, tt * P:(tt + 1) * P]
                            vh = vtok[:, t, (2 * p + hh) * P:(2 * p + hh + 1) * P]
                            mm = [(o, vh, attS[:, n % 2, r, (2 * hh + tt) * P:(2 * hh + tt + 1) * P]) for r in range(2)]
                            for r in range(2):
                                for cc in range(2):
                                    c = 2 * t + cc
                                    if c != order[r][0]:
                                        qd = (qT if r == 0 else kT)[64 * hh:64 * hh + 64, p, c * 64:(c + 1) * 64]
                                        mm.append((o[:, cc * 64:(cc + 1) * 64], SIN[64 * hh:64 * hh + 64, r, c, :], qd))
                            for x, (oo, lhs, rhs) in enumerate(mm):
                                ins = pe.matmul(oo, lhs, rhs, start=(x == 0), stop=(x == len(mm) - 1))
                    ins.then_inc(s_o, 1)
                    pe.wait_ge(s_osq, n + 1)
                    if g >= 2:
                        pe.wait_ge(s_rs, n - 1)
                    pe.matmul(ps[:, n % 2, :], ones[:, :], SQ[n % 2], start=True, stop=True).then_inc(s_ms, 1)
                pe.wait_ge(s_of, 5 * (p + 1))

        def pe_gates_as_rows(pe, l):
            for m in range(4 if l == 0 else 2):
                n0 = (0 if l == 0 else 4) + m
                for k in range(KC):
                    n = n0 * KC + k
                    pe.wait_ge(s_diag, n + 1)
                    if k == 0 and n0 >= 1:
                        pe.wait_ge(s_bc, n0)
                    pe.matmul(ps[:, k // 4, (k % 4) * P:(k % 4 + 1) * P], ones[:, :],
                              diag[:, (n % 2) * P:(n % 2 + 1) * P], start=True, stop=True).then_inc(s_bcp, 1)

        def pe_wout(pe, l):
            nt = NT if l == 0 else TL
            n0 = norm0["ffn0"] if l == 0 else norm0["ffn1"]
            r0 = 0 if l == 0 else NT
            pe_gates_as_rows(pe, l)
            pe.wait_ge(s_bc, 4 if l == 0 else 6)
            pe.wait_ge(s_wo[0], 16 * (l + 1))
            pe.wait_ge(s_wo[1], 16 * (l + 1))
            if l == 0:
                pe.wait_ge(s_of, 10)
            else:
                pe.wait_ge(s_cat, 1)
                pe.wait_ge(s_sge, TL)
                pe.wait_ge(s_ja, emptied["act"][len(jobs)])
            src = cat if l == 0 else cat1
            for i in range(nt + 3):
                if i < nt:
                    if i >= 2:
                        pe.wait_ge(s_x1, r0 + i - 1)
                    for c in range(2):
                        for k in range(KC):
                            ins = pe.matmul(ps[:, 4 + 2 * (i % 2) + c, :], src[:, k, i * P:(i + 1) * P],
                                            wout[:, k, c * BANK:(c + 1) * BANK], start=(k == 0), stop=(k == KC - 1))
                    ins.then_inc(s_y, 1)
                if 1 <= i <= nt:
                    norm_transposes(pe, n0 + i - 1, 0, n0 + i - 2 if i > 1 else None)
                if 2 <= i <= nt + 1:
                    t = i - 2
                    pe.wait_ge(s_hd, n0 + t + 1)
                    pe.wait_ge(s_ha, n0 + t + 1)
                    if t == 0:
                        pe.wait_ge(s_rt, 16 * (l + 1))
                    else:
                        pe.wait_ge(s_ex, r0 + t)
                    for k in range(KC):
                        ins = pe.matmul(ps[:, 2, 0:NE], hT[:, k, t * P:(t + 1) * P], router[:, k * NE:(k + 1) * NE],
                                        start=(k == 0), stop=(k == KC - 1))
                    ins.then_inc(s_lg, 1)
                if i >= 3:
                    t = i - 3
                    pe.wait_ge(s_af, r0 + t + 1)
                    if t >= 1:
                        pe.wait_ge(s_afc, r0 + t)
                    pe.transpose(ps[0:NE, 3, 0:P], sm[:, 32 * (t % 2):32 * (t % 2) + NE], ident[:, :]).then_inc(s_aft, 1)
            ne = 48 if l == 0 else NE
            pe.wait_ge(s_tk, l + 1)
            pe.transpose(ps[:, 2, 0:ne], tkv[0:ne, :], ident[0:ne, 0:ne])
            pe.transpose(ps[:, 3, 0:ne], tkf[0:ne, :], ident[0:ne, 0:ne]).then_inc(s_tkt, 1)

        def act_root(act, n):
            b = n % 2
            act.wait_ge(s_ss, n + 1)
            nc.scalar.activation(st[:, 4 * b + 1:4 * b + 2], st[:, 4 * b:4 * b + 1], ACT.Sqrt,
                                 bias=epsc[:, 0:1], scale=1.0 / D).then_inc(s_sq, 1)

        def columns(l, w, k, t):
            c = 0 if t < TL else 1
            i = ((l * 2 + w) * KC + k) * 2 + c
            m = (l * 48 + (3 * w) * KC + k) * 2 + c
            return scg[:, i:i + 1], modc[:, m:m + 1]

        def act_blocks(act, n, l, w, t, bank):
            act.wait_ge(s_tp, n + 1)
            for k in range(KC // 2, KC):
                sc_, sh_ = columns(l, w, k, t)
                ins = nc.scalar.activation(hT[:, k, t * P:(t + 1) * P], ps[:, bank + k // 4, (k % 4) * P:(k % 4 + 1) * P],
                                           ACT.Identity, bias=sh_, scale=sc_)
            ins.then_inc(s_ha, 1)

        def dve_blocks(dve, n, l, w, t, bank):
            dve.wait_ge(s_tp, n + 1)
            for k in range(KC // 2):
                sc_, sh_ = columns(l, w, k, t)
                ins = nc.vector.tensor_scalar(hT[:, k, t * P:(t + 1) * P],
                                              ps[:, bank + k // 4, (k % 4) * P:(k % 4 + 1) * P], sc_, sh_,
                                              ALU.mult, ALU.add)
            ins.then_inc(s_hd, 1)

        def dve_norm(dve, own, n):
            b = n % 2
            dve.wait_ge(s_sq, n + 1)
            own.do(nc.vector.reciprocal(st[:, 4 * b + 2:4 * b + 3], st[:, 4 * b + 1:4 * b + 2]))
            nc.vector.tensor_scalar(XN, XB[b], st[:, 4 * b + 2:4 * b + 3], None, ALU.mult).then_inc(s_xn, 1)

        def dve_ada(dve, own, a):
            l, g = divmod(a, 3)
            dve.wait_ge(s_used, KC * (a + 1))
            if a >= 1:
                dve.wait_ge(s_adat, a)
            if a == 0:
                dve.wait_ge(s_zero, 2)
            for q in range(4):
                ins = nc.vector.tensor_copy(rowtmp[32 * q:32 * q + 2, :], ps[32 * q:32 * q + 2, 6, :])
            ins.then_inc(s_adar, 1)
            dve.wait_ge(s_adat, a + 1)
            m3 = modc[:, :].rearrange("p (m w) -> p m w", w=2)
            m0 = 48 * l + 16 * g
            for w in range(2):
                src = ps[:, 7, :].rearrange("p (j q r) -> p r q j", j=4, q=4)[:, w]
                ins = nc.vector.tensor_tensor(m3[:, m0:m0 + 16, w].rearrange("p (q j) -> p q j", q=4), src,
                                              adab[:, m0:m0 + 16].rearrange("p (q j) -> p q j", q=4), ALU.add)
            ins.then_inc(s_adac, 1)
            dve.wait_ge(s_adac, a + 1)
            if g in (0, 2):
                w_, blk, v0 = (0, 8, VEC["mix_g"]) if g == 0 else (1, 32, VEC["ffn_g"])
                s3 = scg[:, :].rearrange("p (m w) -> p m w", w=2)
                i0 = (l * 2 + w_) * KC
                for w in range(2):
                    ins = nc.vector.scalar_tensor_tensor(out=s3[:, i0:i0 + KC, w],
                                                         in0=m3[:, 48 * l + blk:48 * l + blk + KC, w], scalar=1.0,
                                                         in1=vcol[:, v0 + l * KC:v0 + (l + 1) * KC],
                                                         op0=ALU.add, op1=ALU.mult)
                ins.then_inc(s_scg, 1)

        def act_even_job(act, own, j):
            kind, b, n, who = jobs[j]
            act.wait_ge(s_job, j + 1)
            w = wide(j % 2, n)
            if kind == "lr":
                ins = nc.scalar.copy(lrT[0:32, :], w[0:32, :])
            elif kind == "k":
                ins = nc.scalar.copy(kT[:, b, :], w)
            elif kind == "q":
                ins = nc.scalar.mul(qT[:, b, :], w, DK ** -0.5)
            elif kind == "g":
                ins = nc.scalar.activation(cat[:, 4 + b, :], w, ACT.Silu)
            elif kind == "cg":
                if b >= 2:
                    act.wait_ge(s_cv, b - 1)
                ins = nc.scalar.copy(TMP[b % 2], w)
            ins.then_inc(s_ja, 1)

        def act_decay(act, own, pd):
            t = TMP[2 + pd % 2]
            act.wait_ge(s_dx, pd + 1)
            own.do(nc.scalar.activation(t, t, ACT.Exp, scale=-1.0))
            nc.scalar.activation(t, t, ACT.Ln, bias=1.0).then_inc(s_dl, 1)

        def dve_decay_in(dve, pd):
            j = job_at[("dec", pd, False)]
            dve.wait_ge(s_job, j + 1)
            nc.vector.tensor_scalar(BX[:, pd, :], wide(j % 2, T), vcol[:, VEC["decay_b"] + pd:VEC["decay_b"] + pd + 1],
                                    None, ALU.add).then_inc(s_jd, 1)
            dve.wait_ge(s_jd, emptied["dve"][j + 1])
            nc.vector.scalar_tensor_tensor(out=TMP[2 + pd % 2], in0=BX[:, pd, :], scalar=-1.0, in1=BX[:, pd, :],
                                           op0=ALU.mult, op1=ALU.max).then_inc(s_dx, 1)

        def dve_decay_out(dve, own, pd):
            t, x = TMP[2 + pd % 2], BX[:, pd, :]
            dve.wait_ge(s_dl, pd + 1)
            own.do(nc.vector.scalar_tensor_tensor(out=t, in0=x, scalar=0.0, in1=t, op0=ALU.min, op1=ALU.subtract))
            if pd < 2:
                ins = nc.vector.tensor_tensor_scan(x, chunk0[:, :], t, 0.0, ALU.mult, ALU.add)
            else:
                ins = nc.vector.tensor_tensor_scan(BX[:, pd, ::-1], chunk0[:, :], t[:, ::-1], 0.0, ALU.mult, ALU.add)
            ins.then_inc(s_dsc, 1)

        def dve_even_job(dve, own, j):
            kind, b, n, who = jobs[j]
            dve.wait_ge(s_job, j + 1)
            w = wide(j % 2, n)
            if kind == "bg":
                dve.wait_ge(s_cv, b + 1)
                nc.vector.tensor_tensor(cat[:, b, :], cat[:, b, :], w, ALU.mult).then_inc(s_jd, 1)
                return
            p = TMP[b % 2]
            dve.wait_ge(s_ja, emptied["act"][job_at[("cg", b, False)] + 1])
            nc.vector.tensor_tensor(p, p, w, ALU.mult).then_inc(s_jd, 1)
            dve.wait_ge(s_jd, emptied["dve"][j + 1])
            w0 = VEC["ev_conv_w"] + b
            tap = [vcol[:, w0 + 4 * i:w0 + 4 * i + 1] for i in range(3)]
            o = cat[:, b, :]
            own.do(nc.vector.tensor_scalar(o, p, tap[1], vcol[:, VEC["ev_conv_b"] + b:VEC["ev_conv_b"] + b + 1],
                                           ALU.mult, ALU.add))
            for src, dst in (((0, GRID - 1), (1, GRID)), ((1, GRID), (0, GRID - 1))):
                tp = tap[0] if dst[0] == 1 else tap[2]
                p3 = p[:, 0:LAT].rearrange("p (r x) -> p r x", x=GRID)[:, :, src[0]:src[1]]
                o3 = o[:, 0:LAT].rearrange("p (r x) -> p r x", x=GRID)[:, :, dst[0]:dst[1]]
                nc.vector.scalar_tensor_tensor(out=o3, in0=p3, scalar=tp, in1=o3, op0=ALU.mult, op1=ALU.add)
                s0, d0 = (0, 1) if dst[0] == 1 else (1, 0)
                pc, oc = p[:, LAT + s0:LAT + s0 + CTX - 1], o[:, LAT + d0:LAT + d0 + CTX - 1]
                ins = nc.vector.scalar_tensor_tensor(out=oc, in0=pc, scalar=tp, in1=oc, op0=ALU.mult, op1=ALU.add)
                own.mark(ins) if dst[0] != 1 else own.do(ins)
            dve.wait_ge(s_dv, own.n)
            dve.sem_inc(s_cv, 1)

        def act_exps(act, p):
            if p == 0:
                act.wait_ge(s_dsc, 4)
                act.wait_ge(s_cv, 4)
            else:
                act.wait_ge(s_qk, 1)
            for r in range(2):
                nc.scalar.activation(TMP[2 * r], BX[:, 2 * r + p, :], ACT.Exp, scale=1.0 / TAU)
                ins = nc.scalar.activation(TMP[2 * r + 1], BX[:, 2 * r + p, :], ACT.Exp, scale=-1.0 / TAU)
            ins.then_inc(s_eb, 1)

        def dve_decayed(dve, own, p):
            dve.wait_ge(s_eb, p + 1)
            if p == 0:
                dve.wait_ge(s_ja, emptied["act"][n_even_jobs])
            for r in range(2):
                e3 = TMP[2 * r].rearrange("p (c i) -> p c i", i=CHUNK)
                i = (CHUNK - 1) * (1 - r)
                nc.vector.tensor_copy(dec[:, (2 * r + p) * NCH:(2 * r + p + 1) * NCH], e3[:, :, i])
                ins = nc.vector.tensor_tensor(BX[:, 2 * r + p, :], kT[:, p, :], TMP[2 * r + 1], ALU.mult)
            own.do(ins)
            own.do(nc.vector.tensor_tensor(kT[:, p, :], qT[:, p, :], TMP[2], ALU.mult))
            nc.vector.tensor_tensor(qT[:, p, :], qT[:, p, :], TMP[0], ALU.mult).then_inc(s_qk, 1)

        def act_gla(act, own):
            act_exps(act, 0)
            act_exps(act, 1)
            for p in range(2):
                for g in range(5):
                    n = 5 * p + g
                    act.wait_ge(s_kt, n + 1)
                    nc.scalar.copy(ktok[:, 2 * g:2 * g + 2, :, :].rearrange("p t r d -> p (t r d)"),
                                   ps[:, n % 2, :]).then_inc(s_kc, 1)
                for s in range(NCH - 1):
                    n = NCH * p + s
                    for r in range(2):
                        act.wait_ge(s_tst, 2 * n + r + 1)
                        c, c1 = order[r][s], order[r][s + 1]
                        i = (2 * r + p) * NCH + c
                        nc.scalar.activation(SIN[:, r, c1, :], TST[:, r, s % 2, :], ACT.Copy,
                                             scale=dec[:, i:i + 1]).then_inc(s_sin, 1)
                for g in range(5):
                    n = 5 * p + g
                    act.wait_ge(s_o, n + 1)
                    if n == 0:
                        act.wait_ge(s_qk, 2)
                    if n >= 2:
                        act.wait_ge(s_ms, n - 1)
                    nc.scalar.activation(SQ[n % 2].rearrange("p (h t) -> p h t", h=2), ps[:, 6:8, 0:256],
                                         ACT.Square).then_inc(s_osq, 1)
                    act.wait_ge(s_ms, n + 1)
                    if n >= 2:
                        act.wait_ge(s_of, n - 1)
                    own.do(nc.scalar.activation(RS[n % 2], ps[:, n % 2, :], ACT.Ln, bias=epsc[:, 0:1], scale=1.0 / P))
                    nc.scalar.activation(RS[n % 2], RS[n % 2], ACT.Exp, scale=-0.5).then_inc(s_rs, 1)

        def dve_gla(dve, own):
            dve_decayed(dve, own, 0)
            dve_decayed(dve, own, 1)
            dve.wait_ge(s_job, n_even_jobs)
            own.do(nc.vector.memset(R_H[:, 7680:9728], 0.0))
            for p in range(2):
                for s in range(NCH):
                    n = NCH * p + s
                    if s % 4 == 0:
                        dve.wait_ge(s_up, (n // 4) + 1)
                    for r in range(2):
                        u = ps[:, 2 * (s // 4 % 2) + order[r][s] % 2, (s % 4) * P:(s % 4 + 1) * P]
                        if s >= 2:
                            dve.wait_ge(s_sin, 38 * p + 2 * (s - 2) + r + 1)
                        elif p == 1 and s == 0 and r == 0:
                            dve.wait_ge(s_sin, 38)
                        if s == 0:
                            ins = nc.vector.tensor_copy(TST[:, r, 0, :], u)
                        else:
                            i = (2 * r + p) * NCH + order[r][s - 1]
                            dve.wait_ge(s_tst, 2 * (n - 1) + r + 1)
                            ins = nc.vector.scalar_tensor_tensor(out=TST[:, r, s % 2, :], in0=TST[:, r, (s - 1) % 2, :],
                                                                 scalar=dec[:, i:i + 1], in1=u,
                                                                 op0=ALU.mult, op1=ALU.add)
                        ins.then_inc(s_tst, 1)
                for g in range(5):
                    n = 5 * p + g
                    dve.wait_ge(s_at, n + 1)
                    if n >= 2:
                        dve.wait_ge(s_o, n - 1)
                    for r in range(2):
                        mask = (maskf, maskb)[r].bitcast(U32).unsqueeze(1).broadcast_to([P, 2, P])
                        for hh in range(2):
                            ins = nc.vector.copy_predicated(
                                attS[:, n % 2, r, 256 * hh:256 * (hh + 1)].rearrange("p (q i) -> p q i", q=2), mask,
                                ps[:, 4 + hh, 256 * r:256 * (r + 1)].rearrange("p (q i) -> p q i", q=2))
                    ins.then_inc(s_am, 1)
                    dve.wait_ge(s_rs, n + 1)
                    for hh in range(2):
                        h = 2 * p + hh
                        o = cat[:, 4 + h, g * 256:(g + 1) * 256]
                        ins = nc.vector.scalar_tensor_tensor(out=o, in0=ps[:, 6 + hh, 0:256],
                                                             scalar=vcol[:, VEC["ev_norm_g"] + h:VEC["ev_norm_g"] + h + 1],
                                                             in1=o, op0=ALU.mult, op1=ALU.mult)
                    own.do(ins)
                    o = cat[:, 4 + 2 * p:6 + 2 * p, g * 256:(g + 1) * 256]
                    nc.vector.tensor_tensor(o, o, RS[n % 2].rearrange("p (h t) -> p h t", h=2), ALU.mult).then_inc(s_of, 1)

        def gate_rows(l):
            return [(0, 2, 0), (1, 2, 1), (2, 5, 0), (3, 5, 1)] if l == 0 else [(0, 2, 0), (2, 5, 0)]

        def dve_gates(dve, l):
            for m, (_, blk, w) in enumerate(gate_rows(l)):
                for k in range(KC):
                    n = ((0 if l == 0 else 4) + m) * KC + k
                    if n >= 2:
                        dve.wait_ge(s_bcp, n - 1)
                    i = (l * 48 + blk * KC + k) * 2 + w
                    nc.vector.tensor_scalar(diag[:, (n % 2) * P:(n % 2 + 1) * P], ident[:, :], modc[:, i:i + 1], None,
                                            ALU.mult).then_inc(s_diag, 1)

        def act_gates(act, l):
            for m, (row, _, _) in enumerate(gate_rows(l)):
                n0 = (0 if l == 0 else 4) + m
                act.wait_ge(s_bcp, KC * (n0 + 1))
                nc.scalar.copy(bc[:, row * D:(row + 1) * D], ps[:, 0:2, :].rearrange("p b n -> p (b n)")).then_inc(s_bc, 1)

        def dve_wout(dve, own, l):
            nt, n0, r0 = (NT, norm0["ffn0"], 0) if l == 0 else (TL, norm0["ffn1"], NT)
            dve_gates(dve, l)
            dve.wait_ge(s_bc, 4 if l == 0 else 6)
            ne = 48 if l == 0 else NE
            if l == 0:
                dve.wait_ge(s_o, 10)
            own.do(nc.vector.memset(affT[0:ne, :], -1.0))
            for i in range(nt + 3):
                if i < nt:
                    n = n0 + i
                    dve.wait_ge(s_y, r0 + i + 1)
                    y = ps[:, 4 + 2 * (i % 2):6 + 2 * (i % 2), :].rearrange("p b n -> p (b n)")
                    row = 0 if i < TL else 1
                    own.do(nc.vector.tensor_tensor(y, y, bc[:, row * D:(row + 1) * D], ALU.mult))
                    dve.wait_ge(s_xl[n % 2], 16 * xl_count[n])
                    nc.vector.tensor_tensor(XB[n % 2], XB[n % 2], y, ALU.add).then_inc(s_x1, 1)
                if 1 <= i <= nt:
                    dve_blocks(dve, n0 + i - 1, l, 1, i - 1, 0)
                if 2 <= i <= nt + 1:
                    t, b = i - 2, 16 + 4 * (i % 2)
                    dve.wait_ge(s_lg, r0 + t + 1)
                    own.do(nc.vector.reduce_max(st[:, b:b + 1], ps[:, 2, 0:NE], AXX))
                    nc.vector.tensor_scalar(st[:, b + 1:b + 2], st[:, b:b + 1], -1.0, None, ALU.mult).then_inc(s_mx, 1)
                if i < nt:
                    dve_norm(dve, own, n0 + i)
                if 2 <= i <= nt + 1:
                    t, b, s0 = i - 2, 16 + 4 * (i % 2), 32 * (i % 2)
                    dve.wait_ge(s_ex, r0 + t + 1)
                    own.do(nc.vector.reciprocal(st[:, b + 3:b + 4], st[:, b + 2:b + 3]))
                    nc.vector.tensor_scalar(sm[:, s0:s0 + NE], sm[:, s0:s0 + NE], st[:, b + 3:b + 4], None,
                                            ALU.mult).then_inc(s_af, 1)
                if i >= 3:
                    t = i - 3
                    dve.wait_ge(s_aft, r0 + t + 1)
                    dst = affT[0:NE, t * P:(t + 1) * P] if t < TL else affT[32:48, (t - TL) * P:(t - TL + 1) * P]
                    nc.vector.tensor_copy(dst, ps[0:NE, 3, 0:P]).then_inc(s_afc, 1)
            dve.wait_ge(s_afc, r0 + nt)
            a = affT[0:ne, :]
            for r in range(CAPL // 8):
                v8, i8 = tkv[0:ne, 8 * r:8 * r + 8], tki[0:ne, 8 * r:8 * r + 8]
                own.do(nc.vector.max(v8, a))
                nc.vector.max_index(i8, v8, a)
                own.do(nc.vector.match_replace(a, v8, a, -2.0))
            nc.vector.tensor_copy(tkf[0:ne, :], tki[0:ne, :]).then_inc(s_tk, 1)
            dve.wait_ge(s_tkt, l + 1)
            nc.vector.tensor_copy(icolT[:, 0:NE], ps[:, 3, 0:NE])
            if l == 0:
                nc.vector.tensor_scalar(icolT[0:CAPC, 32:48], ps[0:CAPC, 3, 32:48], float(LAT), None, ALU.add)
            nc.vector.tensor_copy(gcolT[:, 0:ne], ps[:, 2, 0:ne]).then_inc(s_idx, 1)

        def act_wout(act, own, l):
            nt, n0, r0 = (NT, norm0["ffn0"], 0) if l == 0 else (TL, norm0["ffn1"], NT)
            act_gates(act, l)
            for i in range(nt + 3):
                if 1 <= i <= nt:
                    act_blocks(act, n0 + i - 1, l, 1, i - 1, 0)
                if i < nt:
                    n = n0 + i
                    act.wait_ge(s_x1, r0 + i + 1)
                    if i >= 1:
                        act.wait_ge(s_nst, 16 * (r0 + i))
                    act_square(act, n)
                    act_root(act, n)
                if 2 <= i <= nt + 1:
                    t, b, s0 = i - 2, 16 + 4 * (i % 2), 32 * (i % 2)
                    act.wait_ge(s_mx, r0 + t + 1)
                    if t >= 2:
                        act.wait_ge(s_aft, r0 + t - 1)
                    nc.scalar.activation(sm[:, s0:s0 + NE], ps[:, 2, 0:NE], ACT.Exp, bias=st[:, b + 1:b + 2],
                                         accum_out=st[:, b + 2:b + 3]).then_inc(s_ex, 1)

        def sp_wout(sp, l):
            nt, n0, r0 = (NT, norm0["ffn0"], 0) if l == 0 else (TL, norm0["ffn1"], NT)
            w = (I["ev_w_out"] if l == 0 else I["od_w_out"]).rearrange("l (k p) n -> (l p) k n", p=P)
            if l == 0:
                sp.wait_ge(s_job, n_even_jobs)
                sp.wait_ge(s_used, 6 * KC)
                sp.dma_start(wout[:, 0:6, :], w[:, 0:6, :]).then_inc(s_wo[0], 16)
                sp.wait_ge(s_qk, 2)
                sp.dma_start(wout[:, 6:8, :], w[:, 6:8, :]).then_inc(s_wo[1], 16)
                sp.wait_ge(s_of, 10)
            else:
                sp.wait_ge(s_job, len(jobs))
                sp.wait_ge(s_vm, NT + TL)
                sp.dma_start(wout[:, 0:6, :], w[:, 0:6, :]).then_inc(s_wo[0], 16)
                sp.wait_ge(s_lru, 8)
                sp.dma_start(wout[:, 6:8, :], w[:, 6:8, :]).then_inc(s_wo[1], 16)
            sl, sc_ = (x_rows, c_rows) if l == 0 else (xres, xres)
            for i in range(nt + 1):
                if i < nt:
                    n = n0 + i
                    if i >= 2:
                        sp.wait_ge(s_xst[n % 2], 16 * xst_count[n - 2])
                        sp.wait_ge(s_xn, n - 1)
                    elif l == 1:
                        sp.wait_ge(s_xn, n0)
                    sp.dma_start(XB[n % 2], tok_tile(sl, sc_, i)).then_inc(s_xl[n % 2], 16)
                if i >= 1:
                    t, n = i - 1, n0 + i - 1
                    sp.wait_ge(s_x1, r0 + t + 1)
                    sp.dma_start(xres[t * P:(t + 1) * P, :], XB[n % 2]).then_inc(s_xst[n % 2], 16)
                    sp.wait_ge(s_xn, n + 1)
                    sp.dma_start(xnd[t * P:(t + 1) * P, :], XN).then_inc(s_nst, 16)
                if i == 0:
                    sp.dma_start(router[:, :].rearrange("p (k e) -> p k e", e=NE),
                                 I["moe_router"][l].rearrange("(k p) e -> p k e", p=P)).then_inc(s_rt, 16)

        def act_square(act, n):
            if n >= 1:
                act.wait_ge(s_tp, min(n, norm0["mix1"] + NT + TL))
            nc.scalar.activation(XN, XB[n % 2], ACT.Square, accum_out=st[:, 4 * (n % 2):4 * (n % 2) + 1]).then_inc(s_ss, 1)

        def sp_expert_units(sp, l, n, e, mats):
            for m in mats:
                w = (I["moe_w_gate"], I["moe_w_up"], I["moe_w_down"])[m].rearrange(
                    "l e (j k p) n -> (l e j) p k n", j=4, p=P)
                used = (s_gu, s_uu, s_du)[m]
                for j in range(4):
                    if not isinstance(n, int) or n % NE:
                        sp.wait_ge(used, n * 4 - 3 + j)
                    src = w[bass.ds(n * 4 + j, 1)].rearrange("a p k n -> p (a k) n")
                    sp.dma_start(eslot[4 * m + j].rearrange("p (k n) -> p k n", k=2), src).then_inc(s_el[4 * m + j], 16)

        def sp_moe(sp, l):
            n0 = NE * l
            if l == 0:
                sp.wait_ge(s_o, 10)
            else:
                sp.wait_ge(s_sge, TL)
                sp.wait_ge(s_lru, 8)
            w = [I[x].rearrange("l e (j k p) n -> (l e j) p k n", j=4, p=P) for x in ("moe_w_gate", "moe_w_up")]
            for u in range(8):
                if u == 7:
                    sp.wait_ge(s_lg, NT if l == 0 else NT + TL)
                sp.dma_start(eslot[u].rearrange("p (k n) -> p k n", k=2), w[u // 4][4 * n0 + u % 4]).then_inc(s_el[u], 16)

            def step(n, e, down_first=False):
                sp_expert_units(sp, l, n, e, (0, 1))
                wd = I["moe_w_down"].rearrange("l e (j k p) n -> (l e j) p k n", j=4, p=P)
                for j in range(4):
                    if not down_first:
                        sp.wait_ge(s_du, n * 4 - 7 + j)
                    src = wd[bass.ds(n * 4 - 4 + j, 1)].rearrange("a p k n -> p (a k) n")
                    sp.dma_start(eslot[8 + j].rearrange("p (k n) -> p k n", k=2), src).then_inc(s_el[8 + j], 16)

            step(n0 + 1, 1, True)
            with sp.Fori(n0 + 2, n0 + NE) as n:
                step(n, None)
            n = n0 + NE
            wd = I["moe_w_down"].rearrange("l e (j k p) n -> (l e j) p k n", j=4, p=P)
            for j in range(4):
                sp.wait_ge(s_du, n * 4 - 7 + j)
                sp.dma_start(eslot[8 + j].rearrange("p (k n) -> p k n", k=2), wd[4 * n - 4 + j]).then_inc(s_el[8 + j], 16)

        def pe_moe(pe, l):
            n0 = NE * l
            C = CAPC if l == 0 else 0

            def unit(n, m, j, lhs, bank, cbank, used):
                pe.wait_ge(s_el[4 * m + j], (n + 1) * 16)
                w = eslot[4 * m + j].rearrange("p (k n) -> p k n", k=2)
                for kk in range(2):
                    k = 2 * j + kk
                    for c in range(2):
                        ins = pe.matmul(ps[:, bank + c, :], lhs[:, k, 0:P], w[:, kk, c * BANK:(c + 1) * BANK],
                                        start=(k == 0), stop=(k == KC - 1))
                if C:
                    for kk in range(2):
                        for c in range(2):
                            q = 2 * kk + c
                            ins = pe.matmul(ps[32 * q:32 * q + C, cbank, :], lhs[:, 2 * j + kk, P:P + C],
                                            w[:, kk, c * BANK:(c + 1) * BANK], start=(j == 0), stop=(j == 3))
                ins.then_inc(used, 1)

            def token_columns(n):
                pe.wait_ge(s_gd, (n + 1) * 16)
                for k in range(KC):
                    ins = pe.transpose(ps[:, 4 + k // 4, (k % 4) * P:(k % 4 + 1) * P], xg[:, k * P:(k + 1) * P],
                                       ident[:, :])
                if C:
                    pe.wait_ge(s_const, N_CONST)
                    pe.wait_ge(s_gdc, (n + 1) * 16)
                    for k in range(KC):
                        ins = pe.transpose(ps[:, 7, k * C:(k + 1) * C], xgc[0:C, k * P:(k + 1) * P], ident[0:C, 0:C])
                ins.then_inc(s_tx, 1)

            def down(n):
                pe.wait_ge(s_thd, n + 1)
                pe.wait_ge(s_tha, n + 1)
                for j in range(4):
                    unit(n, 2, j, hidT, 4, 6, s_du)

            def step(n, first, second, last):
                x = xT[pe_parity[0]]
                pe_parity[0] ^= 1
                pe.wait_ge(s_txd, n + 1)
                pe.wait_ge(s_txa, n + 1)
                if not first:
                    pe.wait_ge(s_sil, n)
                    if C and not second:
                        pe.wait_ge(s_c6, n - 1)
                        pe.wait_ge(s_c7, n - 1)
                for j in range(4):
                    unit(n, 0, j, x, 0, 6, s_gu)
                    if j == 2 and not last:
                        if not first:
                            pe.wait_ge(s_thd, n)
                            pe.wait_ge(s_tha, n)
                            if not second:
                                pe.wait_ge(s_eo, n - 1)
                        token_columns(n + 1)
                if not last:
                    pe.wait_ge(s_txd, n + 2)
                    pe.wait_ge(s_txa, n + 2)
                if not first:
                    pe.wait_ge(s_thd, n)
                    pe.wait_ge(s_tha, n)
                    if not second:
                        pe.wait_ge(s_eo, n - 1)
                for j in range(4):
                    unit(n, 1, j, x, 2, 7, s_uu)
                if C:
                    pe.wait_ge(s_c2, n + 1)
                if not first:
                    down(n - 1)
                pe.wait_ge(s_hid, n + 1)
                for k in range(KC):
                    ins = pe.transpose(ps[:, 2 + k // 4, (k % 4) * P:(k % 4 + 1) * P], hid[:, k * P:(k + 1) * P],
                                       ident[:, :])
                if C:
                    pe.wait_ge(s_const, N_CONST)
                    pe.wait_ge(s_hidc, n + 1)
                    for k in range(4):
                        ins = pe.transpose(ps[:, 7, k * 2 * C:(k + 1) * 2 * C], hidc[0:2 * C, k * P:(k + 1) * P],
                                           ident[0:2 * C, 0:2 * C])
                ins.then_inc(s_th, 1)

            pe_parity = [0]
            token_columns(n0)
            step(n0, True, False, False)
            step(n0 + 1, False, True, False)
            with pe.Fori(n0 + 2, n0 + NE - 2, 2) as n:
                step(n, False, False, False)
                step(n + 1, False, False, False)
            step(n0 + NE - 2, False, False, False)
            step(n0 + NE - 1, False, False, True)
            if C:
                pe.wait_ge(s_c6, n0 + NE - 1)
                pe.wait_ge(s_c7, n0 + NE - 1)
            pe.wait_ge(s_eo, n0 + NE - 1)
            down(n0 + NE - 1)

        def act_moe(act, l):
            n0 = NE * l
            C = CAPC if l == 0 else 0
            par = [0]

            def token_columns(n):
                x = xT[par[0]]
                par[0] ^= 1
                act.wait_ge(s_tx, n + 1)
                for k in range(KC // 2, KC):
                    sc_, sh_ = columns(l, 1, k, 0)
                    ins = nc.scalar.activation(x[:, k, 0:P], ps[:, 5, (k % 4) * P:(k % 4 + 1) * P], ACT.Identity,
                                               bias=sh_, scale=sc_)
                ins.then_inc(s_txa, 1)

            def context_down(n):
                act.wait_ge(s_du, n * 4 + 4)
                if not (isinstance(n, int) and n == 0):
                    act.wait_ge(s_eoc, n)
                for c in range(2):
                    ins = nc.scalar.copy(tmo[0:C, c * BANK:(c + 1) * BANK], ps[64 + 32 * c:64 + 32 * c + C, 6, :])
                ins.then_inc(s_c6, 1)

            def step(n, first, last):
                if not last:
                    token_columns(n + 1)
                act.wait_ge(s_gu, n * 4 + 4)
                if not first:
                    act.wait_ge(s_hid, n)
                nc.scalar.activation(sil, ps[:, 0:2, :].rearrange("p b n -> p (b n)"), ACT.Silu).then_inc(s_sil, 1)
                if C:
                    if not first:
                        act.wait_ge(s_hidc, n)
                    nc.scalar.copy(tmc[0:2 * C, :], ps[64:128, 6, :]).then_inc(s_c1, 1)
                    act.wait_ge(s_c2, n + 1)
                    nc.scalar.activation(silx[0:2 * C, :], silx[0:2 * C, :], ACT.Silu).then_inc(s_c3, 1)
                    act.wait_ge(s_uu, n * 4 + 4)
                    nc.scalar.copy(tmc[0:2 * C, :], ps[64:128, 7, :]).then_inc(s_c4, 1)
                    if not first:
                        context_down(n - 1)
                act.wait_ge(s_th, n + 1)
                nc.scalar.copy(hidT[:, 4:8, 0:P], ps[:, 3, :].rearrange("p (k t) -> p k t", k=4)).then_inc(s_tha, 1)

            if l == 0:
                act.wait_ge(s_xst[0], 16 * (NT // 2))
            else:
                act.wait_ge(s_xst[0], 16 * (NT // 2 + TL // 2))
            token_columns(n0)
            step(n0, True, False)
            step(n0 + 1, False, False)
            with act.Fori(n0 + 2, n0 + NE - 2, 2) as n:
                step(n, False, False)
                step(n + 1, False, False)
            step(n0 + NE - 2, False, False)
            step(n0 + NE - 1, False, True)
            if C:
                context_down(n0 + NE - 1)

        def dve_moe(dve, l):
            n0 = NE * l
            C = CAPC if l == 0 else 0
            par = [0]

            def token_columns(n):
                x = xT[par[0]]
                par[0] ^= 1
                dve.wait_ge(s_tx, n + 1)
                for k in range(KC // 2):
                    sc_, sh_ = columns(l, 1, k, 0)
                    ins = nc.vector.tensor_scalar(x[:, k, 0:P], ps[:, 4, (k % 4) * P:(k % 4 + 1) * P], sc_, sh_,
                                                  ALU.mult, ALU.add)
                for k in range(KC if C else 0):
                    sc_, sh_ = columns(l, 1, k, TL)
                    ins = nc.vector.tensor_scalar(x[:, k, P:P + C], ps[:, 7, k * C:(k + 1) * C], sc_, sh_,
                                                  ALU.mult, ALU.add)
                ins.then_inc(s_txd, 1)

            def result(n, first):
                dve.wait_ge(s_du, n * 4 + 4)
                if not first:
                    dve.wait_ge(s_sc, n * 16)
                e = n - n0
                nc.vector.scalar_tensor_tensor(out=eout, in0=ps[:, 4:6, :].rearrange("p b n -> p (b n)"),
                                               scalar=gcolT[:, bass.ds(e, 1)], in1=bc[:, 2 * D:3 * D],
                                               op0=ALU.mult, op1=ALU.mult).then_inc(s_eo, 1)
                if C:
                    dve.wait_ge(s_c6, n + 1)
                    for c in range(2):
                        o = tmo[0:C, c * BANK:(c + 1) * BANK]
                        ins = nc.vector.tensor_tensor(o, o, ps[32 * c:32 * c + C, 6, :], ALU.add)
                    ins.then_inc(s_c7, 1)
                    dve.wait_ge(s_c7, n + 1)
                    if not first:
                        dve.wait_ge(s_scc, n * 16)
                    nc.vector.scalar_tensor_tensor(out=outc[0:C, :], in0=tmo[0:C, :],
                                                   scalar=gcolT[0:C, bass.ds(e + 32, 1)], in1=bc[0:C, 3 * D:4 * D],
                                                   op0=ALU.mult, op1=ALU.mult).then_inc(s_eoc, 1)

            def step(n, first, second, last):
                if not last:
                    token_columns(n + 1)
                if C:
                    dve.wait_ge(s_c1, n + 1)
                    nc.vector.tensor_tensor(silx[0:2 * C, :], tmc[0:2 * C, :], ps[0:2 * C, 6, :], ALU.add).then_inc(s_c2, 1)
                dve.wait_ge(s_uu, n * 4 + 4)
                dve.wait_ge(s_sil, n + 1)
                if not first:
                    dve.wait_ge(s_th, n)
                nc.vector.tensor_tensor(hid, sil, ps[:, 2:4, :].rearrange("p b n -> p (b n)"), ALU.mult).then_inc(s_hid, 1)
                if C:
                    dve.wait_ge(s_c4, n + 1)
                    nc.vector.tensor_tensor(tmc[0:2 * C, :], tmc[0:2 * C, :], ps[0:2 * C, 7, :], ALU.add).then_inc(s_c5, 1)
                    dve.wait_ge(s_c5, n + 1)
                    dve.wait_ge(s_c3, n + 1)
                    nc.vector.tensor_tensor(hidc[0:2 * C, :], tmc[0:2 * C, :], silx[0:2 * C, :], ALU.mult).then_inc(s_hidc, 1)
                if not first:
                    result(n - 1, second)
                dve.wait_ge(s_th, n + 1)
                ins = nc.vector.tensor_copy(hidT[:, 0:4, 0:P], ps[:, 2, :].rearrange("p (k t) -> p k t", k=4))
                if C:
                    src = ps[:, 7, 0:8 * C].rearrange("p (k h t) -> p h k t", k=4, h=2)
                    for h in range(2):
                        ins = nc.vector.tensor_copy(hidT[:, 4 * h:4 * h + 4, P:P + C], src[:, h])
                ins.then_inc(s_thd, 1)

            if l == 0:
                dve.wait_ge(s_xst[1], 16 * (NT // 2))
                dve.wait_ge(s_nst, 16 * NT)
            else:
                dve.wait_ge(s_xst[1], 16 * (NT // 2 + TL // 2))
                dve.wait_ge(s_nst, 16 * (NT + TL))
            token_columns(n0)
            step(n0, True, False, False)
            step(n0 + 1, False, True, False)
            with dve.Fori(n0 + 2, n0 + NE - 2, 2) as n:
                step(n, False, False, False)
                step(n + 1, False, False, False)
            step(n0 + NE - 2, False, False, False)
            step(n0 + NE - 1, False, False, True)
            result(n0 + NE - 1, False)

        def pool_moe(pool, l):
            n0 = NE * l
            C = CAPC if l == 0 else 0

            def gather(count, first):
                n, e = count - 1, count - 1 - n0
                if not first:
                    pool.wait_ge(s_gd, n * 16)
                    pool.wait_ge(s_tx, n)
                pool.tensor_copy(gidx[:, 0:1], icolT[:, bass.ds(e, 1)]).then_inc(s_gi, 1)
                if C:
                    if not first:
                        pool.wait_ge(s_gdc, n * 16)
                    pool.tensor_copy(gidx[0:C, 1:2], icolT[0:C, bass.ds(e + 32, 1)]).then_inc(s_gic, 1)
                pool.wait_ge(s_idx, l + 1)
                pool.wait_ge(s_gi, count)
                pool.indirect_dma_start(out=xg, out_offset=None, in_=xnd,
                                        in_offset=bass.IndirectOffsetOnAxis(ap=gidx[:, 0:1], axis=0)).then_inc(s_gd, 16)
                if C:
                    pool.wait_ge(s_idx, l + 1)
                    pool.wait_ge(s_gic, count)
                    pool.indirect_dma_start(out=xgc[0:C, :], out_offset=None, in_=xnd,
                                            in_offset=bass.IndirectOffsetOnAxis(ap=gidx[0:C, 1:2], axis=0)).then_inc(s_gdc, 16)

            def scatter(count, first):
                n, e = count - 1, count - 1 - n0
                pool.wait_ge(s_eo, count)
                if not first:
                    pool.wait_ge(s_sc, n * 16)
                    if C:
                        pool.wait_ge(s_scc, n * 16)
                pool.tensor_copy(gidx[:, 2:3], icolT[:, bass.ds(e, 1)]).then_inc(s_si, 1)
                if C:
                    pool.tensor_copy(gidx[0:C, 3:4], icolT[0:C, bass.ds(e + 32, 1)]).then_inc(s_sic, 1)
                pool.wait_ge(s_idx, l + 1)
                pool.wait_ge(s_si, count)
                pool.indirect_dma_start(out=xres, out_offset=bass.IndirectOffsetOnAxis(ap=gidx[:, 2:3], axis=0),
                                        in_=eout, in_offset=None, compute_op=ALU.add).then_inc(s_sc, 16)
                if C:
                    pool.wait_ge(s_idx, l + 1)
                    pool.wait_ge(s_sic, count)
                    pool.wait_ge(s_eoc, count)
                    pool.indirect_dma_start(out=xres, out_offset=bass.IndirectOffsetOnAxis(ap=gidx[0:C, 3:4], axis=0),
                                            in_=outc[0:C, :], in_offset=None, compute_op=ALU.add).then_inc(s_scc, 16)

            pool.wait_ge(s_idx, l + 1)
            pool.wait_ge(s_nst, 16 * (NT if l == 0 else NT + TL))
            for b in range(2):
                pool.wait_ge(s_xst[b], 16 * (NT // 2 if l == 0 else NT // 2 + TL // 2))
            gather(n0 + 1, True)
            gather(n0 + 2, False)
            gather(n0 + 3, False)
            scatter(n0 + 1, True)
            with pool.Fori(n0 + 4, n0 + NE + 1) as count:
                gather(count, False)
                scatter(count - 2, False)
            scatter(n0 + NE - 1, False)
            scatter(n0 + NE, False)

        def sp_final(sp):
            n0 = norm0["final"]
            sp.wait_ge(s_sc, 16 * 2 * NE)
            sp.wait_ge(s_eo, 2 * NE)
            sp.dma_start(bc[:, 0:D], I["norm_final_g"].partition_broadcast(P)).then_inc(s_gf, 16)
            for t in range(TL + 1):
                n = n0 + t
                if t < TL:
                    if t >= 2:
                        sp.wait_ge(s_xst[n % 2], 16 * xst_count[n - 2])
                    sp.dma_start(XB[n % 2], xres[t * P:(t + 1) * P, :]).then_inc(s_xl[n % 2], 16)
                if t >= 1:
                    m = n - 1
                    sp.wait_ge(s_fin, t)
                    sp.dma_start(out.rearrange("b t d -> (b t) d")[(t - 1) * P:t * P, :], XB[m % 2]).then_inc(s_xst[m % 2], 16)
            for b in range(2):
                sp.wait_ge(s_xst[b], 16 * max(xst_count[n] for n in xst_count if n % 2 == b))

        def act_final(act):
            for t in range(TL):
                n = norm0["final"] + t
                act.wait_ge(s_xl[n % 2], 16 * xl_count[n])
                nc.scalar.activation(XN, XB[n % 2], ACT.Square, accum_out=st[:, 4 * (n % 2):4 * (n % 2) + 1]).then_inc(s_ss, 1)
                act_root(act, n)

        def dve_final(dve, own):
            dve.wait_ge(s_gf, 16)
            for t in range(TL):
                n = norm0["final"] + t
                b = n % 2
                dve.wait_ge(s_sq, n + 1)
                own.do(nc.vector.reciprocal(st[:, 4 * b + 2:4 * b + 3], st[:, 4 * b + 1:4 * b + 2]))
                nc.vector.scalar_tensor_tensor(out=XB[b], in0=XB[b], scalar=st[:, 4 * b + 2:4 * b + 3], in1=bc[:, 0:D],
                                               op0=ALU.mult, op1=ALU.mult).then_inc(s_fin, 1)

        def pe_odd(pe):
            pe.wait_ge(s_gw, 64)
            for g in range(4):
                ins = pe.transpose(ps[:, 7, g * P:(g + 1) * P], sgw[:, g, :], ident[:, :])
            ins.then_inc(s_sgt, 1)
            n0 = norm0["mix1"]
            for t in range(NT):
                norm_transposes(pe, n0 + t, 2 * (t % 2), n0 + t - 2 if t >= 2 else None)
            pe.wait_ge(s_hd, n0 + NT)
            pe.wait_ge(s_ha, n0 + NT)
            pe.wait_ge(s_sgc, 1)
            j = n_even_jobs
            for kind, b in odd_order:
                if kind in ("ga", "gx"):
                    c, d = b // 2, b % 2
                    banks_free(pe, j)
                    pe.wait_ge(s_xc, c + 1)
                    m = (8 if kind == "gx" else 0) + 4 * d + c
                    for c0, cn in SPLIT:
                        ins = pe.matmul(wide(j % 2, T)[:, c0:c0 + cn], gatew[:, m, :], XC[:, c, c0:c0 + cn],
                                        start=True, stop=True)
                    ins.then_inc(s_job, 1)
                    j += 1
                elif kind == "v":
                    if b == 0:
                        unit_in(pe, index[("w0",)])
                        unit_in(pe, index[("w1",)])
                    if b >= 2:
                        pe.wait_ge(s_vg, b - 1)
                    v_tile(pe, b, index[("w0",)])
                else:
                    job(pe, j, index[(f"{kind}{b // 2}",)], b % 2)
                    j += 1
            pe.wait_ge(s_vn, TL)
            for t in range(TL):
                if t >= 2:
                    pe.wait_ge(s_sge, t - 1)
                for g in range(4):
                    ins = pe.matmul(ps[:, 6 + t % 2, g * P:(g + 1) * P], vln[:, t, g * P:(g + 1) * P], sgwT[:, g, :],
                                    start=True, stop=True)
                ins.then_inc(s_sg, 1)

        groups = {0: (0, 3), 1: (3, 6), 2: (6, 8)}

        def act_odd(act, own):
            act.wait_ge(s_sgt, 1)
            nc.scalar.copy(sgwT.rearrange("p g n -> p (g n)"), ps[:, 7, :]).then_inc(s_sgc, 1)
            n0 = norm0["mix1"]
            for t in range(NT + 1):
                if t < NT:
                    n = n0 + t
                    act.wait_ge(s_xl[n % 2], 16 * xl_count[n])
                    act_square(act, n)
                    act_root(act, n)
                if t >= 1:
                    act_blocks(act, n0 + t - 1, 1, 0, t - 1, 2 * ((t - 1) % 2))
            j = n_even_jobs
            for kind, b in odd_order:
                if kind == "v":
                    act.wait_ge(s_vm, NT + b + 1)
                    nc.scalar.activation(vln[:, b, :], ps[:, 6 + b % 2, :], ACT.Gelu_apprx_tanh).then_inc(s_vg, 1)
                    for i, (a, z) in groups.items():
                        if b == z - 1:
                            act.wait_ge(s_vs, i + 1)
                            nc.scalar.activation(vsd[:, a:z], vmv[:, :].rearrange("p (t m) -> p t m", m=2)[:, a:z, 1],
                                                 ACT.Sqrt, bias=epsc[:, 0:1]).then_inc(s_vq, 1)
                    continue
                act.wait_ge(s_job, j + 1)
                w = wide(j % 2, jobs[j][2])
                if kind == "xb":
                    nc.scalar.copy(TMP[b], w).then_inc(s_ja, 1)
                elif kind in ("gb", "u"):
                    nc.scalar.activation(cat1[:, b + (4 if kind == "u" else 0), :], w, ACT.Gelu_apprx_tanh).then_inc(s_ja, 1)
                else:
                    c, d = b // 2, b % 2
                    x = 1 if kind == "gx" else 0
                    v0 = VEC["gate_x_b" if x else "gate_a_b"] + 4 * d + c
                    if b >= 1:
                        act.wait_ge(s_lru, b)
                    else:
                        act.wait_ge(s_xc, 4)
                    nc.scalar.activation(TMP[x], w, ACT.Sigmoid, bias=vcol[:, v0:v0 + 1]).then_inc(s_ja, 1)
                    if x:
                        m = 4 * d + c
                        act.wait_ge(s_ja, emptied["act"][j + 1])
                        act.wait_ge(s_lc, 1)
                        nc.scalar.activation(TMP[2], TMP[0], ACT.Tanh, scale=lruc[:, m:m + 1])
                        nc.scalar.activation(TMP[0], TMP[0], ACT.Exp, scale=lruc[:, 16 + m:17 + m]).then_inc(s_le, 1)
                        act.wait_ge(s_lv, b + 1)
                        nc.scalar.activation(TMP[2], TMP[2], ACT.Sqrt).then_inc(s_lq, 1)
                j += 1

        def dve_odd(dve, own):
            n0 = norm0["mix1"]
            for t in range(NT + 1):
                if t < NT:
                    dve_norm(dve, own, n0 + t)
                if t >= 1:
                    dve_blocks(dve, n0 + t - 1, 1, 0, t - 1, 2 * ((t - 1) % 2))
            j = n_even_jobs
            for kind, b in odd_order:
                if kind == "v":
                    for i, (a, z) in groups.items():
                        if b == z - 1:
                            for t in range(a, z):
                                dve.wait_ge(s_vg, t + 1)
                                ins = nc.vector.bn_stats(vst[:, 6 * t:6 * t + 6], vln[:, t, :])
                            own.do(ins)
                            for t in range(a, z):
                                ins = nc.vector.bn_aggr(vmv[:, 2 * t:2 * t + 2], vst[:, 6 * t:6 * t + 6])
                            ins.then_inc(s_vs, 1)
                            dve.wait_ge(s_vq, i + 1)
                            own.do(nc.vector.reciprocal(vsd[:, 8 + a:8 + z], vsd[:, a:z]))
                            for t in range(a, z):
                                nc.vector.tensor_scalar(vln[:, t, :], vln[:, t, :], vmv[:, 2 * t:2 * t + 1],
                                                        vsd[:, 8 + t:9 + t], ALU.subtract, ALU.mult).then_inc(s_vn, 1)
                    continue
                if kind == "xb":
                    dve.wait_ge(s_ja, emptied["act"][j + 1])
                    w0 = VEC["od_conv_w"] + b
                    tap = [vcol[:, w0 + 4 * i:w0 + 4 * i + 1] for i in range(4)]
                    own.do(nc.vector.tensor_scalar(XC[:, b, :], TMP[b], tap[2],
                                                   vcol[:, VEC["od_conv_b"] + b:VEC["od_conv_b"] + b + 1],
                                                   ALU.mult, ALU.add))
                    for i, off in ((0, -2), (1, -1), (3, 1)):
                        for s0, sn in ((0, LAT), (LAT, CTX)):
                            d0, x0 = (s0 - off, s0) if off < 0 else (s0, s0 + off)
                            ln = sn - abs(off)
                            ins = nc.vector.scalar_tensor_tensor(out=XC[:, b, d0:d0 + ln], in0=TMP[b][:, x0:x0 + ln],
                                                                 scalar=tap[i], in1=XC[:, b, d0:d0 + ln],
                                                                 op0=ALU.mult, op1=ALU.add)
                        if i < 3:
                            own.do(ins)
                        else:
                            ins.then_inc(s_xc, 1)
                elif kind == "gx":
                    c, d = b // 2, b % 2
                    dve.wait_ge(s_ja, emptied["act"][j + 1])
                    nc.vector.tensor_tensor(TMP[1], TMP[1], XC[:, c, :], ALU.mult)
                    dve.wait_ge(s_le, b + 1)
                    own.do(nc.vector.tensor_tensor(TMP[3], TMP[0], TMP[0], ALU.mult))
                    own.do(nc.vector.scalar_tensor_tensor(out=TMP[2], in0=TMP[3], scalar=1.0, in1=TMP[2],
                                                          op0=ALU.add, op1=ALU.mult))
                    nc.vector.tensor_scalar(TMP[2], TMP[2], 2e-35, None, ALU.max).then_inc(s_lv, 1)
                    dve.wait_ge(s_lq, b + 1)
                    own.do(nc.vector.tensor_tensor(TMP[1], TMP[1], TMP[2], ALU.mult))
                    h = TMP[3]
                    if d == 0:
                        own.do(nc.vector.tensor_tensor_scan(h[:, LAT:T], TMP[0][:, LAT:T], TMP[1][:, LAT:T], 0.0,
                                                            ALU.mult, ALU.add))
                        nc.vector.tensor_tensor_scan(HL[:, c, :], TMP[0][:, 0:LAT], TMP[1][:, 0:LAT], h[:, T - 1:T],
                                                     ALU.mult, ALU.add).then_inc(s_lru, 1)
                    else:
                        rev = slice(None, None, -1)
                        own.do(nc.vector.tensor_tensor_scan(h[:, LAT:T][:, rev], TMP[0][:, LAT:T][:, rev],
                                                            TMP[1][:, LAT:T][:, rev], 0.0, ALU.mult, ALU.add))
                        own.do(nc.vector.tensor_tensor_scan(h[:, 0:LAT][:, rev], TMP[0][:, 0:LAT][:, rev],
                                                            TMP[1][:, 0:LAT][:, rev], h[:, LAT:LAT + 1],
                                                            ALU.mult, ALU.add))
                        nc.vector.tensor_tensor(HL[:, c, :], HL[:, c, :], h[:, 0:LAT], ALU.add).then_inc(s_lru, 1)
                j += 1
            dve.wait_ge(s_lru, 8)
            dve.wait_ge(s_ja, emptied["act"][len(jobs)])
            for c in range(4):
                ins = nc.vector.tensor_tensor(cat1[:, c, :], cat1[:, c, :], HL[:, c, :], ALU.mult)
            ins.then_inc(s_cat, 1)
            for t in range(TL):
                dve.wait_ge(s_sg, t + 1)
                for g in range(4):
                    o = ps[:, 6 + t % 2, g * P:(g + 1) * P]
                    v0 = VEC["sg_norm_g"] + g
                    ins = nc.vector.scalar_tensor_tensor(out=o, in0=o, scalar=vcol[:, v0:v0 + 1], in1=sgb[:, g, :],
                                                         op0=ALU.mult, op1=ALU.add)
                own.do(ins)
                o = cat1[:, 4:8, t * P:(t + 1) * P]
                nc.vector.tensor_tensor(o, o, ps[:, 6 + t % 2, :].rearrange("p (g t) -> p g t", g=4),
                                        ALU.mult).then_inc(s_sge, 1)

        @block.gpsimd
        def _(pool):
            own = Chain(pool, s_po)
            own.do(pool.memset(ident[:, :], 0.0))
            pool.memset(decup[0:32, :], 0.0).then_inc(s_zero, 1)
            pool.memset(rowtmp, 0.0).then_inc(s_zero, 1)
            own.do(pool.memset(maskf[:, :], 1.0))
            own.do(pool.memset(maskb[:, :], 1.0))
            own.do(pool.memset(chunk0[:, :], 1.0))
            pool.affine_select(out=ident[:, :], in_=ident[:, :], compare_op=ALU.not_equal, fill=1.0, base=0,
                               pattern=[[-1, P]], channel_multiplier=1).then_inc(s_const, 1)
            pool.memset(epsc[:, :], EPS)
            pool.memset(ones[:, :], 1.0).then_inc(s_const, 1)
            own.do(pool.affine_select(out=maskf, in_=maskf, compare_op=ALU.is_ge, fill=0.0, base=0,
                                      pattern=[[1, P]], channel_multiplier=-1))
            pool.affine_select(out=maskf[:, CHUNK:P], in_=maskf[:, CHUNK:P], compare_op=ALU.is_ge, fill=0.0,
                               base=-CHUNK, pattern=[[0, CHUNK]], channel_multiplier=1).then_inc(s_const, 1)
            own.do(pool.affine_select(out=maskb, in_=maskb, compare_op=ALU.is_ge, fill=0.0, base=0,
                                      pattern=[[-1, P]], channel_multiplier=1))
            pool.affine_select(out=maskb[:, 0:CHUNK], in_=maskb[:, 0:CHUNK], compare_op=ALU.is_ge, fill=0.0,
                               base=CHUNK - 1, pattern=[[0, CHUNK]], channel_multiplier=-1).then_inc(s_const, 1)
            pool.memset(chunk0[:, :].rearrange("p (c i) -> p c i", i=CHUNK)[:, :, 0:1], 0.0).then_inc(s_const, 1)
            pool_moe(pool, 0)
            pool_moe(pool, 1)

        @block.sync
        def _(sp):
            def load_unit(i):
                if before[i] is not None:
                    sp.wait_ge(*used_when[before[i]])
                dst = ring[slot_of[i]]
                if stream[i][0][0] != "ada":
                    dst = dst.rearrange("p (k n) -> p k n", k=KC)
                sp.dma_start(dst, stream[i][1]).then_inc(s_load[slot_of[i]], 16)

            def load_x(n, t, src_lat, src_ctx):
                if n >= 2:
                    sp.wait_ge(s_xn, n - 1)
                sp.dma_start(XB[n % 2], tok_tile(src_lat, src_ctx, t)).then_inc(s_xl[n % 2], 16)

            for name, src, rows in small:
                sp.dma_start(vrow[VEC[name]:VEC[name] + rows, :],
                             flat(src).rearrange("(r n) -> r n", n=P)).then_inc(s_small, 16)
            sp.dma_start(adab_row[0:96, :], flat(I["ada_b"]).rearrange("(r n) -> r n", n=P)).then_inc(s_small, 16)
            for i in range(3):
                load_unit(i)
            load_x(0, 0, x_rows, c_rows)
            load_x(1, 1, x_rows, c_rows)
            for i in range(3, 8):
                load_unit(i)
            sp.dma_start(wlr[:, :].rearrange("p (k n) -> p k n", k=KC), ev_in[:, :, E_LR:E_LR + 2 * RANK]).then_inc(s_sw, 16)
            sp.wait_ge(s_zero, 1)
            for d in range(2):
                sp.dma_start(decup[RANK * d:RANK * (d + 1), 256 * d:256 * (d + 1)], I["ev_decay_up"][0, d]).then_inc(s_sw, 16)
            for t in range(2, NT):
                load_x(t, t, x_rows, c_rows)
            for i in range(8, n_even):
                load_unit(i)
            sp_wout(sp, 0)
            sp_moe(sp, 0)
            for i in range(n_even, n_even + 3):
                if i != index[("w0",)]:
                    load_unit(i)
            sp.wait_ge(s_sc, 16 * NE)
            sp.wait_ge(s_scc, 16 * NE)
            sp.dma_start(gatew[:, 0:8, :], I["od_gate_a_w"].rearrange("l d h i j -> i (l d h) j")).then_inc(s_gw, 16)
            sp.dma_start(gatew[:, 8:16, :], I["od_gate_x_w"].rearrange("l d h i j -> i (l d h) j")).then_inc(s_gw, 16)
            sp.dma_start(sgw, I["od_sg_w"].rearrange("l g i j -> i (l g) j")).then_inc(s_gw, 16)
            sp.dma_start(sgb, I["od_sg_b"].rearrange("l g i -> (l g) i").partition_broadcast(P)).then_inc(s_gw, 16)
            for t in range(NT):
                load_x(norm0["mix1"] + t, t, xres, xres[LAT:T, :])
            for i in range(n_even + 2, len(stream)):
                load_unit(i)
            sp_wout(sp, 1)
            sp_moe(sp, 1)
            sp_final(sp)
        @block.tensor
        def _(pe):
            pe_start(pe)
            pe_even(pe)
            pe_gla(pe)
            pe_wout(pe, 0)
            pe_moe(pe, 0)
            pe_odd(pe)
            pe_wout(pe, 1)
            pe_moe(pe, 1)

        @block.scalar
        def _(act):
            own = Chain(act, s_ac)
            act.wait_ge(s_vc, 1)
            s3 = silc[:, :].rearrange("p (k w) -> p k w", w=2)
            for w, name in enumerate(("c", "c_ctx")):
                nc.scalar.activation(s3[:, :, w], vcol[:, VEC[name]:VEC[name] + KC], ACT.Silu).then_inc(s_silc, 1)
            act.wait_ge(s_l1, 1)
            own.do(nc.scalar.activation(lruc[:, 8:16], lruc[:, 8:16], ACT.Exp, scale=-1.0))
            nc.scalar.activation(lruc[:, 8:16], lruc[:, 8:16], ACT.Ln, bias=1.0).then_inc(s_l2, 1)
            act.wait_ge(s_const, 2)
            for t in range(NT + 1):
                if t < NT:
                    act.wait_ge(s_xl[t % 2], 16 * xl_count[t])
                    act_square(act, t)
                    act_root(act, t)
                if t >= 1:
                    if t == 1:
                        act.wait_ge(s_scg, 1)
                    act_blocks(act, t - 1, 0, 0, t - 1, 2 * ((t - 1) % 2))
            for j in range(n_even_jobs):
                if jobs[j][3] == "act":
                    act_even_job(act, own, j)
                elif jobs[j][0] == "dec":
                    act_decay(act, own, jobs[j][1])
            act_gla(act, own)
            act_wout(act, own, 0)
            act_moe(act, 0)
            act_odd(act, own)
            act_wout(act, own, 1)
            act_moe(act, 1)
            act_final(act)

        @block.vector
        def _(dve):
            own = Chain(dve, s_dv)
            dve.wait_ge(s_vt, 1)
            nc.vector.tensor_copy(vcol[:, 0:NVEC], ps[:, 7, 0:NVEC]).then_inc(s_vc, 1)
            nc.vector.tensor_copy(adab[:, :], ps[:, 7, P:P + 96]).then_inc(s_vc, 1)
            dve.wait_ge(s_vc, 2)
            lam = vcol[:, VEC["lam"]:VEC["lam"] + 8]
            nc.vector.scalar_tensor_tensor(out=lruc[:, 8:16], in0=lam, scalar=-1.0, in1=lam,
                                           op0=ALU.mult, op1=ALU.max).then_inc(s_l1, 1)
            own.do(nc.vector.tensor_scalar(lruc[:, 0:8], lam, -1.0, 0.0, ALU.mult, ALU.max))
            dve.wait_ge(s_l2, 1)
            own.do(nc.vector.tensor_tensor(lruc[:, 0:8], lruc[:, 0:8], lruc[:, 8:16], ALU.add))
            nc.vector.tensor_scalar(lruc[:, 16:24], lruc[:, 0:8], -LRU_C, None, ALU.mult)
            nc.vector.tensor_scalar(lruc[:, 0:8], lruc[:, 0:8], LRU_C, None, ALU.mult).then_inc(s_lc, 1)
            dve_norm(dve, own, 0)
            dve_ada(dve, own, 0)
            dve.wait_ge(s_scg, 1)
            for t in range(NT + 1):
                if 1 <= t < NT:
                    dve_norm(dve, own, t)
                if t >= 1:
                    dve_blocks(dve, t - 1, 0, 0, t - 1, 2 * ((t - 1) % 2))
            for pd in range(4):
                dve_decay_in(dve, pd)
                if pd >= 1:
                    dve_decay_out(dve, own, pd - 1)
            dve_decay_out(dve, own, 3)
            for t in range(NT):
                dve.wait_ge(s_vm, t + 1)
                nc.vector.tensor_copy(vtok[:, t, :], ps[:, 6 + t % 2, :]).then_inc(s_ve, 1)
            for i in range(index[("q",)], n_even):
                key = stream[i][0]
                if key[0] == "ada":
                    if key[3] == KC - 1:
                        dve_ada(dve, own, 3 * key[1] + key[2])
                else:
                    for j in unit_jobs[i]:
                        if jobs[j][3] == "dve":
                            dve_even_job(dve, own, j)
            dve_gla(dve, own)
            dve_wout(dve, own, 0)
            dve_moe(dve, 0)
            dve_odd(dve, own)
            dve_wout(dve, own, 1)
            dve_moe(dve, 1)
            dve_final(dve, own)


_INS = ["x", "c", "ctx", "c_ctx", "ada_w", "ada_b", "norm_mix_g", "norm_ffn_g", "norm_final_g",
        "ev_w_in", "ev_conv_w", "ev_conv_b", "ev_decay_up", "ev_decay_b", "ev_norm_g", "ev_w_out",
        "od_w_in", "od_conv_w", "od_conv_b", "od_gate_a_w", "od_gate_a_b", "od_gate_x_w", "od_gate_x_b",
        "od_lambda", "od_sg_norm_g", "od_sg_w", "od_sg_b", "od_w_out",
        "moe_router", "moe_w_gate", "moe_w_up", "moe_w_down"]


def kernel(**inputs):
    import numpy as np
    import concourse.bacc as bacc
    from concourse.bass_utils import run_bass_kernel_spmd

    nc = bacc.Bacc("TRN2", target_bir_lowering=False, num_devices=1)
    arrays, aps = {}, {}
    for name in _INS:
        a = np.ascontiguousarray(inputs[name])
        arrays[f"in_{name}"] = a
        aps[name] = nc.dram_tensor(f"in_{name}", a.shape, mybir.dt.from_np(a.dtype), kind="ExternalInput").ap()
    out = nc.dram_tensor("out_0", (1, LAT, D), F32, kind="ExternalOutput").ap()
    build(nc, aps, out)
    return run_bass_kernel_spmd(nc, [arrays], core_ids=[0]).results[0]["out_0"]
```

```python
from contextlib import ExitStack

import concourse.bass as bass
from concourse import mybir

F32 = mybir.dt.float32
F32R = mybir.dt.float32r
U32 = mybir.dt.uint32
ALU = mybir.AluOpType
ACT = mybir.ActivationFunctionType
AXX = mybir.AxisListType.X

P = 128
D = 1024
KC = D // P
TL = 8
TC = 2
NT = TL + TC
T = NT * P
LAT = TL * P
CTX = TC * P
BANK = 512
EPS = 1e-6

HEADS = 4
DK = 64
CHUNK = 64
NCH = T // CHUNK
TAU = 16.0
GRID = 64
RANK = 16
LRU_C = 8.0

NE = 16
CAPL = 2 * LAT // NE
CAPC = 2 * CTX // NE
UNIT = 2048
WS = 3
EU = 12

E_BG, E_CG, E_XA, E_Q, E_G, E_K, E_V, E_LR = 0, 512, 1024, 1536, 1792, 2304, 2560, 3072
O_XB, O_GB, O_U, O_V = 0, 512, 1024, 1536

VEC = {}
_row = 0
for _name, _n in (("c", 8), ("c_ctx", 8), ("mix_g", 16), ("ffn_g", 16), ("ev_conv_w", 12), ("ev_conv_b", 4),
                  ("decay_b", 4), ("ev_norm_g", 4), ("od_conv_w", 16), ("od_conv_b", 4), ("gate_a_b", 8),
                  ("gate_x_b", 8), ("lam", 8), ("sg_norm_g", 4)):
    VEC[_name] = _row
    _row += _n
NVEC = _row


def build(nc, I, out):
    ctx = ExitStack()
    with ctx:
        def sem(name):
            return ctx.enter_context(nc.semaphore(name))

        def sb(name, words, dt=F32):
            return ctx.enter_context(nc.sbuf_tensor(name, [P, words], dt))

        def sb_twice(name, words):
            with nc.sbuf_tensor(name, [P, words], F32) as plain:
                pass
            return plain, ctx.enter_context(nc.sbuf_tensor(name + "_r", [P, words], F32R))

        ident = sb("ident", P)
        ones = sb("ones", P)
        vcol = sb("vcol", P)
        adab = sb("adab", 96)
        silc = sb("silc", 16)
        modc = sb("modc", 192)
        scg = sb("scg", 64)
        bc, bc_r = sb_twice("bc", 4 * D)
        maskf = bc[:, 0:P]
        maskb = bc[:, P:2 * P]
        chunk0 = bc[:, 256:256 + T]
        lrT = bc[:, 1536:1536 + T]
        decup = bc[:, 2816:3328]
        wlr = bc[:, 3328:3328 + KC * 2 * RANK]
        rowtmp = bc[:, 3584:4096]
        tkf = sb("tkf", P)
        st = sb("st", 64)
        router = sb("router", KC * NE)
        dec = sb("dec", 4 * NCH)
        lruc = sb("lruc", 24)
        epsc = sb("epsc", 1)
        vst = sb("vst", 6 * TL)
        vmv = sb("vmv", 2 * TL)
        vsd = sb("vsd", 2 * TL)
        gcolT = sb("gcolT", 48)
        icolT = sb("icolT", 48, U32)
        gidx = sb("gidx", 4, U32)
        sm = sb("sm", 4 * NE)

        R_H, R_Hr = sb_twice("R_H", KC * T)
        R_C, R_Cr = sb_twice("R_C", KC * T)
        vrow, adab_row = R_C[:, 0:P], R_C[:, P:2 * P]
        R_M, R_Mr = sb_twice("R_M", 15360)
        R_W, R_Wr = sb_twice("R_W", 11264)

        hT = R_H[:, :].rearrange("p (k t) -> p k t", k=KC)
        cat = R_C[:, :].rearrange("p (k t) -> p k t", k=KC)
        vtok = R_M[:, 0:NT * 512].rearrange("p (t n) -> p t n", t=NT)
        kT = R_M[:, 5120:7680].rearrange("p (c t) -> p c t", c=2)
        qT = R_M[:, 7680:10240].rearrange("p (c t) -> p c t", c=2)
        BX = R_M[:, 10240:15360].rearrange("p (c t) -> p c t", c=4)
        ring = [R_W[:, UNIT * s:UNIT * (s + 1)] for s in range(WS)]
        TMP = [R_W[:, 6144 + T * i:6144 + T * (i + 1)] for i in range(4)]
        wout = R_W[:, 0:8192].rearrange("p (k n) -> p k n", k=KC)
        XB = [R_W[:, 8192 + D * i:8192 + D * (i + 1)] for i in range(2)]
        XN = R_W[:, 10240:11264]
        whi_out = R_Hr[:, 0:8192].rearrange("p (k n) -> p k n", k=KC)
        wlo_out = R_Wr[:, 0:8192].rearrange("p (k n) -> p k n", k=KC)
        cathi = [R_Mr[:, 12288 + D * i:12288 + D * (i + 1)].rearrange("p (k t) -> p k t", k=KC) for i in range(2)]
        hN = [R_H[:, 8192 + D * i:8192 + D * (i + 1)].rearrange("p (k t) -> p k t", k=KC) for i in range(2)]
        diag = [R_H[:, 8192 + D * i:8192 + D * (i + 1)] for i in range(2)]
        ktok = R_H[:, 0:2560].rearrange("p (t r d) -> p t r d", t=NT, r=2)
        SIN = R_H[:, 2560:7680].rearrange("p (r c e) -> p r c e", r=2, c=NCH)
        attS = R_H[:, 7680:9728].rearrange("p (b r n) -> p b r n", b=2, r=2)
        TST = R_H[:, 9728:10240].rearrange("p (r b e) -> p r b e", r=2, b=2)
        SQ = [R_W[:, 8192 + 512 * i:8192 + 512 * (i + 1)] for i in range(2)]
        RS = [R_W[:, 9216 + 512 * i:9216 + 512 * (i + 1)] for i in range(2)]
        XC = R_M[:, 0:5120].rearrange("p (c t) -> p c t", c=4)
        HL = R_M[:, 5120:9216].rearrange("p (c t) -> p c t", c=4)
        vln = R_M[:, 9216:13312].rearrange("p (t n) -> p t n", t=TL)
        sgw = R_M[:, 13312:13824].rearrange("p (g n) -> p g n", g=4)
        sgwT = R_M[:, 13824:14336].rearrange("p (g n) -> p g n", g=4)
        sgb = R_M[:, 14848:15360].rearrange("p (g n) -> p g n", g=4)
        cat1 = R_C[:, 0:8192].rearrange("p (k t) -> p k t", k=KC)
        catlo = [R_Cr[:, :].rearrange("p (k t) -> p k t", k=KC), R_Cr[:, 0:8192].rearrange("p (k t) -> p k t", k=KC)]
        gatew = R_C[:, 8192:10240].rearrange("p (m j) -> p m j", m=16)
        affT = R_M[:, 14336:15360]
        raw = [R_M[:, UNIT * s:UNIT * (s + 1)] for s in range(7)] + [R_H[:, 0:UNIT]]
        wlo = [R_Hr[:, UNIT * s:UNIT * (s + 1)] for s in range(1, 5)]
        whi = [R_Wr[:, UNIT * s:UNIT * (s + 1)] for s in range(4)]
        xhi = [bc_r[:, D * i:D * (i + 1)].rearrange("p (k t) -> p k t", k=KC) for i in range(2)]
        hidh = R_Mr[:, 14336:15360].rearrange("p (k t) -> p k t", k=KC)
        xT = [R_C[:, 1280 * i:1280 * (i + 1)].rearrange("p (k c) -> p k c", k=KC) for i in range(2)]
        hidT = R_C[:, 2560:3840].rearrange("p (k c) -> p k c", k=KC)
        xlo = [R_Cr[:, 1280 * i:1280 * (i + 1)].rearrange("p (k c) -> p k c", k=KC) for i in range(2)]
        hidlo = R_Cr[:, 2560:3840].rearrange("p (k c) -> p k c", k=KC)
        xg = R_C[:, 3840:4864]
        xgc = R_C[:, 4864:5888]
        tmc = R_C[:, 5888:6400]
        silx = R_C[:, 6400:6912]
        hidc = R_C[:, 6912:7424]
        outc = R_C[:, 7424:8448]
        tkv = R_C[:, 9472:9600]
        tki = R_C[:, 9600:9728].bitcast(U32)
        tmo = R_C[:, 8448:9472]
        late_rows = [R_C[:, 5888 + BANK * i:5888 + BANK * (i + 1)] for i in range(2)]
        late_cols = [R_C[:, 7424 + BANK * i:7424 + BANK * (i + 1)] for i in range(2)]
        sil, hid, eout = XB[0], XB[1], XN
        FB = [R_M[:, D * t:D * (t + 1)] for t in range(TL)]

        ps = ctx.enter_context(nc.psum_tensor("ps", [P, 8, BANK], F32))

        def wide(s, n):
            return ps[:, 3 * s:3 * s + 3, :].rearrange("p b n -> p (b n)")[:, 0:n]

        xres = nc.dram_tensor("xres", [T, D], F32).ap()
        xnd = nc.dram_tensor("xnd", [T, D], F32).ap()

        x_rows = I["x"].rearrange("b t d -> (b t) d")
        c_rows = I["ctx"].rearrange("b t d -> (b t) d")

        def tok_tile(src_lat, src_ctx, t):
            return src_lat[t * P:(t + 1) * P, :] if t < TL else src_ctx[(t - TL) * P:(t - TL + 1) * P, :]

        ev_in = I["ev_w_in"].rearrange("l (k p) n -> (l p) k n", p=P)
        od_in = I["od_w_in"].rearrange("l (k p) n -> (l p) k n", p=P)

        def ada_unit(l, g, k):
            return ("ada", l, g, k), I["ada_w"][l, k * P:(k + 1) * P, g * 2048:(g + 1) * 2048]

        def col_unit(name, src, col):
            return (name,), src[:, :, col:col + 256]

        stream = [ada_unit(0, 0, k) for k in range(KC)]
        stream += [col_unit("k", ev_in, E_K), col_unit("v0", ev_in, E_V), col_unit("v1", ev_in, E_V + 256)]
        slot_of = [i % WS for i in range(len(stream))]
        gap_ada = [ada_unit(l, g, k) for l, g in ((0, 1), (0, 2), (1, 0)) for k in range(KC)]
        proj = [("q", E_Q), ("g0", E_G), ("g1", E_G + 256)] + \
               [(f"{n}{h}", c + 256 * h) for h in range(2) for n, c in (("cg", E_CG), ("xa", E_XA), ("bg", E_BG))]
        even_order, slot, job_no, rows_due = [], (slot_of[-1] + 1) % WS, 7, None
        for name, col in proj:
            unit_no = len(stream)
            stream.append(col_unit(name, ev_in, col))
            slot_of.append(slot)
            for half in range(2):
                even_order.append(("job", job_no, unit_no, half))
                job_no += 1
                if rows_due is not None:
                    even_order.append(("rows", rows_due))
                    rows_due = None
                for beside in ((1, 2), (1,))[half]:
                    if gap_ada:
                        key = gap_ada[0][0]
                        even_order.append(("ada", len(stream)))
                        stream.append(gap_ada.pop(0))
                        slot_of.append((slot + beside) % WS)
                        if key[3] == KC - 1:
                            rows_due = 3 * key[1] + key[2]
                            even_order.append(("copy", rows_due))
            slot = (slot + 2) % WS
        assert not gap_ada and rows_due is None
        n_even = len(stream)
        LATE = (4, 5)
        for l, g in ((1, 1), (1, 2)):
            for k in range(KC):
                slot_of.append(len(stream) % WS)
                stream.append(ada_unit(l, g, k))
        n_late = len(stream)
        for name, col, slot in (("xb0", O_XB, 2), ("xb1", O_XB + 256, 0), ("w0", O_V, 0), ("w1", O_V + 256, 1),
                                ("gb0", O_GB, 2), ("gb1", O_GB + 256, 2), ("u0", O_U, 0), ("u1", O_U + 256, 1)):
            stream.append(col_unit(name, od_in, col))
            slot_of.append(slot)
        index = {key: i for i, (key, _) in enumerate(stream)}
        n_in_slot = [slot_of[:i + 1].count(slot_of[i]) for i in range(len(stream))]
        before = [max([j for j in range(i) if slot_of[j] == slot_of[i]], default=None) for i in range(len(stream))]
        assert slot_of[index[("v0",)]] + 1 == slot_of[index[("v1",)]]

        even_jobs = [("lr", 0, T, "act"), ("k", 0, T, "act"), ("k", 1, T, "act")] + \
                    [("dec", i, T, "dve") for i in range(4)] + \
                    [("q", 0, T, "act"), ("q", 1, T, "act")] + [("g", i, T, "act") for i in range(4)]
        for h in range(2):
            even_jobs += [("cg", 2 * h, T, "act"), ("cg", 2 * h + 1, T, "act"), ("xa", 2 * h, T, "dve"),
                          ("xa", 2 * h + 1, T, "dve"), ("bg", 2 * h, T, "dve"), ("bg", 2 * h + 1, T, "dve")]
        odd_order = [("xb", c) for c in range(4)]
        fill = [[("v", 0), ("v", 1), ("v", 2)], [("v", 3), ("v", 4), ("v", 5)], [("v", 6), ("v", 7), ("gb", 0)],
                [("gb", 1)], [("gb", 2)], [("gb", 3), ("u", 0)], [("u", 1), ("u", 2)], [("u", 3)]]
        for it in range(8):
            odd_order += [("ga", it), ("gx", it)] + fill[it]
        odd_jobs = [(k, i, T if k in ("xb", "ga", "gx") else LAT, "act") for k, i in odd_order if k != "v"]

        jobs = even_jobs + odd_jobs
        n_even_jobs = len(even_jobs)
        emptied = {"act": [0], "dve": [0]}
        for j in jobs:
            for e in emptied:
                emptied[e].append(emptied[e][-1] + (j[3] == e))
        job_at = {j[:2] + (i >= n_even_jobs,): i for i, j in enumerate(jobs)}

        norm0 = {"mix0": 0, "ffn0": NT, "mix1": 2 * NT, "ffn1": 3 * NT, "final": 3 * NT + TL}

        def sems(names):
            return [sem(n) for n in names.split()]

        s_const, s_zero, s_small = sems("s_const s_zero s_small")
        s_load = [sem(f"s_load{i}") for i in range(WS)]
        s_used, s_vt, s_vc, s_silc = sems("s_used s_vt s_vc s_silc")
        s_adlr, s_adlt, s_adlc = sems("s_adlr s_adlt s_adlc")
        s_adar, s_adat, s_adac, s_scg = sems("s_adar s_adat s_adac s_scg")
        s_diag, s_bcp, s_bc = sems("s_diag s_bcp s_bc")
        s_dv, s_ac, s_po = sems("s_dv s_ac s_po")
        s_xl = sems("s_xl0 s_xl1")
        s_ss, s_sq, s_xn, s_tp, s_hd, s_ha = sems("s_ss s_sq s_xn s_tp s_hd s_ha")
        s_job, s_ja, s_jd, s_vm, s_ve = sems("s_job s_ja s_jd s_vm s_ve")
        s_dx, s_dl, s_eb, s_qk = sems("s_dx s_dl s_eb s_qk")
        s_kt, s_kc, s_up, s_tst, s_sin = sems("s_kt s_kc s_up s_tst s_sin")
        s_at, s_am, s_o, s_osq, s_ms, s_rs, s_of = sems("s_at s_am s_o s_osq s_ms s_rs s_of")
        s_wo = sems("s_wo0 s_wo1")
        s_wh, s_wl, s_ch, s_cl = sems("s_wh s_wl s_ch s_cl")
        s_y, s_x1, s_ob = sems("s_y s_x1 s_ob")
        s_dsc, s_cv, s_sw, s_cat, s_sge, s_lru = sems("s_dsc s_cv s_sw s_cat s_sge s_lru")
        s_el = [sem(f"s_el{i}") for i in range(8)]
        s_hi, s_lo, s_mm, s_txh, s_txl = sems("s_hi s_lo s_mm s_txh s_txl")
        s_gd, s_gdc, s_gi, s_gic, s_si, s_sic = sems("s_gd s_gdc s_gi s_gic s_si s_sic")
        s_tx, s_txd, s_txa, s_sil, s_hid, s_hidc = sems("s_tx s_txd s_txa s_sil s_hid s_hidc")
        s_c1, s_c2, s_c3, s_c4, s_c5, s_c6, s_c7 = sems("s_c1 s_c2 s_c3 s_c4 s_c5 s_c6 s_c7")
        s_th, s_thd, s_tha, s_eo, s_eoc, s_sc, s_scc = sems("s_th s_thd s_tha s_eo s_eoc s_sc s_scc")
        s_gw, s_sgt, s_sgc, s_xc, s_vg, s_vn, s_vs, s_vq = sems("s_gw s_sgt s_sgc s_xc s_vg s_vn s_vs s_vq")
        s_sg, s_lc, s_le, s_lv, s_lq, s_l1, s_l2 = sems("s_sg s_lc s_le s_lv s_lq s_l1 s_l2")
        s_gf, s_fin, s_out = sems("s_gf s_fin s_out")
        s_xf = [sem(f"s_xf{i}") for i in range(TL)]
        s_xst, s_nst = sems("s_xst0 s_xst1"), sem("s_nst")
        s_lg, s_mx, s_ex, s_af, s_aft, s_afc = sems("s_lg s_mx s_ex s_af s_aft s_afc")
        s_tk, s_tkt, s_idx, s_rt = sems("s_tk s_tkt s_idx s_rt")

        class Chain:

            def __init__(self, eng, s):
                self.eng, self.s, self.n = eng, s, 0

            def mark(self, ins):
                self.n += 1
                ins.then_inc(self.s, 1)
                return self.n

            def do(self, ins):
                self.eng.wait_ge(self.s, self.mark(ins))

        N_CONST = 5
        small = [("c", I["c"], 8), ("c_ctx", I["c_ctx"], 8), ("mix_g", I["norm_mix_g"], 16),
                 ("ffn_g", I["norm_ffn_g"], 16), ("ev_conv_w", I["ev_conv_w"], 12), ("ev_conv_b", I["ev_conv_b"], 4),
                 ("decay_b", I["ev_decay_b"], 4), ("ev_norm_g", I["ev_norm_g"], 4),
                 ("od_conv_w", I["od_conv_w"], 16), ("od_conv_b", I["od_conv_b"], 4),
                 ("gate_a_b", I["od_gate_a_b"], 8), ("gate_x_b", I["od_gate_x_b"], 8), ("lam", I["od_lambda"], 8),
                 ("sg_norm_g", I["od_sg_norm_g"], 4)]
        N_SMALL = len(small) + 1
        DONE_SMALL = 16 * N_SMALL

        def flat(ap):
            names = "abcd"[:len(ap.shape)]
            return ap if len(names) == 1 else ap.rearrange(" ".join(names) + " -> (" + " ".join(names) + ")")

        xl_count, xst_count = {}, {}
        for n in range(norm0["final"]):
            xl_count[n] = n // 2 + 1
        stored = [n for n in range(norm0["final"])
                  if norm0["ffn0"] <= n < norm0["mix1"] or n >= norm0["ffn1"]]
        for n in stored:
            xst_count[n] = sum(1 for m in stored if m <= n and m % 2 == n % 2)

        block = ctx.enter_context(nc.Block())

        used_when, n_ada = [], 0
        unit_jobs = {}
        for i, (key, _) in enumerate(stream):
            if key[0] == "ada":
                n_ada += 1
                used_when.append((s_used, n_ada))
            elif key[0] in ("v0", "v1"):
                used_when.append((s_vm, NT))
            elif key[0] in ("w0", "w1"):
                used_when.append((s_vm, NT + TL))
            else:
                kind, half = ("k", 0) if key[0] in "kq" else (key[0][:-1], int(key[0][-1]))
                kind = key[0] if key[0] in "kq" else kind
                unit_jobs[i] = [job_at[(kind, 2 * half + h, i >= n_even)] for h in range(2)]
                used_when.append((s_job, unit_jobs[i][1] + 1))

        SPLIT = [(0, BANK), (BANK, BANK), (2 * BANK, T - 2 * BANK)]

        def unit_in(pe, i):
            pe.wait_ge(s_load[slot_of[i]], 16 * n_in_slot[i])

        def ada(pe, i):
            _, l, g, k = stream[i][0]
            if k == 0 and 3 * l + g > 0:
                pe.wait_ge(s_adar, min(3 * l + g, 4))
                if 3 * l + g > LATE[0]:
                    pe.wait_ge(s_adlr, 3 * l + g - LATE[0])
            unit_in(pe, i)
            for q in range(4):
                ins = pe.matmul(ps[32 * q:32 * q + 2, 6, :], silc[:, 2 * k:2 * k + 2],
                                ring[slot_of[i]][:, q * BANK:(q + 1) * BANK], start=(k == 0), stop=(k == KC - 1))
            ins.then_inc(s_used, 1)

        def ada_rows(pe, a):
            pe.wait_ge(s_adar, a + 1)
            pe.wait_ge(s_vc, 2) if a == 0 else pe.wait_ge(s_adac, a)
            for j in range(4):
                ins = pe.transpose(ps[:, 7, j * P:(j + 1) * P], rowtmp[:, j * P:(j + 1) * P], ident[:, :])
            ins.then_inc(s_adat, 1)

        def before_mixer(n):
            return n < norm0["ffn0"] or norm0["mix1"] <= n < norm0["ffn1"]

        def normed(n):
            return R_C[:, D * (1 + n % 2):D * (2 + n % 2)] if before_mixer(n) else XN

        def pe_late_ada(pe):
            pe.wait_ge(s_x1, NT)
            for a in LATE:
                for i in range(n_even + (a - 4) * KC, n_even + (a - 3) * KC):
                    ada(pe, i)
                pe.wait_ge(s_adlr, a - 3)
                for j in range(4):
                    ins = pe.transpose(ps[:, 7 - 2 * (a - 4), j * P:(j + 1) * P],
                                       late_rows[a - 4][:, j * P:(j + 1) * P], ident[:, :])
                ins.then_inc(s_adlt, 1)

        def act_late_ada(act):
            act.wait_ge(s_y, NT)
            for a in LATE:
                act.wait_ge(s_used, KC * (a + 1))
                for q in range(4):
                    ins = nc.scalar.copy(late_rows[a - 4][32 * q:32 * q + 2, :], ps[32 * q:32 * q + 2, 6, :])
                ins.then_inc(s_adlr, 1)
                act.wait_ge(s_adlt, a - 3)
                nc.scalar.copy(late_cols[a - 4], ps[:, 7 - 2 * (a - 4), :]).then_inc(s_adlc, 1)

        def norm_transposes(pe, n, bank, last):
            pe.wait_ge(s_xn, n + 1)
            if last is not None:
                pe.wait_ge(s_hd, last + 1)
                pe.wait_ge(s_ha, last + 1)
            for k in range(KC):
                ins = pe.transpose(ps[:, bank + k // 4, (k % 4) * P:(k % 4 + 1) * P], normed(n)[:, k * P:(k + 1) * P],
                                   ident[:, :])
            ins.then_inc(s_tp, 1)

        def banks_free(pe, j):
            if j >= 2:
                if emptied["act"][j - 1]:
                    pe.wait_ge(s_ja, emptied["act"][j - 1])
                if emptied["dve"][j - 1]:
                    pe.wait_ge(s_jd, emptied["dve"][j - 1])

        def job(pe, j, i, half):
            n = jobs[j][2]
            banks_free(pe, j)
            unit_in(pe, i)
            w = ring[slot_of[i]].rearrange("p (k n) -> p k n", k=KC)
            for c0, cn in SPLIT:
                if c0 >= n:
                    break
                for k in range(KC):
                    ins = pe.matmul(wide(j % 2, n)[:, c0:c0 + cn], w[:, k, half * P:(half + 1) * P],
                                    hT[:, k, c0:c0 + cn], start=(k == 0), stop=(k == KC - 1))
            ins.then_inc(s_job, 1)

        def v_tile(pe, t, unit):
            v2 = R_W[:, UNIT * slot_of[unit]:UNIT * slot_of[unit] + 2 * UNIT].rearrange(
                "p (u k n) -> p k u n", u=2, k=KC)
            out_ = ps[:, 6 + t % 2, :].rearrange("p (u n) -> p u n", u=2)
            for k in range(KC):
                ins = pe.matmul(out_, hT[:, k, t * P:(t + 1) * P], v2[:, k, :, :],
                                start=(k == 0), stop=(k == KC - 1))
            ins.then_inc(s_vm, 1)

        def pe_start(pe):
            pe.wait_ge(s_const, 1)
            pe.wait_ge(s_small, DONE_SMALL)
            pe.transpose(ps[:, 7, 0:NVEC], vrow[0:NVEC, :], ident[0:NVEC, 0:NVEC])
            pe.transpose(ps[:, 7, P:P + 96], adab_row[0:96, :], ident[0:96, 0:96]).then_inc(s_vt, 1)
            pe.wait_ge(s_silc, 2)
            for i in range(8):
                ada(pe, i)
            ada_rows(pe, 0)
            for t in range(NT):
                norm_transposes(pe, t, 2 * (t % 2), t - 2 if t >= 2 else None)

        def pe_even(pe):
            pe.wait_ge(s_sw, 48)
            pe.wait_ge(s_hd, NT)
            pe.wait_ge(s_ha, NT)
            for c0, cn in SPLIT:
                for k in range(KC):
                    ins = pe.matmul(wide(0, T)[0:32, c0:c0 + cn], wlr[:, k * 32:(k + 1) * 32], hT[:, k, c0:c0 + cn],
                                    start=(k == 0), stop=(k == KC - 1))
            ins.then_inc(s_job, 1)
            j = 1
            for half in range(2):
                job(pe, j, index[("k",)], half)
                j += 1
            for pd in range(4):
                banks_free(pe, j)
                for c0, cn in SPLIT:
                    ins = pe.matmul(wide(j % 2, T)[:, c0:c0 + cn], decup[0:32, pd * P:(pd + 1) * P],
                                    lrT[0:32, c0:c0 + cn], start=True, stop=True)
                ins.then_inc(s_job, 1)
                j += 1
            unit_in(pe, index[("v0",)])
            unit_in(pe, index[("v1",)])
            pe.wait_ge(s_adar, 1)
            pe.wait_ge(s_adac, 1)
            for t in range(NT):
                if t >= 2:
                    pe.wait_ge(s_ve, t - 1)
                v_tile(pe, t, index[("v0",)])
            for what, *at in even_order:
                if what == "ada":
                    if stream[at[0]][0][1:] == (0, 1, 0):
                        pe.wait_ge(s_ve, NT)
                    ada(pe, at[0])
                elif what == "rows":
                    ada_rows(pe, at[0])
                elif what == "job":
                    assert j == at[0]
                    job(pe, *at)
                    j += 1
            assert j == n_even_jobs

        order = [[16, 17, 18, 19] + list(range(16)), [19, 18, 17, 16] + list(range(15, -1, -1))]

        def pe_gla(pe):
            pe.wait_ge(s_const, N_CONST)
            for p in range(2):
                pe.wait_ge(s_qk, p + 1)
                for g in range(5):
                    n = 5 * p + g
                    if p == 0 and g == 0:
                        pe.wait_ge(s_ja, emptied["act"][n_even_jobs])
                        pe.wait_ge(s_jd, emptied["dve"][n_even_jobs])
                    if n >= 2:
                        pe.wait_ge(s_kc, n - 1)
                    for q in range(4):
                        t, r = 2 * g + q // 2, q % 2
                        ins = pe.transpose(ps[:, n % 2, q * P:(q + 1) * P], BX[:, 2 * r + p, t * P:(t + 1) * P],
                                           ident[:, :])
                    ins.then_inc(s_kt, 1)
                pe.wait_ge(s_kc, 5 * (p + 1))
                for b in range(NCH // 4):
                    if b >= 2:
                        pe.wait_ge(s_tst, 2 * NCH * p + 8 * (b - 1))
                    for s in range(4 * b, 4 * b + 4):
                        for r in range(2):
                            c = order[r][s]
                            h0, t = 64 * (c % 2), c // 2
                            for hh in range(2):
                                ins = pe.matmul(ps[64 * hh:64 * hh + 64, 2 * (b % 2) + c % 2, (s % 4) * P:(s % 4 + 1) * P],
                                                ktok[h0:h0 + 64, t, r, 64 * hh:64 * hh + 64],
                                                vtok[h0:h0 + 64, t, (2 * p + hh) * P:(2 * p + hh + 1) * P],
                                                start=True, stop=True)
                    ins.then_inc(s_up, 1)
                pe.wait_ge(s_sin, 2 * (NCH - 1) * (p + 1))
                pe.wait_ge(s_tst, 2 * NCH * (p + 1))

                def scores(g):
                    n = 5 * p + g
                    if n >= 1:
                        pe.wait_ge(s_am, n)
                    for hh in range(2):
                        for r in range(2):
                            for tt in range(2):
                                t = 2 * g + tt
                                qd = (qT if r == 0 else kT)[64 * hh:64 * hh + 64, p, t * P:(t + 1) * P]
                                ins = pe.matmul(ps[:, 4 + hh, (2 * r + tt) * P:(2 * r + tt + 1) * P],
                                                BX[64 * hh:64 * hh + 64, 2 * r + p, t * P:(t + 1) * P], qd,
                                                start=True, stop=True)
                    ins.then_inc(s_at, 1)

                def outputs(g):
                    n = 5 * p + g
                    pe.wait_ge(s_am, n + 1)
                    if n >= 1:
                        pe.wait_ge(s_osq, n)
                        pe.wait_ge(s_ob, n)
                    for hh in range(2):
                        for tt in range(2):
                            t = 2 * g + tt
                            o = ps[:, 6 + hh, tt * P:(tt + 1) * P]
                            vh = vtok[:, t, (2 * p + hh) * P:(2 * p + hh + 1) * P]
                            mm = [(o, vh, attS[:, n % 2, r, (2 * hh + tt) * P:(2 * hh + tt + 1) * P]) for r in range(2)]
                            for r in range(2):
                                for cc in range(2):
                                    c = 2 * t + cc
                                    if c != order[r][0]:
                                        qd = (qT if r == 0 else kT)[64 * hh:64 * hh + 64, p, c * 64:(c + 1) * 64]
                                        mm.append((o[:, cc * 64:(cc + 1) * 64], SIN[64 * hh:64 * hh + 64, r, c, :], qd))
                            for x, (oo, lhs, rhs) in enumerate(mm):
                                ins = pe.matmul(oo, lhs, rhs, start=(x == 0), stop=(x == len(mm) - 1))
                    ins.then_inc(s_o, 1)

                def means(g):
                    n = 5 * p + g
                    pe.wait_ge(s_osq, n + 1)
                    if g >= 2:
                        pe.wait_ge(s_rs, n - 1)
                    pe.matmul(ps[:, n % 2, :], ones[:, :], SQ[n % 2], start=True, stop=True).then_inc(s_ms, 1)

                scores(0)
                for g in range(5):
                    if g < 4:
                        scores(g + 1)
                    if g >= 1:
                        means(g - 1)
                    outputs(g)
                means(4)
                pe.wait_ge(s_of, 5 * (p + 1))

        def pe_gates_as_rows(pe, l):
            for m in range(len(gate_rows(l))):
                n = (0 if l == 0 else 4) + m
                pe.wait_ge(s_diag, n + 1)
                if n >= 2:
                    pe.wait_ge(s_bc, n - 1)
                for c in range(2):
                    ins = pe.matmul(ps[:, 2 * (n % 2) + c, :], ones[:, :], diag[n % 2][:, c * BANK:(c + 1) * BANK],
                                    start=True, stop=True)
                ins.then_inc(s_bcp, 1)

        def pe_wout(pe, l):
            nt = NT if l == 0 else TL
            n0 = norm0["ffn0"] if l == 0 else norm0["ffn1"]
            r0 = 0 if l == 0 else NT
            if l == 1:
                pe.wait_ge(s_ja, emptied["act"][len(jobs)])
            pe_gates_as_rows(pe, l)
            pe.wait_ge(s_bc, 4 if l == 0 else 6)
            pe.wait_ge(s_wo[0], 16 * (l + 1))
            pe.wait_ge(s_wo[1], 16 * (l + 1))
            if l == 0:
                pe.wait_ge(s_of, 10)
            else:
                pe.wait_ge(s_cat, 1)
                pe.wait_ge(s_sge, TL)
            pe.wait_ge(s_wh, 4 * (l + 1))
            pe.wait_ge(s_wl, 4 * (l + 1))
            for i in range(nt + 3):
                if i < nt:
                    if i >= 2:
                        pe.wait_ge(s_x1, r0 + i - 1)
                    pe.wait_ge(s_ch, r0 + i + 1)
                    pe.wait_ge(s_cl, r0 + i + 1)
                    for c in range(2):
                        for k in range(KC):
                            o, cs = ps[:, 4 + 2 * (i % 2) + c, :], slice(c * BANK, (c + 1) * BANK)
                            xh, xl = cathi[i % 2][:, k, :], catlo[l][:, k, i * P:(i + 1) * P]
                            pe.matmul(o, xh, whi_out[:, k, cs], start=(k == 0), stop=False)
                            pe.matmul(o, xh, wlo_out[:, k, cs], start=False, stop=False)
                            ins = pe.matmul(o, xl, whi_out[:, k, cs], start=False, stop=(k == KC - 1))
                    ins.then_inc(s_y, 1)
                if 1 <= i <= nt:
                    norm_transposes(pe, n0 + i - 1, 0, n0 + i - 2 if i > 1 else None)
                if 2 <= i <= nt + 1:
                    t = i - 2
                    pe.wait_ge(s_hd, n0 + t + 1)
                    pe.wait_ge(s_ha, n0 + t + 1)
                    if t == 0:
                        pe.wait_ge(s_rt, 16 * (l + 1))
                    else:
                        pe.wait_ge(s_ex, r0 + t)
                    for k in range(KC):
                        ins = pe.matmul(ps[:, 2, 0:NE], hN[t % 2][:, k, :], router[:, k * NE:(k + 1) * NE],
                                        start=(k == 0), stop=(k == KC - 1))
                    ins.then_inc(s_lg, 1)
                if i >= 3:
                    t = i - 3
                    pe.wait_ge(s_af, r0 + t + 1)
                    if t >= 1:
                        pe.wait_ge(s_afc, r0 + t)
                    pe.transpose(ps[0:NE, 3, 0:P], sm[:, 32 * (t % 2):32 * (t % 2) + NE], ident[:, :]).then_inc(s_aft, 1)
            ne = 48 if l == 0 else NE
            if l == 0:
                pe_late_ada(pe)
            pe.wait_ge(s_tk, l + 1)
            pe.transpose(ps[:, 2, 0:ne], tkv[0:ne, :], ident[0:ne, 0:ne])
            pe.transpose(ps[:, 3, 0:ne], tkf[0:ne, :], ident[0:ne, 0:ne]).then_inc(s_tkt, 1)

        def act_root(act, n):
            b = n % 2
            act.wait_ge(s_ss, n + 1)
            nc.scalar.activation(st[:, 4 * b + 1:4 * b + 2], st[:, 4 * b:4 * b + 1], ACT.Sqrt,
                                 bias=epsc[:, 0:1], scale=1.0 / D).then_inc(s_sq, 1)

        def columns(l, w, k, t):
            c = 0 if t < TL else 1
            i = ((l * 2 + w) * KC + k) * 2 + c
            m = (l * 48 + (3 * w) * KC + k) * 2 + c
            return scg[:, i:i + 1], modc[:, m:m + 1]

        def act_blocks(act, n, l, w, t, bank):
            act.wait_ge(s_tp, n + 1)
            if w == 1 and t >= 2:
                act.wait_ge(s_lg, NT * l + t - 1)
            for k in range(KC // 2, KC):
                sc_, sh_ = columns(l, w, k, t)
                dst = hT[:, k, t * P:(t + 1) * P] if w == 0 else hN[t % 2][:, k, :]
                ins = nc.scalar.activation(dst, ps[:, bank + k // 4, (k % 4) * P:(k % 4 + 1) * P],
                                           ACT.Identity, bias=sh_, scale=sc_)
            ins.then_inc(s_ha, 1)

        def dve_blocks(dve, n, l, w, t, bank):
            dve.wait_ge(s_tp, n + 1)
            if w == 1 and t >= 2:
                dve.wait_ge(s_lg, NT * l + t - 1)
            for k in range(KC // 2):
                sc_, sh_ = columns(l, w, k, t)
                dst = hT[:, k, t * P:(t + 1) * P] if w == 0 else hN[t % 2][:, k, :]
                ins = nc.vector.tensor_scalar(dst,
                                              ps[:, bank + k // 4, (k % 4) * P:(k % 4 + 1) * P], sc_, sh_,
                                              ALU.mult, ALU.add)
            ins.then_inc(s_hd, 1)

        def dve_norm(dve, own, n):
            b = n % 2
            dve.wait_ge(s_sq, n + 1)
            own.do(nc.vector.reciprocal(st[:, 4 * b + 2:4 * b + 3], st[:, 4 * b + 1:4 * b + 2]))
            if before_mixer(n) and n >= 2:
                dve.wait_ge(s_tp, n - 1)
            nc.vector.tensor_scalar(normed(n), XB[b], st[:, 4 * b + 2:4 * b + 3], None, ALU.mult).then_inc(s_xn, 1)

        def dve_ada_rows(dve, a):
            dve.wait_ge(s_used, KC * (a + 1))
            if a >= 1:
                dve.wait_ge(s_adat, a)
            if a == 0:
                dve.wait_ge(s_zero, 2)
            for q in range(4):
                ins = nc.vector.tensor_copy(rowtmp[32 * q:32 * q + 2, :], ps[32 * q:32 * q + 2, 6, :])
            ins.then_inc(s_adar, 1)

        def dve_ada_columns(dve, a):
            l, g = divmod(a, 3)
            if a in LATE:
                dve.wait_ge(s_adlc, a - 3)
                columns_ = late_cols[a - 4]
            else:
                dve.wait_ge(s_adat, a + 1)
                columns_ = ps[:, 7, :]
            m3 = modc[:, :].rearrange("p (m w) -> p m w", w=2)
            m0 = 48 * l + 16 * g
            for w in range(2):
                src = columns_.rearrange("p (j q r) -> p r q j", j=4, q=4)[:, w]
                ins = nc.vector.tensor_tensor(m3[:, m0:m0 + 16, w].rearrange("p (q j) -> p q j", q=4), src,
                                              adab[:, m0:m0 + 16].rearrange("p (q j) -> p q j", q=4), ALU.add)
            ins.then_inc(s_adac, 1)
            dve.wait_ge(s_adac, a + 1)
            if g in (0, 2):
                w_, blk, v0 = (0, 8, VEC["mix_g"]) if g == 0 else (1, 32, VEC["ffn_g"])
                s3 = scg[:, :].rearrange("p (m w) -> p m w", w=2)
                i0 = (l * 2 + w_) * KC
                for w in range(2):
                    ins = nc.vector.scalar_tensor_tensor(out=s3[:, i0:i0 + KC, w],
                                                         in0=m3[:, 48 * l + blk:48 * l + blk + KC, w], scalar=1.0,
                                                         in1=vcol[:, v0 + l * KC:v0 + (l + 1) * KC],
                                                         op0=ALU.add, op1=ALU.mult)
                ins.then_inc(s_scg, 1)

        def act_even_job(act, own, j):
            kind, b, n, who = jobs[j]
            act.wait_ge(s_job, j + 1)
            w = wide(j % 2, n)
            if kind == "lr":
                ins = nc.scalar.copy(lrT[0:32, :], w[0:32, :])
            elif kind == "k":
                ins = nc.scalar.copy(kT[:, b, :], w)
            elif kind == "q":
                ins = nc.scalar.mul(qT[:, b, :], w, DK ** -0.5)
            elif kind == "g":
                ins = nc.scalar.activation(cat[:, 4 + b, :], w, ACT.Silu)
            elif kind == "cg":
                if b >= 2:
                    act.wait_ge(s_cv, b - 1)
                ins = nc.scalar.copy(TMP[b % 2], w)
            ins.then_inc(s_ja, 1)

        def act_decay(act, own, pd):
            t = TMP[2 + pd % 2]
            act.wait_ge(s_dx, pd + 1)
            own.do(nc.scalar.activation(t, t, ACT.Exp, scale=-1.0))
            nc.scalar.activation(t, t, ACT.Ln, bias=1.0).then_inc(s_dl, 1)

        def dve_decay_in(dve, pd):
            j = job_at[("dec", pd, False)]
            dve.wait_ge(s_job, j + 1)
            nc.vector.tensor_scalar(BX[:, pd, :], wide(j % 2, T), vcol[:, VEC["decay_b"] + pd:VEC["decay_b"] + pd + 1],
                                    None, ALU.add).then_inc(s_jd, 1)
            dve.wait_ge(s_jd, emptied["dve"][j + 1])
            nc.vector.scalar_tensor_tensor(out=TMP[2 + pd % 2], in0=BX[:, pd, :], scalar=-1.0, in1=BX[:, pd, :],
                                           op0=ALU.mult, op1=ALU.max).then_inc(s_dx, 1)

        def dve_decay_out(dve, own, pd):
            t, x = TMP[2 + pd % 2], BX[:, pd, :]
            dve.wait_ge(s_const, N_CONST)
            dve.wait_ge(s_dl, pd + 1)
            own.do(nc.vector.scalar_tensor_tensor(out=t, in0=x, scalar=0.0, in1=t, op0=ALU.min, op1=ALU.subtract))
            if pd < 2:
                ins = nc.vector.tensor_tensor_scan(x, chunk0[:, :], t, 0.0, ALU.mult, ALU.add)
            else:
                ins = nc.vector.tensor_tensor_scan(BX[:, pd, ::-1], chunk0[:, :], t[:, ::-1], 0.0, ALU.mult, ALU.add)
            ins.then_inc(s_dsc, 1)

        def dve_even_job(dve, own, j):
            kind, b, n, who = jobs[j]
            dve.wait_ge(s_job, j + 1)
            w = wide(j % 2, n)
            if kind == "bg":
                dve.wait_ge(s_cv, b + 1)
                nc.vector.tensor_tensor(cat[:, b, :], cat[:, b, :], w, ALU.mult).then_inc(s_jd, 1)
                return
            p = TMP[b % 2]
            dve.wait_ge(s_ja, emptied["act"][job_at[("cg", b, False)] + 1])
            nc.vector.tensor_tensor(p, p, w, ALU.mult).then_inc(s_jd, 1)
            dve.wait_ge(s_jd, emptied["dve"][j + 1])
            w0 = VEC["ev_conv_w"] + b
            tap = [vcol[:, w0 + 4 * i:w0 + 4 * i + 1] for i in range(3)]
            o = cat[:, b, :]
            own.do(nc.vector.tensor_scalar(o, p, tap[1], vcol[:, VEC["ev_conv_b"] + b:VEC["ev_conv_b"] + b + 1],
                                           ALU.mult, ALU.add))
            for src, dst in (((0, GRID - 1), (1, GRID)), ((1, GRID), (0, GRID - 1))):
                tp = tap[0] if dst[0] == 1 else tap[2]
                p3 = p[:, 0:LAT].rearrange("p (r x) -> p r x", x=GRID)[:, :, src[0]:src[1]]
                o3 = o[:, 0:LAT].rearrange("p (r x) -> p r x", x=GRID)[:, :, dst[0]:dst[1]]
                nc.vector.scalar_tensor_tensor(out=o3, in0=p3, scalar=tp, in1=o3, op0=ALU.mult, op1=ALU.add)
                s0, d0 = (0, 1) if dst[0] == 1 else (1, 0)
                pc, oc = p[:, LAT + s0:LAT + s0 + CTX - 1], o[:, LAT + d0:LAT + d0 + CTX - 1]
                ins = nc.vector.scalar_tensor_tensor(out=oc, in0=pc, scalar=tp, in1=oc, op0=ALU.mult, op1=ALU.add)
                own.mark(ins) if dst[0] != 1 else own.do(ins)
            dve.wait_ge(s_dv, own.n)
            dve.sem_inc(s_cv, 1)

        def act_exps(act, p):
            if p == 0:
                act.wait_ge(s_dsc, 4)
                act.wait_ge(s_cv, 4)
            else:
                act.wait_ge(s_qk, 1)
            for r in range(2):
                nc.scalar.activation(TMP[2 * r], BX[:, 2 * r + p, :], ACT.Exp, scale=1.0 / TAU)
                ins = nc.scalar.activation(TMP[2 * r + 1], BX[:, 2 * r + p, :], ACT.Exp, scale=-1.0 / TAU)
            ins.then_inc(s_eb, 1)

        def dve_decayed(dve, own, p):
            dve.wait_ge(s_eb, p + 1)
            if p == 0:
                dve.wait_ge(s_ja, emptied["act"][n_even_jobs])
            for r in range(2):
                e3 = TMP[2 * r].rearrange("p (c i) -> p c i", i=CHUNK)
                i = (CHUNK - 1) * (1 - r)
                nc.vector.tensor_copy(dec[:, (2 * r + p) * NCH:(2 * r + p + 1) * NCH], e3[:, :, i])
                ins = nc.vector.tensor_tensor(BX[:, 2 * r + p, :], kT[:, p, :], TMP[2 * r + 1], ALU.mult)
            own.do(ins)
            own.do(nc.vector.tensor_tensor(kT[:, p, :], qT[:, p, :], TMP[2], ALU.mult))
            nc.vector.tensor_tensor(qT[:, p, :], qT[:, p, :], TMP[0], ALU.mult).then_inc(s_qk, 1)

        def act_gla(act, own):
            act_exps(act, 0)
            act_exps(act, 1)
            for p in range(2):
                for g in range(5):
                    n = 5 * p + g
                    act.wait_ge(s_kt, n + 1)
                    nc.scalar.copy(ktok[:, 2 * g:2 * g + 2, :, :].rearrange("p t r d -> p (t r d)"),
                                   ps[:, n % 2, :]).then_inc(s_kc, 1)
                for s in range(NCH - 1):
                    n = NCH * p + s
                    for r in range(2):
                        act.wait_ge(s_tst, 2 * n + r + 1)
                        c, c1 = order[r][s], order[r][s + 1]
                        i = (2 * r + p) * NCH + c
                        nc.scalar.activation(SIN[:, r, c1, :], TST[:, r, s % 2, :], ACT.Copy,
                                             scale=dec[:, i:i + 1]).then_inc(s_sin, 1)

                def squares(g):
                    n = 5 * p + g
                    act.wait_ge(s_o, n + 1)
                    if n == 0:
                        act.wait_ge(s_qk, 2)
                    if n >= 2:
                        act.wait_ge(s_ms, n - 1)
                    nc.scalar.activation(SQ[n % 2].rearrange("p (h t) -> p h t", h=2), ps[:, 6:8, 0:256],
                                         ACT.Square).then_inc(s_osq, 1)

                def reciprocal_roots(g):
                    n = 5 * p + g
                    act.wait_ge(s_ms, n + 1)
                    if n >= 2:
                        act.wait_ge(s_of, n - 1)
                    own.do(nc.scalar.activation(RS[n % 2], ps[:, n % 2, :], ACT.Ln, bias=epsc[:, 0:1], scale=1.0 / P))
                    nc.scalar.activation(RS[n % 2], RS[n % 2], ACT.Exp, scale=-0.5).then_inc(s_rs, 1)

                for g in range(5):
                    if g >= 1:
                        reciprocal_roots(g - 1)
                    squares(g)
                reciprocal_roots(4)

        def dve_gla(dve, own):
            dve_decayed(dve, own, 0)
            dve_decayed(dve, own, 1)
            dve.wait_ge(s_job, n_even_jobs)
            own.do(nc.vector.memset(R_H[:, 7680:9728], 0.0))
            for p in range(2):
                for s in range(NCH):
                    n = NCH * p + s
                    if s % 4 == 0:
                        dve.wait_ge(s_up, (n // 4) + 1)
                    for r in range(2):
                        u = ps[:, 2 * (s // 4 % 2) + order[r][s] % 2, (s % 4) * P:(s % 4 + 1) * P]
                        if s >= 2:
                            dve.wait_ge(s_sin, 38 * p + 2 * (s - 2) + r + 1)
                        elif p == 1 and s == 0 and r == 0:
                            dve.wait_ge(s_sin, 38)
                        if s == 0:
                            ins = nc.vector.tensor_copy(TST[:, r, 0, :], u)
                        else:
                            i = (2 * r + p) * NCH + order[r][s - 1]
                            dve.wait_ge(s_tst, 2 * (n - 1) + r + 1)
                            ins = nc.vector.scalar_tensor_tensor(out=TST[:, r, s % 2, :], in0=TST[:, r, (s - 1) % 2, :],
                                                                 scalar=dec[:, i:i + 1], in1=u,
                                                                 op0=ALU.mult, op1=ALU.add)
                        ins.then_inc(s_tst, 1)

                def mask_scores(g):
                    n = 5 * p + g
                    dve.wait_ge(s_at, n + 1)
                    if n >= 2:
                        dve.wait_ge(s_o, n - 1)
                    for r in range(2):
                        mask = (maskf, maskb)[r].bitcast(U32).unsqueeze(1).broadcast_to([P, 2, P])
                        for hh in range(2):
                            ins = nc.vector.copy_predicated(
                                attS[:, n % 2, r, 256 * hh:256 * (hh + 1)].rearrange("p (q i) -> p q i", q=2), mask,
                                ps[:, 4 + hh, 256 * r:256 * (r + 1)].rearrange("p (q i) -> p q i", q=2))
                    ins.then_inc(s_am, 1)

                def gated(g):
                    n = 5 * p + g
                    dve.wait_ge(s_osq, n + 1)
                    for hh in range(2):
                        h = 2 * p + hh
                        o = cat[:, 4 + h, g * 256:(g + 1) * 256]
                        ins = nc.vector.scalar_tensor_tensor(out=o, in0=ps[:, 6 + hh, 0:256],
                                                             scalar=vcol[:, VEC["ev_norm_g"] + h:VEC["ev_norm_g"] + h + 1],
                                                             in1=o, op0=ALU.mult, op1=ALU.mult)
                    ins.then_inc(s_ob, 1)

                def scaled(g):
                    n = 5 * p + g
                    dve.wait_ge(s_ob, n + 1)
                    dve.wait_ge(s_rs, n + 1)
                    o = cat[:, 4 + 2 * p:6 + 2 * p, g * 256:(g + 1) * 256]
                    nc.vector.tensor_tensor(o, o, RS[n % 2].rearrange("p (h t) -> p h t", h=2), ALU.mult).then_inc(s_of, 1)

                mask_scores(0)
                for g in range(5):
                    if g < 4:
                        mask_scores(g + 1)
                    if g >= 1:
                        scaled(g - 1)
                    gated(g)
                scaled(4)

        def gate_rows(l):
            return [(0, 2, 0), (1, 2, 1), (2, 5, 0), (3, 5, 1)] if l == 0 else [(0, 2, 0), (2, 5, 0)]

        def dve_gates(dve, l):
            if l == 1:
                dve.wait_ge(s_job, len(jobs))
                dve.wait_ge(s_vm, NT + TL)
            m3 = modc[:, :].rearrange("p (m w) -> p m w", w=2)
            for m, (_, blk, w) in enumerate(gate_rows(l)):
                n = (0 if l == 0 else 4) + m
                if n >= 2:
                    dve.wait_ge(s_bcp, n - 1)
                gate = m3[:, l * 48 + blk * KC:l * 48 + (blk + 1) * KC, w]
                nc.vector.tensor_tensor(diag[n % 2].rearrange("p (k n) -> p k n", k=KC),
                                        ident[:, :].unsqueeze(1).broadcast_to([P, KC, P]),
                                        gate.unsqueeze(2).broadcast_to([P, KC, P]), ALU.mult).then_inc(s_diag, 1)
            for c in range(4):
                dve.wait_ge(s_wh, 4 * l + c + 1)
                nc.vector.tensor_tensor(wlo_out[:, 2 * c:2 * c + 2, :], wout[:, 2 * c:2 * c + 2, :],
                                        whi_out[:, 2 * c:2 * c + 2, :], ALU.subtract).then_inc(s_wl, 1)

        def act_weights_high(act, l, c):
            act.wait_ge(s_wo[c // 3], 16 * (l + 1))
            if c == 0:
                if l == 0:
                    act.wait_ge(s_o, 10)
                else:
                    act.wait_ge(s_job, len(jobs))
                    act.wait_ge(s_vm, NT + TL)
            nc.scalar.copy(whi_out[:, 2 * c:2 * c + 2, :], wout[:, 2 * c:2 * c + 2, :]).then_inc(s_wh, 1)

        def act_tile_high(act, l, i):
            src = (cat, cat1)[l]
            if i == 0:
                if l == 0:
                    act.wait_ge(s_of, 10)
                else:
                    act.wait_ge(s_cat, 1)
                    act.wait_ge(s_sge, TL)
            if i >= 2:
                act.wait_ge(s_y, NT * l + i - 1)
            nc.scalar.copy(cathi[i % 2], src[:, :, i * P:(i + 1) * P]).then_inc(s_ch, 1)

        def dve_tile_low(dve, l, i):
            src = (cat, cat1)[l]
            dve.wait_ge(s_ch, NT * l + i + 1)
            nc.vector.tensor_tensor(catlo[l][:, :, i * P:(i + 1) * P], src[:, :, i * P:(i + 1) * P], cathi[i % 2],
                                    ALU.subtract).then_inc(s_cl, 1)

        def act_gates(act, l):
            act_weights_high(act, l, 0)
            act_weights_high(act, l, 1)
            for m, (row, _, _) in enumerate(gate_rows(l)):
                n = (0 if l == 0 else 4) + m
                act.wait_ge(s_bcp, n + 1)
                nc.scalar.copy(bc[:, row * D:(row + 1) * D],
                               ps[:, 2 * (n % 2):2 * (n % 2) + 2, :].rearrange("p b n -> p (b n)")).then_inc(s_bc, 1)

        def dve_wout(dve, own, l):
            nt, n0, r0 = (NT, norm0["ffn0"], 0) if l == 0 else (TL, norm0["ffn1"], NT)
            dve_gates(dve, l)
            dve.wait_ge(s_bc, 4 if l == 0 else 6)
            ne = 48 if l == 0 else NE
            if l == 0:
                dve.wait_ge(s_o, 10)
            own.do(nc.vector.memset(affT[0:ne, :], -1.0))
            dve_tile_low(dve, l, 0)
            for i in range(nt + 3):
                if i + 1 < nt:
                    dve_tile_low(dve, l, i + 1)
                if i < nt:
                    n = n0 + i
                    dve.wait_ge(s_y, r0 + i + 1)
                    y = ps[:, 4 + 2 * (i % 2):6 + 2 * (i % 2), :].rearrange("p b n -> p (b n)")
                    row = 0 if i < TL else 1
                    own.do(nc.vector.tensor_tensor(y, y, bc[:, row * D:(row + 1) * D], ALU.mult))
                    dve.wait_ge(s_xl[n % 2], 16 * xl_count[n])
                    nc.vector.tensor_tensor(XB[n % 2], XB[n % 2], y, ALU.add).then_inc(s_x1, 1)
                if 1 <= i <= nt:
                    dve_blocks(dve, n0 + i - 1, l, 1, i - 1, 0)
                if 2 <= i <= nt + 1:
                    t, b = i - 2, 16 + 4 * (i % 2)
                    dve.wait_ge(s_lg, r0 + t + 1)
                    own.do(nc.vector.reduce_max(st[:, b:b + 1], ps[:, 2, 0:NE], AXX))
                    nc.vector.tensor_scalar(st[:, b + 1:b + 2], st[:, b:b + 1], -1.0, None, ALU.mult).then_inc(s_mx, 1)
                if i < nt:
                    dve_norm(dve, own, n0 + i)
                if 2 <= i <= nt + 1:
                    t, b, s0 = i - 2, 16 + 4 * (i % 2), 32 * (i % 2)
                    dve.wait_ge(s_ex, r0 + t + 1)
                    own.do(nc.vector.reciprocal(st[:, b + 3:b + 4], st[:, b + 2:b + 3]))
                    nc.vector.tensor_scalar(sm[:, s0:s0 + NE], sm[:, s0:s0 + NE], st[:, b + 3:b + 4], None,
                                            ALU.mult).then_inc(s_af, 1)
                if i >= 3:
                    t = i - 3
                    dve.wait_ge(s_aft, r0 + t + 1)
                    dst = affT[0:NE, t * P:(t + 1) * P] if t < TL else affT[32:48, (t - TL) * P:(t - TL + 1) * P]
                    nc.vector.tensor_copy(dst, ps[0:NE, 3, 0:P]).then_inc(s_afc, 1)
            dve.wait_ge(s_afc, r0 + nt)
            a = affT[0:ne, :]
            for r in range(CAPL // 8):
                v8, i8 = tkv[0:ne, 8 * r:8 * r + 8], tki[0:ne, 8 * r:8 * r + 8]
                own.do(nc.vector.max(v8, a))
                nc.vector.max_index(i8, v8, a)
                own.do(nc.vector.match_replace(a, v8, a, -2.0))
            nc.vector.tensor_copy(tkf[0:ne, :], tki[0:ne, :]).then_inc(s_tk, 1)
            dve.wait_ge(s_tkt, l + 1)
            nc.vector.tensor_copy(icolT[:, 0:NE], ps[:, 3, 0:NE])
            if l == 0:
                nc.vector.tensor_scalar(icolT[0:CAPC, 32:48], ps[0:CAPC, 3, 32:48], float(LAT), None, ALU.add)
            nc.vector.tensor_copy(gcolT[:, 0:ne], ps[:, 2, 0:ne]).then_inc(s_idx, 1)
            if l == 0:
                for a in LATE:
                    dve_ada_columns(dve, a)

        def act_wout(act, own, l):
            nt, n0, r0 = (NT, norm0["ffn0"], 0) if l == 0 else (TL, norm0["ffn1"], NT)
            act_gates(act, l)
            act_weights_high(act, l, 2)
            act_weights_high(act, l, 3)
            act_tile_high(act, l, 0)
            for i in range(nt + 3):
                if i + 1 < nt:
                    act_tile_high(act, l, i + 1)
                if 1 <= i <= nt:
                    act_blocks(act, n0 + i - 1, l, 1, i - 1, 0)
                if i < nt:
                    n = n0 + i
                    act.wait_ge(s_x1, r0 + i + 1)
                    if i >= 1:
                        act.wait_ge(s_nst, 16 * (r0 + i))
                    act_square(act, n)
                    act_root(act, n)
                if 2 <= i <= nt + 1:
                    t, b, s0 = i - 2, 16 + 4 * (i % 2), 32 * (i % 2)
                    act.wait_ge(s_mx, r0 + t + 1)
                    if t >= 2:
                        act.wait_ge(s_aft, r0 + t - 1)
                    nc.scalar.activation(sm[:, s0:s0 + NE], ps[:, 2, 0:NE], ACT.Exp, bias=st[:, b + 1:b + 2],
                                         accum_out=st[:, b + 2:b + 3]).then_inc(s_ex, 1)
            if l == 0:
                act_late_ada(act)

        def sp_wout(sp, l):
            nt, n0, r0 = (NT, norm0["ffn0"], 0) if l == 0 else (TL, norm0["ffn1"], NT)
            w = (I["ev_w_out"] if l == 0 else I["od_w_out"]).rearrange("l (k p) n -> (l p) k n", p=P)
            if l == 0:
                sp.wait_ge(s_job, n_even_jobs)
                sp.wait_ge(s_used, 4 * KC)
                sp.dma_start(wout[:, 0:6, :], w[:, 0:6, :]).then_inc(s_wo[0], 16)
                sp.wait_ge(s_qk, 2)
                sp.dma_start(wout[:, 6:8, :], w[:, 6:8, :]).then_inc(s_wo[1], 16)
                sp.wait_ge(s_of, 10)
            else:
                sp.wait_ge(s_job, len(jobs))
                sp.wait_ge(s_vm, NT + TL)
                sp.dma_start(wout[:, 0:6, :], w[:, 0:6, :]).then_inc(s_wo[0], 16)
                sp.wait_ge(s_lru, 8)
                sp.dma_start(wout[:, 6:8, :], w[:, 6:8, :]).then_inc(s_wo[1], 16)
            sl, sc_ = (x_rows, c_rows) if l == 0 else (xres, xres)
            if l == 1:
                sp.wait_ge(s_sge, TL)
            for i in range(nt + 1):
                if i < nt:
                    n = n0 + i
                    if i >= 2:
                        sp.wait_ge(s_xst[n % 2], 16 * xst_count[n - 2])
                        sp.wait_ge(s_xn, n - 1)
                    elif l == 1:
                        sp.wait_ge(s_xn, n0)
                    sp.dma_start(XB[n % 2], tok_tile(sl, sc_, i)).then_inc(s_xl[n % 2], 16)
                if i >= 1:
                    t, n = i - 1, n0 + i - 1
                    sp.wait_ge(s_x1, r0 + t + 1)
                    sp.dma_start(xres[t * P:(t + 1) * P, :], XB[n % 2]).then_inc(s_xst[n % 2], 16)
                    sp.wait_ge(s_xn, n + 1)
                    sp.dma_start(xnd[t * P:(t + 1) * P, :], XN).then_inc(s_nst, 16)
                if 1 <= i <= 6:
                    load_first_unit(sp, l, i - 1)
                if i == 0:
                    sp.dma_start(router[:, :].rearrange("p (k e) -> p k e", e=NE),
                                 I["moe_router"][l].rearrange("(k p) e -> p k e", p=P)).then_inc(s_rt, 16)

        def act_square(act, n):
            if not before_mixer(n):
                act.wait_ge(s_tp, n)
            squares = R_C[:, 3 * D:4 * D] if before_mixer(n) else XN
            nc.scalar.activation(squares, XB[n % 2], ACT.Square, accum_out=st[:, 4 * (n % 2):4 * (n % 2) + 1]).then_inc(s_ss, 1)

        def first_unit(l, m, e, odd):
            if isinstance(e, int) and e == 0 and m < 2:
                return 12 * NE * l + 4 * m, 4 * m
            if isinstance(e, int) and e == NE - 1 and m == 2:
                return 12 * NE * (l + 1) - 4, 4
            return 12 * NE * l + 12 * e + (-4, 0, 16)[m], (0 if odd else 4, 4 if odd else 0, 4 if odd else 0)[m]

        def loads_before(l, m, e2, odd):
            if isinstance(e2, int) and e2 == 0 and not odd and m < 2:
                return 24 * l
            if isinstance(e2, int) and e2 == NE // 2 - 1 and odd and m == 2:
                return 24 * l + 23
            return 24 * l + 3 * e2 + (((-1, 0, 2), (1, 1, 3))[odd][m])

        def matrix_order(e2, odd, l):
            e = 2 * e2 + odd
            steps = [] if isinstance(e, int) and e == NE else [(0, e, e2, odd), (1, e, e2, odd)]
            if not (isinstance(e, int) and e == 0):
                steps.append((2, e - 1, e2 if odd else e2 - 1, 1 - odd))
            return steps

        def moe_steps(eng, step):
            step(0, 0)
            step(0, 1)
            with eng.Fori(1, NE // 2 - 1) as e2:
                step(e2, 0)
                step(e2, 1)
            step(NE // 2 - 1, 0)
            step(NE // 2 - 1, 1)

        def units_done(l, m, e):
            return first_unit(l, m, e, 0)[0] + 4

        def load_first_unit(sp, l, u):
            w = (I["moe_w_gate"], I["moe_w_up"])[u // 4].rearrange("l e (j k p) n -> (l e j) p k n", j=4, p=P)
            sp.dma_start(raw[u].rearrange("p (k n) -> p k n", k=2), w[4 * NE * l + u % 4]).then_inc(s_el[u], 16)

        def sp_moe(sp, l):
            n0 = NE * l
            w = [I[x].rearrange("l e (j k p) n -> (l e j) p k n", j=4, p=P)
                 for x in ("moe_w_gate", "moe_w_up", "moe_w_down")]

            def load(m, e, e2, odd):
                u, slot = first_unit(l, m, e, odd)
                for j in range(4):
                    if isinstance(u, int) and u + j < 12 * NE * l + 6:
                        continue
                    if isinstance(u, int) and u + j == 12 * NE * l + 6:
                        sp.wait_ge(s_lg, NT if l == 0 else NT + TL)
                    if not (isinstance(u, int) and u < 12 * NE * l + 8):
                        if l == 0:
                            sp.wait_ge(s_mm, u + j - 7)
                        else:
                            sp.wait_ge(s_lo, u + j - 7)
                    src = w[m][(n0 + e) * 4 + j] if isinstance(e, int) else \
                        w[m][bass.ds((n0 + e) * 4 + j, 1)].rearrange("a p k n -> p (a k) n")
                    sp.dma_start(raw[slot + j].rearrange("p (k n) -> p k n", k=2), src).then_inc(s_el[slot + j], 16)

            if l == 1:
                sp.dma_start(bc[:, 3 * D:4 * D], I["norm_final_g"].partition_broadcast(P)).then_inc(s_gf, 16)

            def step(e2, odd):
                for m in matrix_order(e2, odd, l):
                    load(*m)

            moe_steps(sp, step)
            load(2, NE - 1, NE // 2 - 1, 1)

        def pe_moe(pe, l):
            n0 = NE * l
            C = CAPC if l == 0 else 0

            def unit(m, e, e2, odd, j, full, lo, hi, bank, cbank, context_free=lambda: None):
                u, slot = first_unit(l, m, e, odd)
                pe.wait_ge(s_hi, u + j + 1)
                pe.wait_ge(s_lo, u + j + 1)
                wh, wl = (x[j].rearrange("p (k n) -> p k n", k=2) for x in (whi, wlo))
                for kk in range(2):
                    k = 2 * j + kk
                    for c in range(2):
                        o, cs = ps[:, bank + c, :], slice(c * BANK, (c + 1) * BANK)
                        pe.matmul(o, hi[:, k, :], wh[:, kk, cs], start=(k == 0), stop=False)
                        pe.matmul(o, hi[:, k, :], wl[:, kk, cs], start=False, stop=False)
                        ins = pe.matmul(o, lo[:, k, 0:P], wh[:, kk, cs], start=False, stop=(k == KC - 1))
                if C:
                    w = raw[slot + j].rearrange("p (k n) -> p k n", k=2)
                    context_free()
                    for kk in range(2):
                        for c in range(2):
                            q = 2 * kk + c
                            ins = pe.matmul(ps[32 * q:32 * q + C, cbank, :], full[:, 2 * j + kk, P:P + C],
                                            w[:, kk, c * BANK:(c + 1) * BANK], start=(j == 0), stop=(j == 3))
                ins.then_inc(s_mm, 1)

            def token_columns(n):
                pe.wait_ge(s_gd, (n + 1) * 16)
                for k in range(KC):
                    ins = pe.transpose(ps[:, 4 + k // 4, (k % 4) * P:(k % 4 + 1) * P], xg[:, k * P:(k + 1) * P],
                                       ident[:, :])
                if C:
                    pe.wait_ge(s_const, 1)
                    pe.wait_ge(s_gdc, (n + 1) * 16)
                    for k in range(KC):
                        ins = pe.transpose(ps[:, 7, k * C:(k + 1) * C], xgc[0:C, k * P:(k + 1) * P], ident[0:C, 0:C])
                ins.then_inc(s_tx, 1)

            def down(e, e2, odd, gate_read):
                pe.wait_ge(s_thd, n0 + e + 1)
                for j in range(4):
                    unit(2, e, e2, odd, j, hidT, hidlo, hidh, 4, 6, gate_read if j == 0 else lambda: None)

            def step(e2, odd):
                e = 2 * e2 + odd
                n = n0 + e
                known = isinstance(e2, int)
                first, second, last = known and e == 0, known and e == 1, known and e == NE - 1
                x, xl, xh = xT[odd], xlo[odd], xhi[odd]
                pe.wait_ge(s_txl, n + 1)
                if not first:
                    pe.wait_ge(s_sil, n)

                def down_read():
                    if not first and not second:
                        pe.wait_ge(s_c6, n - 1)
                        pe.wait_ge(s_c7, n - 1)

                def gate_read():
                    pe.wait_ge(s_c2, n + 1)

                for j in range(4):
                    unit(0, e, e2, odd, j, x, xl, xh, 0, 6, down_read if j == 0 else lambda: None)
                    if j == 2 and not last:
                        if not first:
                            pe.wait_ge(s_thd, n)
                            if not second:
                                pe.wait_ge(s_eo, n - 1)
                        token_columns(n + 1)
                if not last:
                    pe.wait_ge(s_txd, n + 2)
                if not first:
                    pe.wait_ge(s_thd, n)
                    if not second:
                        pe.wait_ge(s_eo, n - 1)
                for j in range(4):
                    unit(1, e, e2, odd, j, x, xl, xh, 2, 7)
                if not first:
                    if not last:
                        pe.wait_ge(s_txa, n + 2)
                    down(*matrix_order(e2, odd, l)[2][1:], gate_read)
                pe.wait_ge(s_hid, n + 1)
                for k in range(KC):
                    ins = pe.transpose(ps[:, 2 + k // 4, (k % 4) * P:(k % 4 + 1) * P], hid[:, k * P:(k + 1) * P],
                                       ident[:, :])
                if C:
                    pe.wait_ge(s_const, 1)
                    pe.wait_ge(s_hidc, n + 1)
                    for k in range(4):
                        ins = pe.transpose(ps[:, 7, k * 2 * C:(k + 1) * 2 * C], hidc[0:2 * C, k * P:(k + 1) * P],
                                           ident[0:2 * C, 0:2 * C])
                ins.then_inc(s_th, 1)

            if l == 0:
                pe.wait_ge(s_adlc, 2)
            token_columns(n0)
            moe_steps(pe, step)
            if C:
                pe.wait_ge(s_c6, n0 + NE - 1)
                pe.wait_ge(s_c7, n0 + NE - 1)
            pe.wait_ge(s_eo, n0 + NE - 1)
            down(NE - 1, NE // 2 - 1, 1, lambda: None)

        def act_moe(act, l):
            n0 = NE * l
            C = CAPC if l == 0 else 0

            def high(m, e, e2, odd, j):
                u, slot = first_unit(l, m, e, odd)
                act.wait_ge(s_el[slot + j], 16 * (loads_before(l, m, e2, odd) + 1))
                if not (isinstance(u, int) and u + j < 4):
                    act.wait_ge(s_mm, u + j - 3)
                nc.scalar.copy(whi[j], raw[slot + j]).then_inc(s_hi, 1)

            def token_columns(n, par):
                x = xT[par]
                act.wait_ge(s_tx, n + 1)
                for k in range(KC // 2, KC):
                    sc_, sh_ = columns(l, 1, k, 0)
                    ins = nc.scalar.activation(x[:, k, 0:P], ps[:, 5, (k % 4) * P:(k % 4 + 1) * P], ACT.Identity,
                                               bias=sh_, scale=sc_)
                ins.then_inc(s_txa, 1)

            def token_high(n, par):
                act.wait_ge(s_txa, n + 1)
                act.wait_ge(s_txd, n + 1)
                nc.scalar.copy(xhi[par], xT[par][:, :, 0:P]).then_inc(s_txh, 1)

            def context_down(e):
                n = n0 + e
                act.wait_ge(s_mm, units_done(l, 2, e))
                if not (isinstance(n, int) and n == 0):
                    act.wait_ge(s_eoc, n)
                for c in range(2):
                    ins = nc.scalar.copy(tmo[0:C, c * BANK:(c + 1) * BANK], ps[64 + 32 * c:64 + 32 * c + C, 6, :])
                ins.then_inc(s_c6, 1)

            def step(e2, odd):
                e = 2 * e2 + odd
                n = n0 + e
                known = isinstance(e2, int)
                first, last = known and e == 0, known and e == NE - 1
                order_ = matrix_order(e2, odd, l)
                up, down = order_[1], order_[2] if not first else None
                nxt = matrix_order(*((e2, 1) if odd == 0 else (e2 + 1, 0)), l)
                following = nxt[0]
                high(*order_[0], 3)
                high(*up, 0)
                high(*up, 1)
                if not last:
                    token_columns(n + 1, 1 - odd)
                high(*up, 2)
                act.wait_ge(s_mm, units_done(l, 0, e))
                if not first:
                    act.wait_ge(s_hid, n)
                nc.scalar.activation(sil, ps[:, 0:2, :].rearrange("p b n -> p (b n)"), ACT.Silu).then_inc(s_sil, 1)
                if C:
                    if not first:
                        act.wait_ge(s_hidc, n)
                    nc.scalar.copy(tmc[0:2 * C, :], ps[64:128, 6, :]).then_inc(s_c1, 1)
                high(*up, 3)
                if not last:
                    token_high(n + 1, 1 - odd)
                if C:
                    act.wait_ge(s_c2, n + 1)
                    nc.scalar.activation(silx[0:2 * C, :], silx[0:2 * C, :], ACT.Silu).then_inc(s_c3, 1)
                if not first:
                    for j in range(3):
                        high(*down, j)
                if C:
                    act.wait_ge(s_mm, units_done(l, 1, e))
                    nc.scalar.copy(tmc[0:2 * C, :], ps[64:128, 7, :]).then_inc(s_c4, 1)
                if not first:
                    high(*down, 3)
                for j in range(3):
                    high(*following, j)
                if C and not first:
                    context_down(e - 1)
                act.wait_ge(s_th, n + 1)
                nc.scalar.copy(hidh, ps[:, 2:4, :].rearrange("p b (k t) -> p (b k) t", k=4)).then_inc(s_tha, 1)

            if l == 0:
                act.wait_ge(s_xst[0], 16 * (NT // 2))
            else:
                act.wait_ge(s_xst[0], 16 * (NT // 2 + TL // 2))
            if l == 0:
                act.wait_ge(s_used, 6 * KC)
            act.wait_ge(s_lg, NT if l == 0 else NT + TL)
            for j in range(3):
                high(0, 0, 0, 0, j)
            token_columns(n0, 0)
            token_high(n0, 0)
            moe_steps(act, step)
            high(2, NE - 1, NE // 2 - 1, 1, 3)
            if C:
                context_down(NE - 1)

        def dve_moe(dve, l):
            n0 = NE * l
            C = CAPC if l == 0 else 0

            def low(m, e, e2, odd, j):
                u, slot = first_unit(l, m, e, odd)
                dve.wait_ge(s_hi, u + j + 1)
                nc.vector.tensor_tensor(wlo[j], raw[slot + j], whi[j], ALU.subtract).then_inc(s_lo, 1)

            def token_columns(n, par):
                x = xT[par]
                dve.wait_ge(s_tx, n + 1)
                for k in range(KC // 2):
                    sc_, sh_ = columns(l, 1, k, 0)
                    ins = nc.vector.tensor_scalar(x[:, k, 0:P], ps[:, 4, (k % 4) * P:(k % 4 + 1) * P], sc_, sh_,
                                                  ALU.mult, ALU.add)
                for k in range(KC if C else 0):
                    sc_, sh_ = columns(l, 1, k, TL)
                    ins = nc.vector.tensor_scalar(x[:, k, P:P + C], ps[:, 7, k * C:(k + 1) * C], sc_, sh_,
                                                  ALU.mult, ALU.add)
                ins.then_inc(s_txd, 1)

            def token_low(n, par):
                dve.wait_ge(s_txh, n + 1)
                x = xT[par][:, :, 0:P]
                nc.vector.tensor_tensor(xlo[par][:, :, 0:P], x, xhi[par], ALU.subtract).then_inc(s_txl, 1)

            def result(e):
                n = n0 + e
                first = isinstance(e, int) and e == 0
                dve.wait_ge(s_mm, units_done(l, 2, e))
                if C:
                    dve.wait_ge(s_c6, n + 1)
                    for c in range(2):
                        o = tmo[0:C, c * BANK:(c + 1) * BANK]
                        ins = nc.vector.tensor_tensor(o, o, ps[32 * c:32 * c + C, 6, :], ALU.add)
                    ins.then_inc(s_c7, 1)
                if not first:
                    dve.wait_ge(s_sc, n * 16)
                nc.vector.scalar_tensor_tensor(out=eout, in0=ps[:, 4:6, :].rearrange("p b n -> p (b n)"),
                                               scalar=gcolT[:, bass.ds(e, 1)], in1=bc[:, 2 * D:3 * D],
                                               op0=ALU.mult, op1=ALU.mult).then_inc(s_eo, 1)
                if C:
                    dve.wait_ge(s_c7, n + 1)
                    if not first:
                        dve.wait_ge(s_scc, n * 16)
                    nc.vector.scalar_tensor_tensor(out=outc[0:C, :], in0=tmo[0:C, :],
                                                   scalar=gcolT[0:C, bass.ds(e + 32, 1)], in1=bc[0:C, 3 * D:4 * D],
                                                   op0=ALU.mult, op1=ALU.mult).then_inc(s_eoc, 1)

            def step(e2, odd):
                e = 2 * e2 + odd
                n = n0 + e
                known = isinstance(e2, int)
                first, last = known and e == 0, known and e == NE - 1
                order_ = matrix_order(e2, odd, l)
                up, down = order_[1], order_[2] if not first else None
                following = matrix_order(*((e2, 1) if odd == 0 else (e2 + 1, 0)), l)[0]
                low(*order_[0], 3)
                low(*up, 0)
                low(*up, 1)
                if not last:
                    token_columns(n + 1, 1 - odd)
                low(*up, 2)
                low(*up, 3)
                if C:
                    dve.wait_ge(s_c1, n + 1)
                    nc.vector.tensor_tensor(silx[0:2 * C, :], tmc[0:2 * C, :], ps[0:2 * C, 6, :], ALU.add).then_inc(s_c2, 1)
                if not last:
                    token_low(n + 1, 1 - odd)
                if not first:
                    for j in range(3):
                        low(*down, j)
                dve.wait_ge(s_mm, units_done(l, 1, e))
                dve.wait_ge(s_sil, n + 1)
                if not first:
                    dve.wait_ge(s_th, n)
                nc.vector.tensor_tensor(hid, sil, ps[:, 2:4, :].rearrange("p b n -> p (b n)"), ALU.mult).then_inc(s_hid, 1)
                if C:
                    dve.wait_ge(s_c4, n + 1)
                    nc.vector.tensor_tensor(tmc[0:2 * C, :], tmc[0:2 * C, :], ps[0:2 * C, 7, :], ALU.add).then_inc(s_c5, 1)
                    dve.wait_ge(s_c5, n + 1)
                    dve.wait_ge(s_c3, n + 1)
                    nc.vector.tensor_tensor(hidc[0:2 * C, :], tmc[0:2 * C, :], silx[0:2 * C, :], ALU.mult).then_inc(s_hidc, 1)
                if not first:
                    low(*down, 3)
                for j in range(3):
                    low(*following, j)
                if not first:
                    result(e - 1)
                dve.wait_ge(s_tha, n + 1)
                ins = nc.vector.tensor_tensor(hidlo[:, :, 0:P],
                                              ps[:, 2:4, :].rearrange("p b (k t) -> p (b k) t", k=4), hidh, ALU.subtract)
                if C:
                    src = ps[:, 7, 0:8 * C].rearrange("p (k h t) -> p h k t", k=4, h=2)
                    for h in range(2):
                        ins = nc.vector.tensor_copy(hidT[:, 4 * h:4 * h + 4, P:P + C], src[:, h])
                ins.then_inc(s_thd, 1)

            if l == 0:
                dve.wait_ge(s_xst[1], 16 * (NT // 2))
                dve.wait_ge(s_nst, 16 * NT)
            else:
                dve.wait_ge(s_xst[1], 16 * (NT // 2 + TL // 2))
                dve.wait_ge(s_nst, 16 * (NT + TL))
            low(0, 0, 0, 0, 0)
            low(0, 0, 0, 0, 1)
            token_columns(n0, 0)
            token_low(n0, 0)
            low(0, 0, 0, 0, 2)
            moe_steps(dve, step)
            low(2, NE - 1, NE // 2 - 1, 1, 3)
            result(NE - 1)

        def pool_moe(pool, l):
            n0 = NE * l
            C = CAPC if l == 0 else 0

            def gather(count, first):
                n, e = count - 1, count - 1 - n0
                if not first:
                    pool.wait_ge(s_gd, n * 16)
                    pool.wait_ge(s_tx, n)
                pool.tensor_copy(gidx[:, 0:1], icolT[:, bass.ds(e, 1)]).then_inc(s_gi, 1)
                if C:
                    if not first:
                        pool.wait_ge(s_gdc, n * 16)
                    pool.tensor_copy(gidx[0:C, 1:2], icolT[0:C, bass.ds(e + 32, 1)]).then_inc(s_gic, 1)
                pool.wait_ge(s_idx, l + 1)
                pool.wait_ge(s_gi, count)
                pool.indirect_dma_start(out=xg, out_offset=None, in_=xnd,
                                        in_offset=bass.IndirectOffsetOnAxis(ap=gidx[:, 0:1], axis=0)).then_inc(s_gd, 16)
                if C:
                    pool.wait_ge(s_idx, l + 1)
                    pool.wait_ge(s_gic, count)
                    pool.indirect_dma_start(out=xgc[0:C, :], out_offset=None, in_=xnd,
                                            in_offset=bass.IndirectOffsetOnAxis(ap=gidx[0:C, 1:2], axis=0)).then_inc(s_gdc, 16)

            def scatter(count, first):
                n, e = count - 1, count - 1 - n0
                pool.wait_ge(s_eo, count)
                if not first:
                    pool.wait_ge(s_sc, n * 16)
                    if C:
                        pool.wait_ge(s_scc, n * 16)
                pool.tensor_copy(gidx[:, 2:3], icolT[:, bass.ds(e, 1)]).then_inc(s_si, 1)
                if C:
                    pool.tensor_copy(gidx[0:C, 3:4], icolT[0:C, bass.ds(e + 32, 1)]).then_inc(s_sic, 1)
                pool.wait_ge(s_idx, l + 1)
                pool.wait_ge(s_si, count)
                pool.indirect_dma_start(out=xres, out_offset=bass.IndirectOffsetOnAxis(ap=gidx[:, 2:3], axis=0),
                                        in_=eout, in_offset=None, compute_op=ALU.add).then_inc(s_sc, 16)
                if C:
                    pool.wait_ge(s_idx, l + 1)
                    pool.wait_ge(s_sic, count)
                    pool.wait_ge(s_eoc, count)
                    pool.indirect_dma_start(out=xres, out_offset=bass.IndirectOffsetOnAxis(ap=gidx[0:C, 3:4], axis=0),
                                            in_=outc[0:C, :], in_offset=None, compute_op=ALU.add).then_inc(s_scc, 16)

            pool.wait_ge(s_idx, l + 1)
            pool.wait_ge(s_nst, 16 * (NT if l == 0 else NT + TL))
            for b in range(2):
                pool.wait_ge(s_xst[b], 16 * (NT // 2 if l == 0 else NT // 2 + TL // 2))
            gather(n0 + 1, True)
            gather(n0 + 2, False)
            gather(n0 + 3, False)
            gather(n0 + 4, False)
            scatter(n0 + 1, True)
            with pool.Fori(n0 + 5, n0 + NE + 1) as count:
                gather(count, False)
                scatter(count - 3, False)
            scatter(n0 + NE - 2, False)
            scatter(n0 + NE - 1, False)
            scatter(n0 + NE, False)

        def sp_final(sp):
            sp.wait_ge(s_sc, 16 * 2 * NE)
            sp.wait_ge(s_eo, 2 * NE)
            for t in range(TL):
                sp.dma_start(FB[t], xres[t * P:(t + 1) * P, :]).then_inc(s_xf[t], 16)
            for t in range(TL):
                sp.wait_ge(s_fin, t + 1)
                sp.dma_start(out.rearrange("b t d -> (b t) d")[t * P:(t + 1) * P, :], FB[t]).then_inc(s_out, 16)
            sp.wait_ge(s_out, 16 * TL)
            for b in range(2):
                sp.wait_ge(s_xst[b], 16 * max(xst_count[n] for n in xst_count if n % 2 == b))

        def act_final(act):
            n0 = norm0["final"]
            act.wait_ge(s_sc, 16 * 2 * NE)
            for t in range(TL):
                q = 32 + 4 * t
                act.wait_ge(s_xf[t], 16)
                nc.scalar.activation(XN, FB[t], ACT.Square, accum_out=st[:, q:q + 1]).then_inc(s_ss, 1)
                act.wait_ge(s_ss, n0 + t + 1)
                nc.scalar.activation(st[:, q + 1:q + 2], st[:, q:q + 1], ACT.Sqrt, bias=epsc[:, 0:1],
                                     scale=1.0 / D).then_inc(s_sq, 1)

        def dve_final(dve, own):
            dve.wait_ge(s_gf, 16)
            for t in range(TL):
                q = 32 + 4 * t
                dve.wait_ge(s_sq, norm0["final"] + t + 1)
                own.do(nc.vector.reciprocal(st[:, q + 2:q + 3], st[:, q + 1:q + 2]))
                nc.vector.scalar_tensor_tensor(out=FB[t], in0=FB[t], scalar=st[:, q + 2:q + 3], in1=bc[:, 3 * D:4 * D],
                                               op0=ALU.mult, op1=ALU.mult).then_inc(s_fin, 1)

        def pe_odd(pe):
            n0 = norm0["mix1"]
            for t in range(NT):
                norm_transposes(pe, n0 + t, 2 * (t % 2), n0 + t - 2 if t >= 2 else None)
            pe.wait_ge(s_gw, 64)
            for g in range(4):
                ins = pe.transpose(ps[:, 7, g * P:(g + 1) * P], sgw[:, g, :], ident[:, :])
            ins.then_inc(s_sgt, 1)
            pe.wait_ge(s_hd, n0 + NT)
            pe.wait_ge(s_ha, n0 + NT)
            j = n_even_jobs
            for kind, b in odd_order:
                if kind in ("ga", "gx"):
                    c, d = b // 2, b % 2
                    banks_free(pe, j)
                    pe.wait_ge(s_xc, c + 1)
                    m = (8 if kind == "gx" else 0) + 4 * d + c
                    for c0, cn in SPLIT:
                        ins = pe.matmul(wide(j % 2, T)[:, c0:c0 + cn], gatew[:, m, :], XC[:, c, c0:c0 + cn],
                                        start=True, stop=True)
                    ins.then_inc(s_job, 1)
                    j += 1
                elif kind == "v":
                    if b == 0:
                        pe.wait_ge(s_sgc, 1)
                        unit_in(pe, index[("w0",)])
                        unit_in(pe, index[("w1",)])
                    if b >= 2:
                        pe.wait_ge(s_vg, b - 1)
                    v_tile(pe, b, index[("w0",)])
                else:
                    job(pe, j, index[(f"{kind}{b // 2}",)], b % 2)
                    j += 1
            pe.wait_ge(s_vn, TL)
            for t in range(TL):
                if t >= 2:
                    pe.wait_ge(s_sge, t - 1)
                for g in range(4):
                    ins = pe.matmul(ps[:, 6 + t % 2, g * P:(g + 1) * P], vln[:, t, g * P:(g + 1) * P], sgwT[:, g, :],
                                    start=True, stop=True)
                ins.then_inc(s_sg, 1)

        groups = {0: (0, 3), 1: (3, 6), 2: (6, 8)}

        def act_odd(act, own):
            n0 = norm0["mix1"]
            for t in range(NT + 1):
                if t < NT:
                    n = n0 + t
                    act.wait_ge(s_xl[n % 2], 16 * xl_count[n])
                    act_square(act, n)
                    act_root(act, n)
                if t >= 1:
                    act_blocks(act, n0 + t - 1, 1, 0, t - 1, 2 * ((t - 1) % 2))
            act.wait_ge(s_sgt, 1)
            nc.scalar.copy(sgwT.rearrange("p g n -> p (g n)"), ps[:, 7, :]).then_inc(s_sgc, 1)
            j = n_even_jobs
            for kind, b in odd_order:
                if kind == "v":
                    act.wait_ge(s_vm, NT + b + 1)
                    nc.scalar.activation(vln[:, b, :], ps[:, 6 + b % 2, :], ACT.Gelu_apprx_tanh).then_inc(s_vg, 1)
                    for i, (a, z) in groups.items():
                        if b == z - 1:
                            act.wait_ge(s_vs, i + 1)
                            nc.scalar.activation(vsd[:, a:z], vmv[:, :].rearrange("p (t m) -> p t m", m=2)[:, a:z, 1],
                                                 ACT.Sqrt, bias=epsc[:, 0:1]).then_inc(s_vq, 1)
                    continue
                act.wait_ge(s_job, j + 1)
                w = wide(j % 2, jobs[j][2])
                if kind == "xb":
                    nc.scalar.copy(TMP[b], w).then_inc(s_ja, 1)
                elif kind in ("gb", "u"):
                    nc.scalar.activation(cat1[:, b + (4 if kind == "u" else 0), :], w, ACT.Gelu_apprx_tanh).then_inc(s_ja, 1)
                else:
                    c, d = b // 2, b % 2
                    x = 1 if kind == "gx" else 0
                    v0 = VEC["gate_x_b" if x else "gate_a_b"] + 4 * d + c
                    if b >= 1:
                        act.wait_ge(s_lru, b)
                    else:
                        act.wait_ge(s_xc, 4)
                    nc.scalar.activation(TMP[x], w, ACT.Sigmoid, bias=vcol[:, v0:v0 + 1]).then_inc(s_ja, 1)
                    if x:
                        m = 4 * d + c
                        act.wait_ge(s_ja, emptied["act"][j + 1])
                        act.wait_ge(s_lc, 1)
                        nc.scalar.activation(TMP[2], TMP[0], ACT.Tanh, scale=lruc[:, m:m + 1])
                        nc.scalar.activation(TMP[0], TMP[0], ACT.Exp, scale=lruc[:, 16 + m:17 + m]).then_inc(s_le, 1)
                        act.wait_ge(s_lv, b + 1)
                        nc.scalar.activation(TMP[2], TMP[2], ACT.Sqrt).then_inc(s_lq, 1)
                j += 1

        def dve_odd(dve, own):
            n0 = norm0["mix1"]
            for t in range(NT + 1):
                if t < NT:
                    dve_norm(dve, own, n0 + t)
                if t >= 1:
                    dve_blocks(dve, n0 + t - 1, 1, 0, t - 1, 2 * ((t - 1) % 2))
            j = n_even_jobs
            for kind, b in odd_order:
                if kind == "v":
                    for i, (a, z) in groups.items():
                        if b == z - 1:
                            for t in range(a, z):
                                dve.wait_ge(s_vg, t + 1)
                                ins = nc.vector.bn_stats(vst[:, 6 * t:6 * t + 6], vln[:, t, :])
                            own.do(ins)
                            for t in range(a, z):
                                ins = nc.vector.bn_aggr(vmv[:, 2 * t:2 * t + 2], vst[:, 6 * t:6 * t + 6])
                            ins.then_inc(s_vs, 1)
                            dve.wait_ge(s_vq, i + 1)
                            own.do(nc.vector.reciprocal(vsd[:, 8 + a:8 + z], vsd[:, a:z]))
                            for t in range(a, z):
                                nc.vector.tensor_scalar(vln[:, t, :], vln[:, t, :], vmv[:, 2 * t:2 * t + 1],
                                                        vsd[:, 8 + t:9 + t], ALU.subtract, ALU.mult).then_inc(s_vn, 1)
                    continue
                if kind == "xb":
                    dve.wait_ge(s_ja, emptied["act"][j + 1])
                    w0 = VEC["od_conv_w"] + b
                    tap = [vcol[:, w0 + 4 * i:w0 + 4 * i + 1] for i in range(4)]
                    own.do(nc.vector.tensor_scalar(XC[:, b, :], TMP[b], tap[2],
                                                   vcol[:, VEC["od_conv_b"] + b:VEC["od_conv_b"] + b + 1],
                                                   ALU.mult, ALU.add))
                    for i, off in ((0, -2), (1, -1), (3, 1)):
                        for s0, sn in ((0, LAT), (LAT, CTX)):
                            d0, x0 = (s0 - off, s0) if off < 0 else (s0, s0 + off)
                            ln = sn - abs(off)
                            ins = nc.vector.scalar_tensor_tensor(out=XC[:, b, d0:d0 + ln], in0=TMP[b][:, x0:x0 + ln],
                                                                 scalar=tap[i], in1=XC[:, b, d0:d0 + ln],
                                                                 op0=ALU.mult, op1=ALU.add)
                        if i < 3:
                            own.do(ins)
                        else:
                            ins.then_inc(s_xc, 1)
                elif kind == "gx":
                    c, d = b // 2, b % 2
                    dve.wait_ge(s_ja, emptied["act"][j + 1])
                    nc.vector.tensor_tensor(TMP[1], TMP[1], XC[:, c, :], ALU.mult)
                    dve.wait_ge(s_le, b + 1)
                    own.do(nc.vector.tensor_tensor(TMP[3], TMP[0], TMP[0], ALU.mult))
                    own.do(nc.vector.scalar_tensor_tensor(out=TMP[2], in0=TMP[3], scalar=1.0, in1=TMP[2],
                                                          op0=ALU.add, op1=ALU.mult))
                    nc.vector.tensor_scalar(TMP[2], TMP[2], 2e-35, None, ALU.max).then_inc(s_lv, 1)
                    dve.wait_ge(s_lq, b + 1)
                    own.do(nc.vector.tensor_tensor(TMP[1], TMP[1], TMP[2], ALU.mult))
                    h = TMP[3]
                    if d == 0:
                        own.do(nc.vector.tensor_tensor_scan(h[:, LAT:T], TMP[0][:, LAT:T], TMP[1][:, LAT:T], 0.0,
                                                            ALU.mult, ALU.add))
                        nc.vector.tensor_tensor_scan(HL[:, c, :], TMP[0][:, 0:LAT], TMP[1][:, 0:LAT], h[:, T - 1:T],
                                                     ALU.mult, ALU.add).then_inc(s_lru, 1)
                    else:
                        rev = slice(None, None, -1)
                        own.do(nc.vector.tensor_tensor_scan(h[:, LAT:T][:, rev], TMP[0][:, LAT:T][:, rev],
                                                            TMP[1][:, LAT:T][:, rev], 0.0, ALU.mult, ALU.add))
                        own.do(nc.vector.tensor_tensor_scan(h[:, 0:LAT][:, rev], TMP[0][:, 0:LAT][:, rev],
                                                            TMP[1][:, 0:LAT][:, rev], h[:, LAT:LAT + 1],
                                                            ALU.mult, ALU.add))
                        nc.vector.tensor_tensor(HL[:, c, :], HL[:, c, :], h[:, 0:LAT], ALU.add).then_inc(s_lru, 1)
                j += 1
            dve.wait_ge(s_lru, 8)
            dve.wait_ge(s_ja, emptied["act"][len(jobs)])
            for c in range(4):
                ins = nc.vector.tensor_tensor(cat1[:, c, :], cat1[:, c, :], HL[:, c, :], ALU.mult)
            ins.then_inc(s_cat, 1)
            for t in range(TL):
                dve.wait_ge(s_sg, t + 1)
                for g in range(4):
                    o = ps[:, 6 + t % 2, g * P:(g + 1) * P]
                    v0 = VEC["sg_norm_g"] + g
                    ins = nc.vector.scalar_tensor_tensor(out=o, in0=o, scalar=vcol[:, v0:v0 + 1], in1=sgb[:, g, :],
                                                         op0=ALU.mult, op1=ALU.add)
                own.do(ins)
                o = cat1[:, 4:8, t * P:(t + 1) * P]
                nc.vector.tensor_tensor(o, o, ps[:, 6 + t % 2, :].rearrange("p (g t) -> p g t", g=4),
                                        ALU.mult).then_inc(s_sge, 1)

        @block.gpsimd
        def _(pool):
            own = Chain(pool, s_po)
            own.do(pool.memset(ident[:, :], 0.0))
            pool.affine_select(out=ident[:, :], in_=ident[:, :], compare_op=ALU.not_equal, fill=1.0, base=0,
                               pattern=[[-1, P]], channel_multiplier=1).then_inc(s_const, 1)
            pool.memset(decup[0:32, :], 0.0).then_inc(s_zero, 1)
            pool.memset(rowtmp, 0.0).then_inc(s_zero, 1)
            own.do(pool.memset(maskf[:, :], 1.0))
            own.do(pool.memset(maskb[:, :], 1.0))
            own.do(pool.memset(chunk0[:, :], 1.0))
            pool.memset(epsc[:, :], EPS)
            pool.memset(ones[:, :], 1.0).then_inc(s_const, 1)
            own.do(pool.affine_select(out=maskf, in_=maskf, compare_op=ALU.is_ge, fill=0.0, base=0,
                                      pattern=[[1, P]], channel_multiplier=-1))
            pool.affine_select(out=maskf[:, CHUNK:P], in_=maskf[:, CHUNK:P], compare_op=ALU.is_ge, fill=0.0,
                               base=-CHUNK, pattern=[[0, CHUNK]], channel_multiplier=1).then_inc(s_const, 1)
            own.do(pool.affine_select(out=maskb, in_=maskb, compare_op=ALU.is_ge, fill=0.0, base=0,
                                      pattern=[[-1, P]], channel_multiplier=1))
            pool.affine_select(out=maskb[:, 0:CHUNK], in_=maskb[:, 0:CHUNK], compare_op=ALU.is_ge, fill=0.0,
                               base=CHUNK - 1, pattern=[[0, CHUNK]], channel_multiplier=-1).then_inc(s_const, 1)
            pool.memset(chunk0[:, :].rearrange("p (c i) -> p c i", i=CHUNK)[:, :, 0:1], 0.0).then_inc(s_const, 1)
            pool_moe(pool, 0)
            pool_moe(pool, 1)

        @block.sync
        def _(sp):
            def load_unit(i):
                if before[i] is not None:
                    sp.wait_ge(*used_when[before[i]])
                dst = ring[slot_of[i]]
                if stream[i][0][0] != "ada":
                    dst = dst.rearrange("p (k n) -> p k n", k=KC)
                sp.dma_start(dst, stream[i][1]).then_inc(s_load[slot_of[i]], 16)

            def load_x(n, t, src_lat, src_ctx):
                if n >= 2:
                    sp.wait_ge(s_xn, n - 1)
                sp.dma_start(XB[n % 2], tok_tile(src_lat, src_ctx, t)).then_inc(s_xl[n % 2], 16)

            for i in range(3):
                load_unit(i)
            for name, src, rows in small:
                sp.dma_start(vrow[VEC[name]:VEC[name] + rows, :],
                             flat(src).rearrange("(r n) -> r n", n=P)).then_inc(s_small, 16)
            sp.dma_start(adab_row[0:96, :], flat(I["ada_b"]).rearrange("(r n) -> r n", n=P)).then_inc(s_small, 16)
            for i in range(3, 8):
                load_unit(i)
            load_x(0, 0, x_rows, c_rows)
            load_x(1, 1, x_rows, c_rows)
            sp.dma_start(wlr[:, :].rearrange("p (k n) -> p k n", k=KC), ev_in[:, :, E_LR:E_LR + 2 * RANK]).then_inc(s_sw, 16)
            sp.wait_ge(s_zero, 1)
            for d in range(2):
                sp.dma_start(decup[RANK * d:RANK * (d + 1), 256 * d:256 * (d + 1)], I["ev_decay_up"][0, d]).then_inc(s_sw, 16)
            for t in range(2, NT):
                load_x(t, t, x_rows, c_rows)
            for i in range(8, n_even):
                load_unit(i)
            sp_wout(sp, 0)
            sp.wait_ge(s_y, NT)
            for i in range(n_even, n_late):
                load_unit(i)
            sp_moe(sp, 0)
            sp.wait_ge(s_mm, 12 * NE)
            for i in range(n_late, n_late + 3):
                if i != index[("w0",)]:
                    load_unit(i)
            sp.wait_ge(s_sc, 16 * NE)
            sp.wait_ge(s_scc, 16 * NE)
            for t in range(4):
                load_x(norm0["mix1"] + t, t, xres, xres[LAT:T, :])
            sp.dma_start(gatew[:, 0:8, :], I["od_gate_a_w"].rearrange("l d h i j -> i (l d h) j")).then_inc(s_gw, 16)
            sp.dma_start(gatew[:, 8:16, :], I["od_gate_x_w"].rearrange("l d h i j -> i (l d h) j")).then_inc(s_gw, 16)
            sp.dma_start(sgw, I["od_sg_w"].rearrange("l g i j -> i (l g) j")).then_inc(s_gw, 16)
            sp.dma_start(sgb, I["od_sg_b"].rearrange("l g i -> (l g) i").partition_broadcast(P)).then_inc(s_gw, 16)
            for t in range(4, NT):
                load_x(norm0["mix1"] + t, t, xres, xres[LAT:T, :])
            for i in range(n_late + 2, len(stream)):
                load_unit(i)
            sp_wout(sp, 1)
            sp_moe(sp, 1)
            sp_final(sp)
        @block.tensor
        def _(pe):
            pe_start(pe)
            pe_even(pe)
            pe_gla(pe)
            pe_wout(pe, 0)
            pe_moe(pe, 0)
            pe_odd(pe)
            pe_wout(pe, 1)
            pe_moe(pe, 1)

        @block.scalar
        def _(act):
            own = Chain(act, s_ac)
            act.wait_ge(s_vc, 1)
            s3 = silc[:, :].rearrange("p (k w) -> p k w", w=2)
            for w, name in enumerate(("c", "c_ctx")):
                nc.scalar.activation(s3[:, :, w], vcol[:, VEC[name]:VEC[name] + KC], ACT.Silu).then_inc(s_silc, 1)
            act.wait_ge(s_l1, 1)
            own.do(nc.scalar.activation(lruc[:, 8:16], lruc[:, 8:16], ACT.Exp, scale=-1.0))
            nc.scalar.activation(lruc[:, 8:16], lruc[:, 8:16], ACT.Ln, bias=1.0).then_inc(s_l2, 1)
            act.wait_ge(s_const, 2)
            for t in range(NT + 1):
                if t < NT:
                    act.wait_ge(s_xl[t % 2], 16 * xl_count[t])
                    act_square(act, t)
                    act_root(act, t)
                if t >= 1:
                    if t == 1:
                        act.wait_ge(s_scg, 1)
                    act_blocks(act, t - 1, 0, 0, t - 1, 2 * ((t - 1) % 2))
            for j in range(n_even_jobs):
                if jobs[j][3] == "act":
                    act_even_job(act, own, j)
                elif jobs[j][0] == "dec":
                    act_decay(act, own, jobs[j][1])
            act_gla(act, own)
            act_wout(act, own, 0)
            act_moe(act, 0)
            act_odd(act, own)
            act_wout(act, own, 1)
            act_moe(act, 1)
            act_final(act)

        @block.vector
        def _(dve):
            own = Chain(dve, s_dv)
            dve.wait_ge(s_vt, 1)
            nc.vector.tensor_copy(vcol[:, 0:NVEC], ps[:, 7, 0:NVEC]).then_inc(s_vc, 1)
            nc.vector.tensor_copy(adab[:, :], ps[:, 7, P:P + 96]).then_inc(s_vc, 1)
            dve.wait_ge(s_vc, 2)
            lam = vcol[:, VEC["lam"]:VEC["lam"] + 8]
            nc.vector.scalar_tensor_tensor(out=lruc[:, 8:16], in0=lam, scalar=-1.0, in1=lam,
                                           op0=ALU.mult, op1=ALU.max).then_inc(s_l1, 1)
            own.do(nc.vector.tensor_scalar(lruc[:, 0:8], lam, -1.0, 0.0, ALU.mult, ALU.max))
            dve.wait_ge(s_l2, 1)
            own.do(nc.vector.tensor_tensor(lruc[:, 0:8], lruc[:, 0:8], lruc[:, 8:16], ALU.add))
            nc.vector.tensor_scalar(lruc[:, 16:24], lruc[:, 0:8], -LRU_C, None, ALU.mult)
            nc.vector.tensor_scalar(lruc[:, 0:8], lruc[:, 0:8], LRU_C, None, ALU.mult).then_inc(s_lc, 1)
            dve_norm(dve, own, 0)
            dve_ada_rows(dve, 0)
            dve_ada_columns(dve, 0)
            dve.wait_ge(s_scg, 1)
            for t in range(NT + 1):
                if 1 <= t < NT:
                    dve_norm(dve, own, t)
                if t >= 1:
                    dve_blocks(dve, t - 1, 0, 0, t - 1, 2 * ((t - 1) % 2))
            for pd in range(4):
                dve_decay_in(dve, pd)
                if pd >= 1:
                    dve_decay_out(dve, own, pd - 1)
            dve_decay_out(dve, own, 3)
            for t in range(NT):
                dve.wait_ge(s_vm, t + 1)
                nc.vector.tensor_copy(vtok[:, t, :], ps[:, 6 + t % 2, :]).then_inc(s_ve, 1)
            for what, *at in even_order:
                if what == "copy":
                    dve_ada_rows(dve, at[0])
                elif what == "rows":
                    dve_ada_columns(dve, at[0])
                elif what == "job" and jobs[at[0]][3] == "dve":
                    dve_even_job(dve, own, at[0])
            dve_gla(dve, own)
            dve_wout(dve, own, 0)
            dve_moe(dve, 0)
            dve_odd(dve, own)
            dve_wout(dve, own, 1)
            dve_moe(dve, 1)
            dve_final(dve, own)


_INS = ["x", "c", "ctx", "c_ctx", "ada_w", "ada_b", "norm_mix_g", "norm_ffn_g", "norm_final_g",
        "ev_w_in", "ev_conv_w", "ev_conv_b", "ev_decay_up", "ev_decay_b", "ev_norm_g", "ev_w_out",
        "od_w_in", "od_conv_w", "od_conv_b", "od_gate_a_w", "od_gate_a_b", "od_gate_x_w", "od_gate_x_b",
        "od_lambda", "od_sg_norm_g", "od_sg_w", "od_sg_b", "od_w_out",
        "moe_router", "moe_w_gate", "moe_w_up", "moe_w_down"]


def kernel(**inputs):
    import numpy as np
    import concourse.bacc as bacc
    from concourse.bass_utils import run_bass_kernel_spmd

    nc = bacc.Bacc("TRN2", target_bir_lowering=False, num_devices=1)
    arrays, aps = {}, {}
    for name in _INS:
        a = np.ascontiguousarray(inputs[name])
        arrays[f"in_{name}"] = a
        aps[name] = nc.dram_tensor(f"in_{name}", a.shape, mybir.dt.from_np(a.dtype), kind="ExternalInput").ap()
    out = nc.dram_tensor("out_0", (1, LAT, D), F32, kind="ExternalOutput").ap()
    build(nc, aps, out)
    return run_bass_kernel_spmd(nc, [arrays], core_ids=[0]).results[0]["out_0"]
```

```python
from contextlib import ExitStack

import concourse.bass as bass
from concourse import mybir

F32 = mybir.dt.float32
F32R = mybir.dt.float32r
U32 = mybir.dt.uint32
ALU = mybir.AluOpType
ACT = mybir.ActivationFunctionType
AXX = mybir.AxisListType.X

P = 128
D = 1024
KC = D // P
TL = 8
TC = 2
NT = TL + TC
T = NT * P
LAT = TL * P
CTX = TC * P
BANK = 512
EPS = 1e-6

HEADS = 4
DK = 64
CHUNK = 64
NCH = T // CHUNK
TAU = 16.0
GRID = 64
RANK = 16
LRU_C = 8.0

NE = 16
CAPL = 2 * LAT // NE
CAPC = 2 * CTX // NE
UNIT = 2048
WS = 3

E_BG, E_CG, E_XA, E_Q, E_G, E_K, E_V, E_LR = 0, 512, 1024, 1536, 1792, 2304, 2560, 3072
O_XB, O_GB, O_U, O_V = 0, 512, 1024, 1536

VEC = {}
_row = 0
for _name, _n in (("c", 8), ("c_ctx", 8), ("mix_g", 16), ("ffn_g", 16), ("ev_conv_w", 12), ("ev_conv_b", 4),
                  ("decay_b", 4), ("ev_norm_g", 4), ("od_conv_w", 16), ("od_conv_b", 4), ("gate_a_b", 8),
                  ("gate_x_b", 8), ("lam", 8), ("sg_norm_g", 4)):
    VEC[_name] = _row
    _row += _n
NVEC = _row


def build(nc, I, out):
    ctx = ExitStack()
    with ctx:
        def sem(name):
            return ctx.enter_context(nc.semaphore(name))

        def sb(name, words, dt=F32):
            return ctx.enter_context(nc.sbuf_tensor(name, [P, words], dt))

        def sb_twice(name, words):
            with nc.sbuf_tensor(name, [P, words], F32) as plain:
                pass
            return plain, ctx.enter_context(nc.sbuf_tensor(name + "_r", [P, words], F32R))

        ident = sb("ident", P)
        ones = sb("ones", P)
        vcol = sb("vcol", P)
        adab = sb("adab", 96)
        silc = sb("silc", 16)
        modc = sb("modc", 192)
        scg = sb("scg", 64)
        bc, bc_r = sb_twice("bc", 4 * D)
        maskf = bc[:, 0:P]
        maskb = bc[:, P:2 * P]
        chunk0 = bc[:, 256:256 + T]
        lrT = bc[:, 1536:1536 + T]
        decup = bc[:, 2816:3328]
        wlr = bc[:, 3328:3328 + KC * 2 * RANK]
        rowtmp = bc[:, 3584:4096]
        tkf = sb("tkf", P)
        tkg = sb("tkg", P)
        st = sb("st", 64)
        router = sb("router", KC * NE)
        dec = sb("dec", 4 * NCH)
        lruc = sb("lruc", 24)
        epsc = sb("epsc", 1)
        vst = sb("vst", 6 * TL)
        vmv = sb("vmv", 2 * TL)
        vsd = sb("vsd", 2 * TL)
        gcolT = sb("gcolT", 48)
        icolT = sb("icolT", 48, U32)
        gidx = sb("gidx", 4, U32)
        sm = sb("sm", 4 * NE)

        R_H, R_Hr = sb_twice("R_H", KC * T)
        R_C, R_Cr = sb_twice("R_C", KC * T)
        vrow, adab_row = R_C[:, 0:P], R_C[:, P:2 * P]
        R_M, R_Mr = sb_twice("R_M", 15360)
        R_W, R_Wr = sb_twice("R_W", 11264)

        hT = R_H[:, :].rearrange("p (k t) -> p k t", k=KC)
        cat = R_C[:, :].rearrange("p (k t) -> p k t", k=KC)
        vtok = R_M[:, 0:NT * 512].rearrange("p (t n) -> p t n", t=NT)
        kT = R_M[:, 5120:7680].rearrange("p (c t) -> p c t", c=2)
        qT = R_M[:, 7680:10240].rearrange("p (c t) -> p c t", c=2)
        BX = R_M[:, 10240:15360].rearrange("p (c t) -> p c t", c=4)
        ring = [R_W[:, UNIT * s:UNIT * (s + 1)] for s in range(WS)]
        TMP = [R_W[:, 6144 + T * i:6144 + T * (i + 1)] for i in range(4)]
        wout = R_W[:, 0:8192].rearrange("p (k n) -> p k n", k=KC)
        XB = [R_W[:, 8192 + D * i:8192 + D * (i + 1)] for i in range(2)]
        XN = R_W[:, 10240:11264]
        whi_out = R_Hr[:, 0:8192].rearrange("p (k n) -> p k n", k=KC)
        wlo_out = R_Wr[:, 0:8192].rearrange("p (k n) -> p k n", k=KC)
        cathi = [R_Mr[:, 12288 + D * i:12288 + D * (i + 1)].rearrange("p (k t) -> p k t", k=KC) for i in range(2)]
        hN = [R_H[:, 8192 + D * i:8192 + D * (i + 1)].rearrange("p (k t) -> p k t", k=KC) for i in range(2)]
        diag = [R_H[:, 8192 + D * i:8192 + D * (i + 1)] for i in range(2)]
        ktok = R_H[:, 0:2560].rearrange("p (t r d) -> p t r d", t=NT, r=2)
        SIN = R_H[:, 2560:7680].rearrange("p (r c e) -> p r c e", r=2, c=NCH)
        attS = R_H[:, 7680:9728].rearrange("p (b r n) -> p b r n", b=2, r=2)
        TST = R_H[:, 9728:10240].rearrange("p (r b e) -> p r b e", r=2, b=2)
        SQ = [R_W[:, 8192 + 512 * i:8192 + 512 * (i + 1)] for i in range(2)]
        RS = [R_W[:, 9216 + 512 * i:9216 + 512 * (i + 1)] for i in range(2)]
        XC = R_M[:, 0:5120].rearrange("p (c t) -> p c t", c=4)
        HL = R_M[:, 5120:9216].rearrange("p (c t) -> p c t", c=4)
        vln = R_M[:, 9216:13312].rearrange("p (t n) -> p t n", t=TL)
        sgw = R_M[:, 13312:13824].rearrange("p (g n) -> p g n", g=4)
        sgwT = R_M[:, 13824:14336].rearrange("p (g n) -> p g n", g=4)
        sgb = R_M[:, 14848:15360].rearrange("p (g n) -> p g n", g=4)
        cat1 = R_C[:, 0:8192].rearrange("p (k t) -> p k t", k=KC)
        catlo = [R_Cr[:, :].rearrange("p (k t) -> p k t", k=KC), R_Cr[:, 0:8192].rearrange("p (k t) -> p k t", k=KC)]
        gatew = R_C[:, 8192:10240].rearrange("p (m j) -> p m j", m=16)
        affT = R_M[:, 14336:14336 + LAT // 2]
        raw = [R_M[:, UNIT * s:UNIT * (s + 1)] for s in range(7)] + [R_H[:, 0:UNIT]]
        wlo = [R_Hr[:, UNIT * s:UNIT * (s + 1)] for s in range(1, 5)]
        whi = [R_Wr[:, UNIT * s:UNIT * (s + 1)] for s in range(4)]
        xhi = [bc_r[:, D * i:D * (i + 1)].rearrange("p (k t) -> p k t", k=KC) for i in range(2)]
        hidh = R_Mr[:, 14336:15360].rearrange("p (k t) -> p k t", k=KC)
        xT = [R_C[:, 1280 * i:1280 * (i + 1)].rearrange("p (k c) -> p k c", k=KC) for i in range(2)]
        hidT = R_C[:, 2560:3840].rearrange("p (k c) -> p k c", k=KC)
        xlo = [R_Cr[:, 1280 * i:1280 * (i + 1)].rearrange("p (k c) -> p k c", k=KC) for i in range(2)]
        hidlo = R_Cr[:, 2560:3840].rearrange("p (k c) -> p k c", k=KC)
        xg = R_C[:, 3840:4864]
        xgc = R_C[:, 4864:5888]
        tmc = R_C[:, 5888:6400]
        silx = R_C[:, 6400:6912]
        hidc = R_C[:, 6912:7424]
        outc = R_C[:, 7424:8448]
        tkv = R_C[:, 9472:9600]
        tki = R_C[:, 9600:9728].bitcast(U32)
        tmo = R_C[:, 8448:9472]
        late_rows = [R_C[:, 5888 + BANK * i:5888 + BANK * (i + 1)] for i in range(2)]
        late_cols = [R_C[:, 7424 + BANK * i:7424 + BANK * (i + 1)] for i in range(2)]
        sil, hid, eout = XB[0], XB[1], XN
        FB = [R_M[:, D * t:D * (t + 1)] for t in range(TL)]

        ps = ctx.enter_context(nc.psum_tensor("ps", [P, 8, BANK], F32))

        def wide(s, n):
            return ps[:, 3 * s:3 * s + 3, :].rearrange("p b n -> p (b n)")[:, 0:n]

        xres = nc.dram_tensor("xres", [T, D], F32).ap()
        xnd = nc.dram_tensor("xnd", [T, D], F32).ap()

        x_rows = I["x"].rearrange("b t d -> (b t) d")
        c_rows = I["ctx"].rearrange("b t d -> (b t) d")

        def tok_tile(src_lat, src_ctx, t):
            return src_lat[t * P:(t + 1) * P, :] if t < TL else src_ctx[(t - TL) * P:(t - TL + 1) * P, :]

        ev_in = I["ev_w_in"].rearrange("l (k p) n -> (l p) k n", p=P)
        od_in = I["od_w_in"].rearrange("l (k p) n -> (l p) k n", p=P)

        def ada_unit(l, g, k):
            return ("ada", l, g, k), I["ada_w"][l, k * P:(k + 1) * P, g * 2048:(g + 1) * 2048]

        def col_unit(name, src, col):
            return (name,), src[:, :, col:col + 256]

        stream = [ada_unit(0, 0, k) for k in range(KC)]
        stream += [col_unit("k", ev_in, E_K), col_unit("v0", ev_in, E_V), col_unit("v1", ev_in, E_V + 256)]
        slot_of = [i % WS for i in range(len(stream))]
        gap_ada = [ada_unit(l, g, k) for l, g in ((0, 1), (0, 2), (1, 0)) for k in range(KC)]
        proj = [("q", E_Q), ("g0", E_G), ("g1", E_G + 256)] + \
               [(f"{n}{h}", c + 256 * h) for h in range(2) for n, c in (("cg", E_CG), ("xa", E_XA), ("bg", E_BG))]
        even_order, slot, job_no, rows_due = [], (slot_of[-1] + 1) % WS, 7, None
        for name, col in proj:
            unit_no = len(stream)
            stream.append(col_unit(name, ev_in, col))
            slot_of.append(slot)
            for half in range(2):
                even_order.append(("job", job_no, unit_no, half))
                job_no += 1
                if rows_due is not None:
                    even_order.append(("rows", rows_due))
                    rows_due = None
                for beside in ((1, 2), (1,))[half]:
                    if gap_ada:
                        key = gap_ada[0][0]
                        even_order.append(("ada", len(stream)))
                        stream.append(gap_ada.pop(0))
                        slot_of.append((slot + beside) % WS)
                        if key[3] == KC - 1:
                            rows_due = 3 * key[1] + key[2]
                            even_order.append(("copy", rows_due))
            slot = (slot + 2) % WS
        assert not gap_ada and rows_due is None
        n_even = len(stream)
        LATE = (4, 5)
        for l, g in ((1, 1), (1, 2)):
            for k in range(KC):
                slot_of.append(len(stream) % WS)
                stream.append(ada_unit(l, g, k))
        n_late = len(stream)
        for name, col, slot in (("xb0", O_XB, 2), ("xb1", O_XB + 256, 0), ("w0", O_V, 0), ("w1", O_V + 256, 1),
                                ("gb0", O_GB, 2), ("gb1", O_GB + 256, 2), ("u0", O_U, 0), ("u1", O_U + 256, 1)):
            stream.append(col_unit(name, od_in, col))
            slot_of.append(slot)
        index = {key: i for i, (key, _) in enumerate(stream)}
        n_in_slot = [slot_of[:i + 1].count(slot_of[i]) for i in range(len(stream))]
        before = [max([j for j in range(i) if slot_of[j] == slot_of[i]], default=None) for i in range(len(stream))]
        assert slot_of[index[("v0",)]] + 1 == slot_of[index[("v1",)]]

        even_jobs = [("lr", 0, T, "act"), ("k", 0, T, "act"), ("k", 1, T, "act")] + \
                    [("dec", i, T, "dve") for i in range(4)] + \
                    [("q", 0, T, "act"), ("q", 1, T, "act")] + [("g", i, T, "act") for i in range(4)]
        for h in range(2):
            even_jobs += [("cg", 2 * h, T, "act"), ("cg", 2 * h + 1, T, "act"), ("xa", 2 * h, T, "dve"),
                          ("xa", 2 * h + 1, T, "dve"), ("bg", 2 * h, T, "dve"), ("bg", 2 * h + 1, T, "dve")]
        odd_order = [("xb", c) for c in range(4)]
        fill = [[("v", 0), ("v", 1), ("v", 2)], [("v", 3), ("v", 4), ("v", 5)], [("v", 6), ("v", 7), ("gb", 0)],
                [("gb", 1)], [("gb", 2)], [("gb", 3), ("u", 0)], [("u", 1), ("u", 2)], [("u", 3)]]
        for it in range(8):
            odd_order += [("ga", it), ("gx", it)] + fill[it]
        odd_jobs = [(k, i, T if k in ("xb", "ga", "gx") else LAT, "act") for k, i in odd_order if k != "v"]

        jobs = even_jobs + odd_jobs
        n_even_jobs = len(even_jobs)
        emptied = {"act": [0], "dve": [0]}
        for j in jobs:
            for e in emptied:
                emptied[e].append(emptied[e][-1] + (j[3] == e))
        job_at = {j[:2] + (i >= n_even_jobs,): i for i, j in enumerate(jobs)}

        norm0 = {"mix0": 0, "ffn0": NT, "mix1": 2 * NT, "ffn1": 3 * NT, "final": 3 * NT + TL}

        def sems(names):
            return [sem(n) for n in names.split()]

        constants_made = sem("constants_made")
        zeros_made = sem("zeros_made")
        small_vectors_loaded = sem("small_vectors_loaded")
        unit_loaded = [sem(f"unit_loaded{i}") for i in range(WS)]
        ada_unit_used = sem("ada_unit_used")
        vectors_transposed = sem("vectors_transposed")
        vectors_copied = sem("vectors_copied")
        cond_silu_done = sem("cond_silu_done")
        late_rows_copied = sem("late_rows_copied")
        late_rows_transposed = sem("late_rows_transposed")
        late_columns_copied = sem("late_columns_copied")
        ada_rows_copied = sem("ada_rows_copied")
        ada_rows_transposed = sem("ada_rows_transposed")
        ada_columns_added = sem("ada_columns_added")
        scales_done = sem("scales_done")
        diagonal_made = sem("diagonal_made")
        gate_row_in_psum = sem("gate_row_in_psum")
        gate_row_copied = sem("gate_row_copied")
        vector_own = sem("vector_own")
        scalar_own = sem("scalar_own")
        pool_own = sem("pool_own")
        tile_loaded = sems("tile_loaded0 tile_loaded1")
        squares_summed = sem("squares_summed")
        root_taken = sem("root_taken")
        tile_normed = sem("tile_normed")
        normed_transposed = sem("normed_transposed")
        h_written_by_vector = sem("h_written_by_vector")
        h_written_by_scalar = sem("h_written_by_scalar")
        job_done = sem("job_done")
        job_emptied_by_scalar = sem("job_emptied_by_scalar")
        job_emptied_by_vector = sem("job_emptied_by_vector")
        v_tile_done = sem("v_tile_done")
        v_tile_copied = sem("v_tile_copied")
        decay_abs_done = sem("decay_abs_done")
        decay_log_done = sem("decay_log_done")
        decay_exps_done = sem("decay_exps_done")
        keys_decayed = sem("keys_decayed")
        keys_transposed = sem("keys_transposed")
        key_tokens_copied = sem("key_tokens_copied")
        updates_done = sem("updates_done")
        state_updated = sem("state_updated")
        state_in_scaled = sem("state_in_scaled")
        scores_done = sem("scores_done")
        scores_masked = sem("scores_masked")
        outputs_done = sem("outputs_done")
        outputs_squared = sem("outputs_squared")
        square_means_done = sem("square_means_done")
        recip_roots_done = sem("recip_roots_done")
        outputs_scaled = sem("outputs_scaled")
        wout_loaded = sems("wout_loaded0 wout_loaded1")
        wout_high_done = sem("wout_high_done")
        wout_low_done = sem("wout_low_done")
        mixed_high_done = sem("mixed_high_done")
        mixed_low_done = sem("mixed_low_done")
        projected = sem("projected")
        residual_added = sem("residual_added")
        outputs_gated = sem("outputs_gated")
        decays_summed = sem("decays_summed")
        conv_done = sem("conv_done")
        lowrank_weights_loaded = sem("lowrank_weights_loaded")
        recurrent_part_done = sem("recurrent_part_done")
        spatial_gate_applied = sem("spatial_gate_applied")
        lru_item_done = sem("lru_item_done")
        raw_slot_loaded = [sem(f"raw_slot_loaded{i}") for i in range(8)]
        unit_high_done = sem("unit_high_done")
        unit_low_done = sem("unit_low_done")
        expert_unit_used = sem("expert_unit_used")
        tokens_high_done = sem("tokens_high_done")
        tokens_low_done = sem("tokens_low_done")
        rows_gathered = sem("rows_gathered")
        context_rows_gathered = sem("context_rows_gathered")
        gather_index_set = sem("gather_index_set")
        context_gather_index_set = sem("context_gather_index_set")
        scatter_index_set = sem("scatter_index_set")
        context_scatter_index_set = sem("context_scatter_index_set")
        rows_transposed = sem("rows_transposed")
        tokens_by_vector = sem("tokens_by_vector")
        tokens_by_scalar = sem("tokens_by_scalar")
        silu_done = sem("silu_done")
        hidden_done = sem("hidden_done")
        context_hidden_done = sem("context_hidden_done")
        context_gate_half_copied = sem("context_gate_half_copied")
        context_gate_summed = sem("context_gate_summed")
        context_silu_done = sem("context_silu_done")
        context_up_half_copied = sem("context_up_half_copied")
        context_up_summed = sem("context_up_summed")
        context_down_half_copied = sem("context_down_half_copied")
        context_down_summed = sem("context_down_summed")
        hidden_transposed = sem("hidden_transposed")
        hidden_low_done = sem("hidden_low_done")
        hidden_high_done = sem("hidden_high_done")
        expert_rows_done = sem("expert_rows_done")
        context_expert_rows_done = sem("context_expert_rows_done")
        rows_scattered = sem("rows_scattered")
        context_rows_scattered = sem("context_rows_scattered")
        odd_weights_loaded = sem("odd_weights_loaded")
        spatial_weights_transposed = sem("spatial_weights_transposed")
        spatial_weights_copied = sem("spatial_weights_copied")
        odd_conv_done = sem("odd_conv_done")
        v_gelu_done = sem("v_gelu_done")
        v_normed = sem("v_normed")
        v_statistics_done = sem("v_statistics_done")
        v_deviation_done = sem("v_deviation_done")
        spatial_mixed = sem("spatial_mixed")
        lru_constants_done = sem("lru_constants_done")
        lru_a_done = sem("lru_a_done")
        lru_square_done = sem("lru_square_done")
        lru_root_done = sem("lru_root_done")
        lambda_abs_done = sem("lambda_abs_done")
        lambda_log_done = sem("lambda_log_done")
        final_gain_loaded = sem("final_gain_loaded")
        final_tile_done = sem("final_tile_done")
        final_tile_stored = sem("final_tile_stored")
        final_tile_loaded = [sem(f"final_tile_loaded{i}") for i in range(TL)]
        tile_stored = sems("tile_stored0 tile_stored1")
        normed_stored = sem("normed_stored")
        logits_done = sem("logits_done")
        logit_max_done = sem("logit_max_done")
        logit_exps_done = sem("logit_exps_done")
        affinities_done = sem("affinities_done")
        affinities_transposed = sem("affinities_transposed")
        affinities_copied = sem("affinities_copied")
        ranked = sem("ranked")
        ranked_transposed = sem("ranked_transposed")
        tokens_chosen = sem("tokens_chosen")
        router_loaded = sem("router_loaded")

        class Chain:

            def __init__(self, eng, s):
                self.eng, self.s, self.n = eng, s, 0

            def mark(self, ins):
                self.n += 1
                ins.then_inc(self.s, 1)
                return self.n

            def do(self, ins):
                self.eng.wait_ge(self.s, self.mark(ins))

        N_CONST = 5
        small = [("c", I["c"], 8), ("c_ctx", I["c_ctx"], 8), ("mix_g", I["norm_mix_g"], 16),
                 ("ffn_g", I["norm_ffn_g"], 16), ("ev_conv_w", I["ev_conv_w"], 12), ("ev_conv_b", I["ev_conv_b"], 4),
                 ("decay_b", I["ev_decay_b"], 4), ("ev_norm_g", I["ev_norm_g"], 4),
                 ("od_conv_w", I["od_conv_w"], 16), ("od_conv_b", I["od_conv_b"], 4),
                 ("gate_a_b", I["od_gate_a_b"], 8), ("gate_x_b", I["od_gate_x_b"], 8), ("lam", I["od_lambda"], 8),
                 ("sg_norm_g", I["od_sg_norm_g"], 4)]
        N_SMALL = len(small) + 1
        DONE_SMALL = 16 * N_SMALL

        def flat(ap):
            names = "abcd"[:len(ap.shape)]
            return ap if len(names) == 1 else ap.rearrange(" ".join(names) + " -> (" + " ".join(names) + ")")

        xl_count, xst_count = {}, {}
        for n in range(norm0["final"]):
            xl_count[n] = n // 2 + 1
        stored = [n for n in range(norm0["final"])
                  if norm0["ffn0"] <= n < norm0["mix1"] or n >= norm0["ffn1"]]
        for n in stored:
            xst_count[n] = sum(1 for m in stored if m <= n and m % 2 == n % 2)

        block = ctx.enter_context(nc.Block())

        used_when, n_ada = [], 0
        unit_jobs = {}
        for i, (key, _) in enumerate(stream):
            if key[0] == "ada":
                n_ada += 1
                used_when.append((ada_unit_used, n_ada))
            elif key[0] in ("v0", "v1"):
                used_when.append((v_tile_done, NT))
            elif key[0] in ("w0", "w1"):
                used_when.append((v_tile_done, NT + TL))
            else:
                kind, half = ("k", 0) if key[0] in "kq" else (key[0][:-1], int(key[0][-1]))
                kind = key[0] if key[0] in "kq" else kind
                unit_jobs[i] = [job_at[(kind, 2 * half + h, i >= n_even)] for h in range(2)]
                used_when.append((job_done, unit_jobs[i][1] + 1))

        SPLIT = [(0, BANK), (BANK, BANK), (2 * BANK, T - 2 * BANK)]

        def unit_in(pe, i):
            pe.wait_ge(unit_loaded[slot_of[i]], 16 * n_in_slot[i])

        def ada(pe, i):
            _, l, g, k = stream[i][0]
            if k == 0 and 3 * l + g > 0:
                pe.wait_ge(ada_rows_copied, min(3 * l + g, 4))
                if 3 * l + g > LATE[0]:
                    pe.wait_ge(late_rows_copied, 3 * l + g - LATE[0])
            unit_in(pe, i)
            for q in range(4):
                ins = pe.matmul(ps[32 * q:32 * q + 2, 6, :], silc[:, 2 * k:2 * k + 2],
                                ring[slot_of[i]][:, q * BANK:(q + 1) * BANK], start=(k == 0), stop=(k == KC - 1))
            ins.then_inc(ada_unit_used, 1)

        def ada_rows(pe, a):
            pe.wait_ge(ada_rows_copied, a + 1)
            pe.wait_ge(vectors_copied, 2) if a == 0 else pe.wait_ge(ada_columns_added, a)
            for j in range(4):
                ins = pe.transpose(ps[:, 7, j * P:(j + 1) * P], rowtmp[:, j * P:(j + 1) * P], ident[:, :])
            ins.then_inc(ada_rows_transposed, 1)

        def before_mixer(n):
            return n < norm0["ffn0"] or norm0["mix1"] <= n < norm0["ffn1"]

        def normed(n):
            return R_C[:, D * (1 + n % 2):D * (2 + n % 2)] if before_mixer(n) else XN

        def pe_late_ada(pe):
            pe.wait_ge(residual_added, NT)
            for a in LATE:
                for i in range(n_even + (a - 4) * KC, n_even + (a - 3) * KC):
                    ada(pe, i)
                pe.wait_ge(late_rows_copied, a - 3)
                for j in range(4):
                    ins = pe.transpose(ps[:, 7 - 2 * (a - 4), j * P:(j + 1) * P],
                                       late_rows[a - 4][:, j * P:(j + 1) * P], ident[:, :])
                ins.then_inc(late_rows_transposed, 1)

        def act_late_ada(act):
            act.wait_ge(projected, NT)
            for a in LATE:
                act.wait_ge(ada_unit_used, KC * (a + 1))
                for q in range(4):
                    ins = nc.scalar.copy(late_rows[a - 4][32 * q:32 * q + 2, :], ps[32 * q:32 * q + 2, 6, :])
                ins.then_inc(late_rows_copied, 1)
                act.wait_ge(late_rows_transposed, a - 3)
                nc.scalar.copy(late_cols[a - 4], ps[:, 7 - 2 * (a - 4), :]).then_inc(late_columns_copied, 1)

        def norm_transposes(pe, n, bank, last):
            pe.wait_ge(tile_normed, n + 1)
            if last is not None:
                pe.wait_ge(h_written_by_vector, last + 1)
                pe.wait_ge(h_written_by_scalar, last + 1)
            for k in range(KC):
                ins = pe.transpose(ps[:, bank + k // 4, (k % 4) * P:(k % 4 + 1) * P], normed(n)[:, k * P:(k + 1) * P],
                                   ident[:, :])
            ins.then_inc(normed_transposed, 1)

        def banks_free(pe, j):
            if j >= 2:
                if emptied["act"][j - 1]:
                    pe.wait_ge(job_emptied_by_scalar, emptied["act"][j - 1])
                if emptied["dve"][j - 1]:
                    pe.wait_ge(job_emptied_by_vector, emptied["dve"][j - 1])

        def job(pe, j, i, half):
            n = jobs[j][2]
            banks_free(pe, j)
            unit_in(pe, i)
            w = ring[slot_of[i]].rearrange("p (k n) -> p k n", k=KC)
            for c0, cn in SPLIT:
                if c0 >= n:
                    break
                for k in range(KC):
                    ins = pe.matmul(wide(j % 2, n)[:, c0:c0 + cn], w[:, k, half * P:(half + 1) * P],
                                    hT[:, k, c0:c0 + cn], start=(k == 0), stop=(k == KC - 1))
            ins.then_inc(job_done, 1)

        def v_tile(pe, t, unit):
            v2 = R_W[:, UNIT * slot_of[unit]:UNIT * slot_of[unit] + 2 * UNIT].rearrange(
                "p (u k n) -> p k u n", u=2, k=KC)
            out_ = ps[:, 6 + t % 2, :].rearrange("p (u n) -> p u n", u=2)
            for k in range(KC):
                ins = pe.matmul(out_, hT[:, k, t * P:(t + 1) * P], v2[:, k, :, :],
                                start=(k == 0), stop=(k == KC - 1))
            ins.then_inc(v_tile_done, 1)

        def pe_start(pe):
            pe.wait_ge(constants_made, 1)
            pe.wait_ge(small_vectors_loaded, DONE_SMALL)
            pe.transpose(ps[:, 7, 0:NVEC], vrow[0:NVEC, :], ident[0:NVEC, 0:NVEC])
            pe.transpose(ps[:, 7, P:P + 96], adab_row[0:96, :], ident[0:96, 0:96]).then_inc(vectors_transposed, 1)
            pe.wait_ge(cond_silu_done, 2)
            for i in range(8):
                ada(pe, i)
            ada_rows(pe, 0)
            for t in range(NT):
                norm_transposes(pe, t, 2 * (t % 2), t - 2 if t >= 2 else None)

        def pe_even(pe):
            pe.wait_ge(lowrank_weights_loaded, 48)
            pe.wait_ge(h_written_by_vector, NT)
            pe.wait_ge(h_written_by_scalar, NT)
            for c0, cn in SPLIT:
                for k in range(KC):
                    ins = pe.matmul(wide(0, T)[0:32, c0:c0 + cn], wlr[:, k * 32:(k + 1) * 32], hT[:, k, c0:c0 + cn],
                                    start=(k == 0), stop=(k == KC - 1))
            ins.then_inc(job_done, 1)
            j = 1
            for half in range(2):
                job(pe, j, index[("k",)], half)
                j += 1
            for pd in range(4):
                banks_free(pe, j)
                for c0, cn in SPLIT:
                    ins = pe.matmul(wide(j % 2, T)[:, c0:c0 + cn], decup[0:32, pd * P:(pd + 1) * P],
                                    lrT[0:32, c0:c0 + cn], start=True, stop=True)
                ins.then_inc(job_done, 1)
                j += 1
            unit_in(pe, index[("v0",)])
            unit_in(pe, index[("v1",)])
            pe.wait_ge(ada_rows_copied, 1)
            pe.wait_ge(ada_columns_added, 1)
            for t in range(NT):
                if t >= 2:
                    pe.wait_ge(v_tile_copied, t - 1)
                v_tile(pe, t, index[("v0",)])
            for what, *at in even_order:
                if what == "ada":
                    if stream[at[0]][0][1:] == (0, 1, 0):
                        pe.wait_ge(v_tile_copied, NT)
                    ada(pe, at[0])
                elif what == "rows":
                    ada_rows(pe, at[0])
                elif what == "job":
                    assert j == at[0]
                    job(pe, *at)
                    j += 1
            assert j == n_even_jobs

        order = [[16, 17, 18, 19] + list(range(16)), [19, 18, 17, 16] + list(range(15, -1, -1))]

        def pe_gla(pe):
            pe.wait_ge(constants_made, N_CONST)
            for p in range(2):
                pe.wait_ge(keys_decayed, p + 1)
                for g in range(5):
                    n = 5 * p + g
                    if p == 0 and g == 0:
                        pe.wait_ge(job_emptied_by_scalar, emptied["act"][n_even_jobs])
                        pe.wait_ge(job_emptied_by_vector, emptied["dve"][n_even_jobs])
                    if n >= 2:
                        pe.wait_ge(key_tokens_copied, n - 1)
                    for q in range(4):
                        t, r = 2 * g + q // 2, q % 2
                        ins = pe.transpose(ps[:, n % 2, q * P:(q + 1) * P], BX[:, 2 * r + p, t * P:(t + 1) * P],
                                           ident[:, :])
                    ins.then_inc(keys_transposed, 1)
                pe.wait_ge(key_tokens_copied, 5 * (p + 1))
                for b in range(NCH // 4):
                    if b >= 2:
                        pe.wait_ge(state_updated, 2 * NCH * p + 8 * (b - 1))
                    for s in range(4 * b, 4 * b + 4):
                        for r in range(2):
                            c = order[r][s]
                            h0, t = 64 * (c % 2), c // 2
                            for hh in range(2):
                                ins = pe.matmul(ps[64 * hh:64 * hh + 64, 2 * (b % 2) + c % 2, (s % 4) * P:(s % 4 + 1) * P],
                                                ktok[h0:h0 + 64, t, r, 64 * hh:64 * hh + 64],
                                                vtok[h0:h0 + 64, t, (2 * p + hh) * P:(2 * p + hh + 1) * P],
                                                start=True, stop=True)
                    ins.then_inc(updates_done, 1)
                pe.wait_ge(state_in_scaled, 2 * (NCH - 1) * (p + 1))
                pe.wait_ge(state_updated, 2 * NCH * (p + 1))

                def scores(g):
                    n = 5 * p + g
                    if n >= 1:
                        pe.wait_ge(scores_masked, n)
                    for hh in range(2):
                        for r in range(2):
                            for tt in range(2):
                                t = 2 * g + tt
                                qd = (qT if r == 0 else kT)[64 * hh:64 * hh + 64, p, t * P:(t + 1) * P]
                                ins = pe.matmul(ps[:, 4 + hh, (2 * r + tt) * P:(2 * r + tt + 1) * P],
                                                BX[64 * hh:64 * hh + 64, 2 * r + p, t * P:(t + 1) * P], qd,
                                                start=True, stop=True)
                    ins.then_inc(scores_done, 1)

                def outputs(g):
                    n = 5 * p + g
                    pe.wait_ge(scores_masked, n + 1)
                    if n >= 1:
                        pe.wait_ge(outputs_squared, n)
                        pe.wait_ge(outputs_gated, n)
                    for hh in range(2):
                        for tt in range(2):
                            t = 2 * g + tt
                            o = ps[:, 6 + hh, tt * P:(tt + 1) * P]
                            vh = vtok[:, t, (2 * p + hh) * P:(2 * p + hh + 1) * P]
                            mm = [(o, vh, attS[:, n % 2, r, (2 * hh + tt) * P:(2 * hh + tt + 1) * P]) for r in range(2)]
                            for r in range(2):
                                for cc in range(2):
                                    c = 2 * t + cc
                                    if c != order[r][0]:
                                        qd = (qT if r == 0 else kT)[64 * hh:64 * hh + 64, p, c * 64:(c + 1) * 64]
                                        mm.append((o[:, cc * 64:(cc + 1) * 64], SIN[64 * hh:64 * hh + 64, r, c, :], qd))
                            for x, (oo, lhs, rhs) in enumerate(mm):
                                ins = pe.matmul(oo, lhs, rhs, start=(x == 0), stop=(x == len(mm) - 1))
                    ins.then_inc(outputs_done, 1)

                def means(g):
                    n = 5 * p + g
                    pe.wait_ge(outputs_squared, n + 1)
                    if g >= 2:
                        pe.wait_ge(recip_roots_done, n - 1)
                    pe.matmul(ps[:, n % 2, :], ones[:, :], SQ[n % 2], start=True, stop=True).then_inc(square_means_done, 1)

                scores(0)
                for g in range(5):
                    if g < 4:
                        scores(g + 1)
                    if g >= 1:
                        means(g - 1)
                    outputs(g)
                means(4)
                pe.wait_ge(outputs_scaled, 5 * (p + 1))

        def pe_gates_as_rows(pe, l):
            for m in range(len(gate_rows(l))):
                n = (0 if l == 0 else 4) + m
                pe.wait_ge(diagonal_made, n + 1)
                if n >= 2:
                    pe.wait_ge(gate_row_copied, n - 1)
                for c in range(2):
                    ins = pe.matmul(ps[:, 2 * (n % 2) + c, :], ones[:, :], diag[n % 2][:, c * BANK:(c + 1) * BANK],
                                    start=True, stop=True)
                ins.then_inc(gate_row_in_psum, 1)

        def pe_wout(pe, l):
            nt = NT if l == 0 else TL
            n0 = norm0["ffn0"] if l == 0 else norm0["ffn1"]
            r0 = 0 if l == 0 else NT
            if l == 1:
                pe.wait_ge(job_emptied_by_scalar, emptied["act"][len(jobs)])
            pe_gates_as_rows(pe, l)
            pe.wait_ge(gate_row_copied, 4 if l == 0 else 6)
            pe.wait_ge(wout_loaded[0], 16 * (l + 1))
            pe.wait_ge(wout_loaded[1], 16 * (l + 1))
            if l == 0:
                pe.wait_ge(outputs_scaled, 10)
            else:
                pe.wait_ge(recurrent_part_done, 1)
                pe.wait_ge(spatial_gate_applied, TL)
            for i in range(nt + 3):
                if i < nt:
                    if i >= 2:
                        pe.wait_ge(residual_added, r0 + i - 1)
                    pe.wait_ge(mixed_high_done, r0 + i + 1)
                    pe.wait_ge(mixed_low_done, r0 + i + 1)
                    for k in range(KC):
                        if i == 0 and k % 2 == 0:
                            pe.wait_ge(wout_high_done, 4 * l + k // 2 + 1)
                            pe.wait_ge(wout_low_done, 4 * l + k // 2 + 1)
                        for c in range(2):
                            o, cs = ps[:, 4 + 2 * (i % 2) + c, :], slice(c * BANK, (c + 1) * BANK)
                            xh, xl = cathi[i % 2][:, k, :], catlo[l][:, k, i * P:(i + 1) * P]
                            pe.matmul(o, xh, whi_out[:, k, cs], start=(k == 0), stop=False)
                            pe.matmul(o, xh, wlo_out[:, k, cs], start=False, stop=False)
                            ins = pe.matmul(o, xl, whi_out[:, k, cs], start=False, stop=(k == KC - 1))
                    ins.then_inc(projected, 1)
                if 1 <= i <= nt:
                    norm_transposes(pe, n0 + i - 1, 0, n0 + i - 2 if i > 1 else None)
                if 2 <= i <= nt + 1:
                    t = i - 2
                    pe.wait_ge(h_written_by_vector, n0 + t + 1)
                    pe.wait_ge(h_written_by_scalar, n0 + t + 1)
                    if t == 0:
                        pe.wait_ge(router_loaded, 16 * (l + 1))
                    else:
                        pe.wait_ge(logit_exps_done, r0 + t)
                    for k in range(KC):
                        ins = pe.matmul(ps[:, 2, 0:NE], hN[t % 2][:, k, :], router[:, k * NE:(k + 1) * NE],
                                        start=(k == 0), stop=(k == KC - 1))
                    ins.then_inc(logits_done, 1)
                if i >= 3:
                    t = i - 3
                    pe.wait_ge(affinities_done, r0 + t + 1)
                    if t >= 1:
                        pe.wait_ge(affinities_copied, r0 + t)
                    pe.transpose(ps[0:NE, 3, 0:P], sm[:, 32 * (t % 2):32 * (t % 2) + NE], ident[:, :]).then_inc(affinities_transposed, 1)
            ne = 64 + NE if l == 0 else 32 + NE
            if l == 0:
                pe_late_ada(pe)
            pe.wait_ge(ranked, l + 1)
            pe.transpose(ps[:, 2, 0:ne], tkg[0:ne, :], ident[0:ne, 0:ne])
            pe.transpose(ps[:, 3, 0:ne], tkf[0:ne, :], ident[0:ne, 0:ne]).then_inc(ranked_transposed, 1)

        def act_root(act, n):
            b = n % 2
            act.wait_ge(squares_summed, n + 1)
            nc.scalar.activation(st[:, 4 * b + 1:4 * b + 2], st[:, 4 * b:4 * b + 1], ACT.Sqrt,
                                 bias=epsc[:, 0:1], scale=1.0 / D).then_inc(root_taken, 1)

        def columns(l, w, k, t):
            c = 0 if t < TL else 1
            i = ((l * 2 + w) * KC + k) * 2 + c
            m = (l * 48 + (3 * w) * KC + k) * 2 + c
            return scg[:, i:i + 1], modc[:, m:m + 1]

        def act_blocks(act, n, l, w, t, bank):
            act.wait_ge(normed_transposed, n + 1)
            if w == 1 and t >= 2:
                act.wait_ge(logits_done, NT * l + t - 1)
            for k in range(KC // 2, KC):
                sc_, sh_ = columns(l, w, k, t)
                dst = hT[:, k, t * P:(t + 1) * P] if w == 0 else hN[t % 2][:, k, :]
                ins = nc.scalar.activation(dst, ps[:, bank + k // 4, (k % 4) * P:(k % 4 + 1) * P],
                                           ACT.Identity, bias=sh_, scale=sc_)
            ins.then_inc(h_written_by_scalar, 1)

        def dve_blocks(dve, n, l, w, t, bank):
            dve.wait_ge(normed_transposed, n + 1)
            if w == 1 and t >= 2:
                dve.wait_ge(logits_done, NT * l + t - 1)
            for k in range(KC // 2):
                sc_, sh_ = columns(l, w, k, t)
                dst = hT[:, k, t * P:(t + 1) * P] if w == 0 else hN[t % 2][:, k, :]
                ins = nc.vector.tensor_scalar(dst,
                                              ps[:, bank + k // 4, (k % 4) * P:(k % 4 + 1) * P], sc_, sh_,
                                              ALU.mult, ALU.add)
            ins.then_inc(h_written_by_vector, 1)

        def dve_norm(dve, own, n):
            b = n % 2
            dve.wait_ge(root_taken, n + 1)
            own.do(nc.vector.reciprocal(st[:, 4 * b + 2:4 * b + 3], st[:, 4 * b + 1:4 * b + 2]))
            if before_mixer(n) and n >= 2:
                dve.wait_ge(normed_transposed, n - 1)
            nc.vector.tensor_scalar(normed(n), XB[b], st[:, 4 * b + 2:4 * b + 3], None, ALU.mult).then_inc(tile_normed, 1)

        def dve_ada_rows(dve, a):
            dve.wait_ge(ada_unit_used, KC * (a + 1))
            if a >= 1:
                dve.wait_ge(ada_rows_transposed, a)
            if a == 0:
                dve.wait_ge(zeros_made, 2)
            for q in range(4):
                ins = nc.vector.tensor_copy(rowtmp[32 * q:32 * q + 2, :], ps[32 * q:32 * q + 2, 6, :])
            ins.then_inc(ada_rows_copied, 1)

        def dve_ada_columns(dve, a):
            l, g = divmod(a, 3)
            if a in LATE:
                dve.wait_ge(late_columns_copied, a - 3)
                columns_ = late_cols[a - 4]
            else:
                dve.wait_ge(ada_rows_transposed, a + 1)
                columns_ = ps[:, 7, :]
            m3 = modc[:, :].rearrange("p (m w) -> p m w", w=2)
            m0 = 48 * l + 16 * g
            for w in range(2):
                src = columns_.rearrange("p (j q r) -> p r q j", j=4, q=4)[:, w]
                ins = nc.vector.tensor_tensor(m3[:, m0:m0 + 16, w].rearrange("p (q j) -> p q j", q=4), src,
                                              adab[:, m0:m0 + 16].rearrange("p (q j) -> p q j", q=4), ALU.add)
            ins.then_inc(ada_columns_added, 1)
            dve.wait_ge(ada_columns_added, a + 1)
            if g in (0, 2):
                w_, blk, v0 = (0, 8, VEC["mix_g"]) if g == 0 else (1, 32, VEC["ffn_g"])
                s3 = scg[:, :].rearrange("p (m w) -> p m w", w=2)
                i0 = (l * 2 + w_) * KC
                for w in range(2):
                    ins = nc.vector.scalar_tensor_tensor(out=s3[:, i0:i0 + KC, w],
                                                         in0=m3[:, 48 * l + blk:48 * l + blk + KC, w], scalar=1.0,
                                                         in1=vcol[:, v0 + l * KC:v0 + (l + 1) * KC],
                                                         op0=ALU.add, op1=ALU.mult)
                ins.then_inc(scales_done, 1)

        def act_even_job(act, own, j):
            kind, b, n, who = jobs[j]
            act.wait_ge(job_done, j + 1)
            w = wide(j % 2, n)
            if kind == "lr":
                ins = nc.scalar.copy(lrT[0:32, :], w[0:32, :])
            elif kind == "k":
                ins = nc.scalar.copy(kT[:, b, :], w)
            elif kind == "q":
                ins = nc.scalar.mul(qT[:, b, :], w, DK ** -0.5)
            elif kind == "g":
                ins = nc.scalar.activation(cat[:, 4 + b, :], w, ACT.Silu)
            elif kind == "cg":
                if b >= 2:
                    act.wait_ge(conv_done, b - 1)
                ins = nc.scalar.copy(TMP[b % 2], w)
            ins.then_inc(job_emptied_by_scalar, 1)

        def act_decay(act, own, pd):
            t = TMP[2 + pd % 2]
            act.wait_ge(decay_abs_done, pd + 1)
            own.do(nc.scalar.activation(t, t, ACT.Exp, scale=-1.0))
            nc.scalar.activation(t, t, ACT.Ln, bias=1.0).then_inc(decay_log_done, 1)

        def dve_decay_in(dve, pd):
            j = job_at[("dec", pd, False)]
            dve.wait_ge(job_done, j + 1)
            nc.vector.tensor_scalar(BX[:, pd, :], wide(j % 2, T), vcol[:, VEC["decay_b"] + pd:VEC["decay_b"] + pd + 1],
                                    None, ALU.add).then_inc(job_emptied_by_vector, 1)
            dve.wait_ge(job_emptied_by_vector, emptied["dve"][j + 1])
            nc.vector.scalar_tensor_tensor(out=TMP[2 + pd % 2], in0=BX[:, pd, :], scalar=-1.0, in1=BX[:, pd, :],
                                           op0=ALU.mult, op1=ALU.max).then_inc(decay_abs_done, 1)

        def dve_decay_out(dve, own, pd):
            t, x = TMP[2 + pd % 2], BX[:, pd, :]
            dve.wait_ge(constants_made, N_CONST)
            dve.wait_ge(decay_log_done, pd + 1)
            own.do(nc.vector.scalar_tensor_tensor(out=t, in0=x, scalar=0.0, in1=t, op0=ALU.min, op1=ALU.subtract))
            if pd < 2:
                ins = nc.vector.tensor_tensor_scan(x, chunk0[:, :], t, 0.0, ALU.mult, ALU.add)
            else:
                ins = nc.vector.tensor_tensor_scan(BX[:, pd, ::-1], chunk0[:, :], t[:, ::-1], 0.0, ALU.mult, ALU.add)
            ins.then_inc(decays_summed, 1)

        def dve_even_job(dve, own, j):
            kind, b, n, who = jobs[j]
            dve.wait_ge(job_done, j + 1)
            w = wide(j % 2, n)
            if kind == "bg":
                dve.wait_ge(conv_done, b + 1)
                nc.vector.tensor_tensor(cat[:, b, :], cat[:, b, :], w, ALU.mult).then_inc(job_emptied_by_vector, 1)
                return
            p = TMP[b % 2]
            dve.wait_ge(job_emptied_by_scalar, emptied["act"][job_at[("cg", b, False)] + 1])
            nc.vector.tensor_tensor(p, p, w, ALU.mult).then_inc(job_emptied_by_vector, 1)
            dve.wait_ge(job_emptied_by_vector, emptied["dve"][j + 1])
            w0 = VEC["ev_conv_w"] + b
            tap = [vcol[:, w0 + 4 * i:w0 + 4 * i + 1] for i in range(3)]
            o = cat[:, b, :]
            own.do(nc.vector.tensor_scalar(o, p, tap[1], vcol[:, VEC["ev_conv_b"] + b:VEC["ev_conv_b"] + b + 1],
                                           ALU.mult, ALU.add))
            for src, dst in (((0, GRID - 1), (1, GRID)), ((1, GRID), (0, GRID - 1))):
                tp = tap[0] if dst[0] == 1 else tap[2]
                p3 = p[:, 0:LAT].rearrange("p (r x) -> p r x", x=GRID)[:, :, src[0]:src[1]]
                o3 = o[:, 0:LAT].rearrange("p (r x) -> p r x", x=GRID)[:, :, dst[0]:dst[1]]
                nc.vector.scalar_tensor_tensor(out=o3, in0=p3, scalar=tp, in1=o3, op0=ALU.mult, op1=ALU.add)
                s0, d0 = (0, 1) if dst[0] == 1 else (1, 0)
                pc, oc = p[:, LAT + s0:LAT + s0 + CTX - 1], o[:, LAT + d0:LAT + d0 + CTX - 1]
                ins = nc.vector.scalar_tensor_tensor(out=oc, in0=pc, scalar=tp, in1=oc, op0=ALU.mult, op1=ALU.add)
                own.mark(ins) if dst[0] != 1 else own.do(ins)
            dve.wait_ge(vector_own, own.n)
            dve.sem_inc(conv_done, 1)

        def act_exps(act, p):
            if p == 0:
                act.wait_ge(decays_summed, 4)
                act.wait_ge(conv_done, 4)
            else:
                act.wait_ge(keys_decayed, 1)
            for r in range(2):
                nc.scalar.activation(TMP[2 * r], BX[:, 2 * r + p, :], ACT.Exp, scale=1.0 / TAU)
                ins = nc.scalar.activation(TMP[2 * r + 1], BX[:, 2 * r + p, :], ACT.Exp, scale=-1.0 / TAU)
            ins.then_inc(decay_exps_done, 1)

        def dve_decayed(dve, own, p):
            dve.wait_ge(decay_exps_done, p + 1)
            if p == 0:
                dve.wait_ge(job_emptied_by_scalar, emptied["act"][n_even_jobs])
            for r in range(2):
                e3 = TMP[2 * r].rearrange("p (c i) -> p c i", i=CHUNK)
                i = (CHUNK - 1) * (1 - r)
                nc.vector.tensor_copy(dec[:, (2 * r + p) * NCH:(2 * r + p + 1) * NCH], e3[:, :, i])
                ins = nc.vector.tensor_tensor(BX[:, 2 * r + p, :], kT[:, p, :], TMP[2 * r + 1], ALU.mult)
            own.do(ins)
            own.do(nc.vector.tensor_tensor(kT[:, p, :], qT[:, p, :], TMP[2], ALU.mult))
            nc.vector.tensor_tensor(qT[:, p, :], qT[:, p, :], TMP[0], ALU.mult).then_inc(keys_decayed, 1)

        def act_gla(act, own):
            act_exps(act, 0)
            act_exps(act, 1)
            for p in range(2):
                for g in range(5):
                    n = 5 * p + g
                    act.wait_ge(keys_transposed, n + 1)
                    nc.scalar.copy(ktok[:, 2 * g:2 * g + 2, :, :].rearrange("p t r d -> p (t r d)"),
                                   ps[:, n % 2, :]).then_inc(key_tokens_copied, 1)
                for s in range(NCH - 1):
                    n = NCH * p + s
                    for r in range(2):
                        act.wait_ge(state_updated, 2 * n + r + 1)
                        c, c1 = order[r][s], order[r][s + 1]
                        i = (2 * r + p) * NCH + c
                        nc.scalar.activation(SIN[:, r, c1, :], TST[:, r, s % 2, :], ACT.Copy,
                                             scale=dec[:, i:i + 1]).then_inc(state_in_scaled, 1)

                def squares(g):
                    n = 5 * p + g
                    act.wait_ge(outputs_done, n + 1)
                    if n == 0:
                        act.wait_ge(keys_decayed, 2)
                    if n >= 2:
                        act.wait_ge(square_means_done, n - 1)
                    nc.scalar.activation(SQ[n % 2].rearrange("p (h t) -> p h t", h=2), ps[:, 6:8, 0:256],
                                         ACT.Square).then_inc(outputs_squared, 1)

                def reciprocal_roots(g):
                    n = 5 * p + g
                    act.wait_ge(square_means_done, n + 1)
                    if n >= 2:
                        act.wait_ge(outputs_scaled, n - 1)
                    own.do(nc.scalar.activation(RS[n % 2], ps[:, n % 2, :], ACT.Ln, bias=epsc[:, 0:1], scale=1.0 / P))
                    nc.scalar.activation(RS[n % 2], RS[n % 2], ACT.Exp, scale=-0.5).then_inc(recip_roots_done, 1)

                for g in range(5):
                    if g >= 1:
                        reciprocal_roots(g - 1)
                    squares(g)
                reciprocal_roots(4)

        def dve_gla(dve, own):
            dve_decayed(dve, own, 0)
            dve_decayed(dve, own, 1)
            dve.wait_ge(job_done, n_even_jobs)
            own.do(nc.vector.memset(R_H[:, 7680:9728], 0.0))
            for p in range(2):
                for s in range(NCH):
                    n = NCH * p + s
                    if s % 4 == 0:
                        dve.wait_ge(updates_done, (n // 4) + 1)
                    for r in range(2):
                        u = ps[:, 2 * (s // 4 % 2) + order[r][s] % 2, (s % 4) * P:(s % 4 + 1) * P]
                        if s >= 2:
                            dve.wait_ge(state_in_scaled, 38 * p + 2 * (s - 2) + r + 1)
                        elif p == 1 and s == 0 and r == 0:
                            dve.wait_ge(state_in_scaled, 38)
                        if s == 0:
                            ins = nc.vector.tensor_copy(TST[:, r, 0, :], u)
                        else:
                            i = (2 * r + p) * NCH + order[r][s - 1]
                            dve.wait_ge(state_updated, 2 * (n - 1) + r + 1)
                            ins = nc.vector.scalar_tensor_tensor(out=TST[:, r, s % 2, :], in0=TST[:, r, (s - 1) % 2, :],
                                                                 scalar=dec[:, i:i + 1], in1=u,
                                                                 op0=ALU.mult, op1=ALU.add)
                        ins.then_inc(state_updated, 1)

                def mask_scores(g):
                    n = 5 * p + g
                    dve.wait_ge(scores_done, n + 1)
                    if n >= 2:
                        dve.wait_ge(outputs_done, n - 1)
                    for r in range(2):
                        mask = (maskf, maskb)[r].bitcast(U32).unsqueeze(1).broadcast_to([P, 2, P])
                        for hh in range(2):
                            ins = nc.vector.copy_predicated(
                                attS[:, n % 2, r, 256 * hh:256 * (hh + 1)].rearrange("p (q i) -> p q i", q=2), mask,
                                ps[:, 4 + hh, 256 * r:256 * (r + 1)].rearrange("p (q i) -> p q i", q=2))
                    ins.then_inc(scores_masked, 1)

                def gated(g):
                    n = 5 * p + g
                    dve.wait_ge(outputs_squared, n + 1)
                    for hh in range(2):
                        h = 2 * p + hh
                        o = cat[:, 4 + h, g * 256:(g + 1) * 256]
                        ins = nc.vector.scalar_tensor_tensor(out=o, in0=ps[:, 6 + hh, 0:256],
                                                             scalar=vcol[:, VEC["ev_norm_g"] + h:VEC["ev_norm_g"] + h + 1],
                                                             in1=o, op0=ALU.mult, op1=ALU.mult)
                    ins.then_inc(outputs_gated, 1)

                def scaled(g):
                    n = 5 * p + g
                    dve.wait_ge(outputs_gated, n + 1)
                    dve.wait_ge(recip_roots_done, n + 1)
                    o = cat[:, 4 + 2 * p:6 + 2 * p, g * 256:(g + 1) * 256]
                    nc.vector.tensor_tensor(o, o, RS[n % 2].rearrange("p (h t) -> p h t", h=2), ALU.mult).then_inc(outputs_scaled, 1)

                mask_scores(0)
                for g in range(5):
                    if g < 4:
                        mask_scores(g + 1)
                    if g >= 1:
                        scaled(g - 1)
                    gated(g)
                scaled(4)

        def gate_rows(l):
            return [(0, 2, 0), (1, 2, 1), (2, 5, 0), (3, 5, 1)] if l == 0 else [(0, 2, 0), (2, 5, 0)]

        def dve_gates(dve, own, l, ne):
            if l == 1:
                dve.wait_ge(job_done, len(jobs))
                dve.wait_ge(v_tile_done, NT + TL)
            m3 = modc[:, :].rearrange("p (m w) -> p m w", w=2)
            for m, (_, blk, w) in enumerate(gate_rows(l)):
                n = (0 if l == 0 else 4) + m
                if n >= 2:
                    dve.wait_ge(gate_row_in_psum, n - 1)
                gate = m3[:, l * 48 + blk * KC:l * 48 + (blk + 1) * KC, w]
                nc.vector.tensor_tensor(diag[n % 2].rearrange("p (k n) -> p k n", k=KC),
                                        ident[:, :].unsqueeze(1).broadcast_to([P, KC, P]),
                                        gate.unsqueeze(2).broadcast_to([P, KC, P]), ALU.mult).then_inc(diagonal_made, 1)
            dve.wait_ge(gate_row_copied, 4 if l == 0 else 6)
            if l == 0:
                dve.wait_ge(outputs_done, 10)
            own.do(nc.vector.memset(affT[0:ne, :], -1.0))
            for c in range(4):
                if c == 2:
                    dve_tile_low(dve, l, 0)
                dve.wait_ge(wout_high_done, 4 * l + c + 1)
                nc.vector.tensor_tensor(wlo_out[:, 2 * c:2 * c + 2, :], wout[:, 2 * c:2 * c + 2, :],
                                        whi_out[:, 2 * c:2 * c + 2, :], ALU.subtract).then_inc(wout_low_done, 1)

        def act_weights_high(act, l, c):
            act.wait_ge(wout_loaded[c // 3], 16 * (l + 1))
            if c == 0:
                if l == 0:
                    act.wait_ge(outputs_done, 10)
                else:
                    act.wait_ge(job_done, len(jobs))
                    act.wait_ge(v_tile_done, NT + TL)
            nc.scalar.copy(whi_out[:, 2 * c:2 * c + 2, :], wout[:, 2 * c:2 * c + 2, :]).then_inc(wout_high_done, 1)

        def act_tile_high(act, l, i):
            src = (cat, cat1)[l]
            if i == 0:
                if l == 0:
                    act.wait_ge(outputs_scaled, 10)
                else:
                    act.wait_ge(recurrent_part_done, 1)
                    act.wait_ge(spatial_gate_applied, TL)
            if i >= 2:
                act.wait_ge(projected, NT * l + i - 1)
            nc.scalar.copy(cathi[i % 2], src[:, :, i * P:(i + 1) * P]).then_inc(mixed_high_done, 1)

        def dve_tile_low(dve, l, i):
            src = (cat, cat1)[l]
            dve.wait_ge(mixed_high_done, NT * l + i + 1)
            nc.vector.tensor_tensor(catlo[l][:, :, i * P:(i + 1) * P], src[:, :, i * P:(i + 1) * P], cathi[i % 2],
                                    ALU.subtract).then_inc(mixed_low_done, 1)

        def act_gates(act, l):
            for m, (row, _, _) in enumerate(gate_rows(l)):
                n = (0 if l == 0 else 4) + m
                if m < 2:
                    act_weights_high(act, l, m)
                act.wait_ge(gate_row_in_psum, n + 1)
                nc.scalar.copy(bc[:, row * D:(row + 1) * D],
                               ps[:, 2 * (n % 2):2 * (n % 2) + 2, :].rearrange("p b n -> p (b n)")).then_inc(gate_row_copied, 1)

        def dve_wout(dve, own, l):
            nt, n0, r0 = (NT, norm0["ffn0"], 0) if l == 0 else (TL, norm0["ffn1"], NT)
            ne = 64 + NE if l == 0 else 32 + NE
            dve_gates(dve, own, l, ne)
            for i in range(nt + 3):
                if i + 1 < nt:
                    dve_tile_low(dve, l, i + 1)
                if i < nt:
                    n = n0 + i
                    dve.wait_ge(projected, r0 + i + 1)
                    y = ps[:, 4 + 2 * (i % 2):6 + 2 * (i % 2), :].rearrange("p b n -> p (b n)")
                    row = 0 if i < TL else 1
                    own.do(nc.vector.tensor_tensor(y, y, bc[:, row * D:(row + 1) * D], ALU.mult))
                    dve.wait_ge(tile_loaded[n % 2], 16 * xl_count[n])
                    nc.vector.tensor_tensor(XB[n % 2], XB[n % 2], y, ALU.add).then_inc(residual_added, 1)
                if 1 <= i <= nt:
                    dve_blocks(dve, n0 + i - 1, l, 1, i - 1, 0)
                if 2 <= i <= nt + 1:
                    t, b = i - 2, 16 + 4 * (i % 2)
                    dve.wait_ge(logits_done, r0 + t + 1)
                    own.do(nc.vector.reduce_max(st[:, b:b + 1], ps[:, 2, 0:NE], AXX))
                    nc.vector.tensor_scalar(st[:, b + 1:b + 2], st[:, b:b + 1], -1.0, None, ALU.mult).then_inc(logit_max_done, 1)
                if i < nt:
                    dve_norm(dve, own, n0 + i)
                if 2 <= i <= nt + 1:
                    t, b, s0 = i - 2, 16 + 4 * (i % 2), 32 * (i % 2)
                    dve.wait_ge(logit_exps_done, r0 + t + 1)
                    own.do(nc.vector.reciprocal(st[:, b + 3:b + 4], st[:, b + 2:b + 3]))
                    nc.vector.tensor_scalar(sm[:, s0:s0 + NE], sm[:, s0:s0 + NE], st[:, b + 3:b + 4], None,
                                            ALU.mult).then_inc(affinities_done, 1)
                if i >= 3:
                    t = i - 3
                    dve.wait_ge(affinities_transposed, r0 + t + 1)
                    part, col = 32 * (t // (TL // 2)), (t % (TL // 2)) * P
                    nc.vector.tensor_copy(affT[part:part + NE, col:col + P], ps[0:NE, 3, 0:P]).then_inc(affinities_copied, 1)
            dve.wait_ge(affinities_copied, r0 + nt)
            a = affT[0:ne, :]
            for r in range(CAPL // 8):
                v8, i8 = tkv[0:ne, 8 * r:8 * r + 8], tki[0:ne, 8 * r:8 * r + 8]
                own.do(nc.vector.max(v8, a))
                nc.vector.max_index(i8, v8, a)
                own.do(nc.vector.match_replace(a, v8, a, -2.0))
            for dst, src in ((tkf, tki), (tkg, tkv)):
                own.do(nc.vector.tensor_copy(dst[0:ne, :], src[0:ne, :]))
                ins = nc.vector.tensor_copy(dst[32:32 + NE, :], src[32:32 + NE, ::-1])
            ins.then_inc(ranked, 1)
            dve.wait_ge(ranked_transposed, l + 1)
            v1, i1 = ps[:, 2, 0:NE], ps[:, 3, 0:NE]
            first, diff, v2, i2 = sm[:, 0:NE], sm[:, NE:2 * NE], sm[:, 2 * NE:3 * NE], sm[:, 3 * NE:4 * NE]
            nc.vector.tensor_copy(v2, ps[:, 2, 32:32 + NE])
            own.do(nc.vector.tensor_scalar(i2, ps[:, 3, 32:32 + NE], float(LAT // 2), None, ALU.add))
            nc.vector.tensor_tensor(gcolT[:, 0:NE], v2, v1, ALU.max)
            nc.vector.tensor_tensor(first, v2, v1, ALU.is_le)
            own.do(nc.vector.tensor_tensor(diff, i2, i1, ALU.subtract))
            own.do(nc.vector.tensor_tensor(diff, diff, first, ALU.mult))
            ins = nc.vector.tensor_tensor(icolT[:, 0:NE], i2, diff, ALU.subtract)
            if l == 0:
                nc.vector.tensor_scalar(icolT[0:CAPC, 32:48], ps[0:CAPC, 3, 64:64 + NE], float(LAT), None, ALU.add)
                ins = nc.vector.tensor_copy(gcolT[0:CAPC, 32:48], ps[0:CAPC, 2, 64:64 + NE])
            ins.then_inc(tokens_chosen, 1)
            if l == 0:
                for a in LATE:
                    dve_ada_columns(dve, a)

        def act_wout(act, own, l):
            nt, n0, r0 = (NT, norm0["ffn0"], 0) if l == 0 else (TL, norm0["ffn1"], NT)
            act_gates(act, l)
            act_tile_high(act, l, 0)
            act_weights_high(act, l, 2)
            act_weights_high(act, l, 3)
            for i in range(nt + 3):
                if i + 1 < nt:
                    act_tile_high(act, l, i + 1)
                if 1 <= i <= nt:
                    act_blocks(act, n0 + i - 1, l, 1, i - 1, 0)
                if i < nt:
                    n = n0 + i
                    act.wait_ge(residual_added, r0 + i + 1)
                    if i >= 1:
                        act.wait_ge(normed_stored, 16 * (r0 + i))
                    act_square(act, n)
                    act_root(act, n)
                if 2 <= i <= nt + 1:
                    t, b, s0 = i - 2, 16 + 4 * (i % 2), 32 * (i % 2)
                    act.wait_ge(logit_max_done, r0 + t + 1)
                    if t >= 2:
                        act.wait_ge(affinities_transposed, r0 + t - 1)
                    nc.scalar.activation(sm[:, s0:s0 + NE], ps[:, 2, 0:NE], ACT.Exp, bias=st[:, b + 1:b + 2],
                                         accum_out=st[:, b + 2:b + 3]).then_inc(logit_exps_done, 1)
            if l == 0:
                act_late_ada(act)

        def sp_wout(sp, l):
            nt, n0, r0 = (NT, norm0["ffn0"], 0) if l == 0 else (TL, norm0["ffn1"], NT)
            w = (I["ev_w_out"] if l == 0 else I["od_w_out"]).rearrange("l (k p) n -> (l p) k n", p=P)
            if l == 0:
                sp.wait_ge(job_done, n_even_jobs)
                sp.wait_ge(ada_unit_used, 4 * KC)
                sp.dma_start(wout[:, 0:6, :], w[:, 0:6, :]).then_inc(wout_loaded[0], 16)
                sp.wait_ge(keys_decayed, 2)
                sp.dma_start(wout[:, 6:8, :], w[:, 6:8, :]).then_inc(wout_loaded[1], 16)
                sp.wait_ge(outputs_scaled, 10)
            else:
                sp.wait_ge(job_done, len(jobs))
                sp.wait_ge(v_tile_done, NT + TL)
                sp.dma_start(wout[:, 0:6, :], w[:, 0:6, :]).then_inc(wout_loaded[0], 16)
                sp.wait_ge(lru_item_done, 8)
                sp.dma_start(wout[:, 6:8, :], w[:, 6:8, :]).then_inc(wout_loaded[1], 16)
            sl, sc_ = (x_rows, c_rows) if l == 0 else (xres, xres)
            if l == 1:
                sp.wait_ge(spatial_gate_applied, TL)
            for i in range(nt + 1):
                if i < nt:
                    n = n0 + i
                    if i >= 2:
                        sp.wait_ge(tile_stored[n % 2], 16 * xst_count[n - 2])
                        sp.wait_ge(tile_normed, n - 1)
                    elif l == 1:
                        sp.wait_ge(tile_normed, n0)
                    sp.dma_start(XB[n % 2], tok_tile(sl, sc_, i)).then_inc(tile_loaded[n % 2], 16)
                if i >= 1:
                    t, n = i - 1, n0 + i - 1
                    sp.wait_ge(residual_added, r0 + t + 1)
                    sp.dma_start(xres[t * P:(t + 1) * P, :], XB[n % 2]).then_inc(tile_stored[n % 2], 16)
                    sp.wait_ge(tile_normed, n + 1)
                    sp.dma_start(xnd[t * P:(t + 1) * P, :], XN).then_inc(normed_stored, 16)
                if 1 <= i <= 6:
                    load_first_unit(sp, l, i - 1)
                if i == 0:
                    sp.dma_start(router[:, :].rearrange("p (k e) -> p k e", e=NE),
                                 I["moe_router"][l].rearrange("(k p) e -> p k e", p=P)).then_inc(router_loaded, 16)

        def act_square(act, n):
            if not before_mixer(n):
                act.wait_ge(normed_transposed, n)
            squares = R_C[:, 3 * D:4 * D] if before_mixer(n) else XN
            nc.scalar.activation(squares, XB[n % 2], ACT.Square, accum_out=st[:, 4 * (n % 2):4 * (n % 2) + 1]).then_inc(squares_summed, 1)

        def first_unit(l, m, e, odd):
            if isinstance(e, int) and e == 0 and m < 2:
                return 12 * NE * l + 4 * m, 4 * m
            if isinstance(e, int) and e == NE - 1 and m == 2:
                return 12 * NE * (l + 1) - 4, 4
            return 12 * NE * l + 12 * e + (-4, 0, 16)[m], (0 if odd else 4, 4 if odd else 0, 4 if odd else 0)[m]

        def loads_before(l, m, e2, odd):
            if isinstance(e2, int) and e2 == 0 and not odd and m < 2:
                return 24 * l
            if isinstance(e2, int) and e2 == NE // 2 - 1 and odd and m == 2:
                return 24 * l + 23
            return 24 * l + 3 * e2 + (((-1, 0, 2), (1, 1, 3))[odd][m])

        def matrix_order(e2, odd, l):
            e = 2 * e2 + odd
            steps = [] if isinstance(e, int) and e == NE else [(0, e, e2, odd), (1, e, e2, odd)]
            if not (isinstance(e, int) and e == 0):
                steps.append((2, e - 1, e2 if odd else e2 - 1, 1 - odd))
            return steps

        def moe_steps(eng, step):
            step(0, 0)
            step(0, 1)
            with eng.Fori(1, NE // 2 - 1) as e2:
                step(e2, 0)
                step(e2, 1)
            step(NE // 2 - 1, 0)
            step(NE // 2 - 1, 1)

        def units_done(l, m, e):
            return first_unit(l, m, e, 0)[0] + 4

        def load_first_unit(sp, l, u):
            w = (I["moe_w_gate"], I["moe_w_up"])[u // 4].rearrange("l e (j k p) n -> (l e j) p k n", j=4, p=P)
            sp.dma_start(raw[u].rearrange("p (k n) -> p k n", k=2), w[4 * NE * l + u % 4]).then_inc(raw_slot_loaded[u], 16)

        def sp_moe(sp, l):
            n0 = NE * l
            w = [I[x].rearrange("l e (j k p) n -> (l e j) p k n", j=4, p=P)
                 for x in ("moe_w_gate", "moe_w_up", "moe_w_down")]

            def load(m, e, e2, odd):
                u, slot = first_unit(l, m, e, odd)
                for j in range(4):
                    if isinstance(u, int) and u + j < 12 * NE * l + 6:
                        continue
                    if isinstance(u, int) and u + j == 12 * NE * l + 6:
                        sp.wait_ge(logits_done, NT if l == 0 else NT + TL)
                    if not (isinstance(u, int) and u < 12 * NE * l + 8):
                        if l == 0:
                            sp.wait_ge(expert_unit_used, u + j - 7)
                        else:
                            sp.wait_ge(unit_low_done, u + j - 7)
                    src = w[m][(n0 + e) * 4 + j] if isinstance(e, int) else \
                        w[m][bass.ds((n0 + e) * 4 + j, 1)].rearrange("a p k n -> p (a k) n")
                    sp.dma_start(raw[slot + j].rearrange("p (k n) -> p k n", k=2), src).then_inc(raw_slot_loaded[slot + j], 16)

            if l == 1:
                sp.dma_start(bc[:, 3 * D:4 * D], I["norm_final_g"].partition_broadcast(P)).then_inc(final_gain_loaded, 16)

            def step(e2, odd):
                for m in matrix_order(e2, odd, l):
                    load(*m)

            moe_steps(sp, step)
            load(2, NE - 1, NE // 2 - 1, 1)

        def pe_moe(pe, l):
            n0 = NE * l
            C = CAPC if l == 0 else 0

            def unit(m, e, e2, odd, j, full, lo, hi, bank, cbank, context_free=lambda: None):
                u, slot = first_unit(l, m, e, odd)
                pe.wait_ge(unit_high_done, u + j + 1)
                pe.wait_ge(unit_low_done, u + j + 1)
                wh, wl = (x[j].rearrange("p (k n) -> p k n", k=2) for x in (whi, wlo))
                for kk in range(2):
                    k = 2 * j + kk
                    for c in range(2):
                        o, cs = ps[:, bank + c, :], slice(c * BANK, (c + 1) * BANK)
                        pe.matmul(o, hi[:, k, :], wh[:, kk, cs], start=(k == 0), stop=False)
                        pe.matmul(o, hi[:, k, :], wl[:, kk, cs], start=False, stop=False)
                        ins = pe.matmul(o, lo[:, k, 0:P], wh[:, kk, cs], start=False, stop=(k == KC - 1))
                if C:
                    w = raw[slot + j].rearrange("p (k n) -> p k n", k=2)
                    context_free()
                    for kk in range(2):
                        for c in range(2):
                            q = 2 * kk + c
                            ins = pe.matmul(ps[32 * q:32 * q + C, cbank, :], full[:, 2 * j + kk, P:P + C],
                                            w[:, kk, c * BANK:(c + 1) * BANK], start=(j == 0), stop=(j == 3))
                ins.then_inc(expert_unit_used, 1)

            def token_columns(n):
                pe.wait_ge(rows_gathered, (n + 1) * 16)
                for k in range(KC):
                    ins = pe.transpose(ps[:, 4 + k // 4, (k % 4) * P:(k % 4 + 1) * P], xg[:, k * P:(k + 1) * P],
                                       ident[:, :])
                if C:
                    pe.wait_ge(constants_made, 1)
                    pe.wait_ge(context_rows_gathered, (n + 1) * 16)
                    for k in range(KC):
                        ins = pe.transpose(ps[:, 7, k * C:(k + 1) * C], xgc[0:C, k * P:(k + 1) * P], ident[0:C, 0:C])
                ins.then_inc(rows_transposed, 1)

            def down(e, e2, odd, gate_read):
                pe.wait_ge(hidden_low_done, n0 + e + 1)
                for j in range(4):
                    unit(2, e, e2, odd, j, hidT, hidlo, hidh, 4, 6, gate_read if j == 0 else lambda: None)

            def step(e2, odd):
                e = 2 * e2 + odd
                n = n0 + e
                known = isinstance(e2, int)
                first, second, last = known and e == 0, known and e == 1, known and e == NE - 1
                x, xl, xh = xT[odd], xlo[odd], xhi[odd]
                pe.wait_ge(tokens_low_done, n + 1)
                if not first:
                    pe.wait_ge(silu_done, n)

                def down_read():
                    if not first and not second:
                        pe.wait_ge(context_down_half_copied, n - 1)
                        pe.wait_ge(context_down_summed, n - 1)

                def gate_read():
                    pe.wait_ge(context_gate_summed, n + 1)

                for j in range(4):
                    unit(0, e, e2, odd, j, x, xl, xh, 0, 6, down_read if j == 0 else lambda: None)
                    if j == 2 and not last:
                        if not first:
                            pe.wait_ge(hidden_low_done, n)
                            if not second:
                                pe.wait_ge(expert_rows_done, n - 1)
                        token_columns(n + 1)
                if not last:
                    pe.wait_ge(tokens_by_vector, n + 2)
                if not first:
                    pe.wait_ge(hidden_low_done, n)
                    if not second:
                        pe.wait_ge(expert_rows_done, n - 1)
                for j in range(4):
                    unit(1, e, e2, odd, j, x, xl, xh, 2, 7)
                if not first:
                    if not last:
                        pe.wait_ge(tokens_by_scalar, n + 2)
                    down(*matrix_order(e2, odd, l)[2][1:], gate_read)
                pe.wait_ge(hidden_done, n + 1)
                for k in range(KC):
                    ins = pe.transpose(ps[:, 2 + k // 4, (k % 4) * P:(k % 4 + 1) * P], hid[:, k * P:(k + 1) * P],
                                       ident[:, :])
                if C:
                    pe.wait_ge(constants_made, 1)
                    pe.wait_ge(context_hidden_done, n + 1)
                    for k in range(4):
                        ins = pe.transpose(ps[:, 7, k * 2 * C:(k + 1) * 2 * C], hidc[0:2 * C, k * P:(k + 1) * P],
                                           ident[0:2 * C, 0:2 * C])
                ins.then_inc(hidden_transposed, 1)

            if l == 0:
                pe.wait_ge(late_columns_copied, 2)
            token_columns(n0)
            moe_steps(pe, step)
            if C:
                pe.wait_ge(context_down_half_copied, n0 + NE - 1)
                pe.wait_ge(context_down_summed, n0 + NE - 1)
            pe.wait_ge(expert_rows_done, n0 + NE - 1)
            down(NE - 1, NE // 2 - 1, 1, lambda: None)

        def act_moe(act, l):
            n0 = NE * l
            C = CAPC if l == 0 else 0

            def high(m, e, e2, odd, j):
                u, slot = first_unit(l, m, e, odd)
                act.wait_ge(raw_slot_loaded[slot + j], 16 * (loads_before(l, m, e2, odd) + 1))
                if not (isinstance(u, int) and u + j < 4):
                    act.wait_ge(expert_unit_used, u + j - 3)
                nc.scalar.copy(whi[j], raw[slot + j]).then_inc(unit_high_done, 1)

            def token_columns(n, par):
                x = xT[par]
                act.wait_ge(rows_transposed, n + 1)
                for k in range(KC // 2, KC):
                    sc_, sh_ = columns(l, 1, k, 0)
                    ins = nc.scalar.activation(x[:, k, 0:P], ps[:, 5, (k % 4) * P:(k % 4 + 1) * P], ACT.Identity,
                                               bias=sh_, scale=sc_)
                ins.then_inc(tokens_by_scalar, 1)

            def token_high(n, par):
                act.wait_ge(tokens_by_scalar, n + 1)
                act.wait_ge(tokens_by_vector, n + 1)
                nc.scalar.copy(xhi[par], xT[par][:, :, 0:P]).then_inc(tokens_high_done, 1)

            def context_down(e):
                n = n0 + e
                act.wait_ge(expert_unit_used, units_done(l, 2, e))
                if not (isinstance(n, int) and n == 0):
                    act.wait_ge(context_expert_rows_done, n)
                for c in range(2):
                    ins = nc.scalar.copy(tmo[0:C, c * BANK:(c + 1) * BANK], ps[64 + 32 * c:64 + 32 * c + C, 6, :])
                ins.then_inc(context_down_half_copied, 1)

            def step(e2, odd):
                e = 2 * e2 + odd
                n = n0 + e
                known = isinstance(e2, int)
                first, last = known and e == 0, known and e == NE - 1
                order_ = matrix_order(e2, odd, l)
                up, down = order_[1], order_[2] if not first else None
                nxt = matrix_order(*((e2, 1) if odd == 0 else (e2 + 1, 0)), l)
                following = nxt[0]
                high(*order_[0], 3)
                high(*up, 0)
                high(*up, 1)
                if not last:
                    token_columns(n + 1, 1 - odd)
                high(*up, 2)
                act.wait_ge(expert_unit_used, units_done(l, 0, e))
                if not first:
                    act.wait_ge(hidden_done, n)
                nc.scalar.activation(sil, ps[:, 0:2, :].rearrange("p b n -> p (b n)"), ACT.Silu).then_inc(silu_done, 1)
                if C:
                    if not first:
                        act.wait_ge(context_hidden_done, n)
                    nc.scalar.copy(tmc[0:2 * C, :], ps[64:128, 6, :]).then_inc(context_gate_half_copied, 1)
                high(*up, 3)
                if not last:
                    token_high(n + 1, 1 - odd)
                if C:
                    act.wait_ge(context_gate_summed, n + 1)
                    nc.scalar.activation(silx[0:2 * C, :], silx[0:2 * C, :], ACT.Silu).then_inc(context_silu_done, 1)
                if not first:
                    for j in range(3):
                        high(*down, j)
                if C:
                    act.wait_ge(expert_unit_used, units_done(l, 1, e))
                    nc.scalar.copy(tmc[0:2 * C, :], ps[64:128, 7, :]).then_inc(context_up_half_copied, 1)
                if not first:
                    high(*down, 3)
                for j in range(2 if last else 3):
                    high(*following, j)
                if C and not first:
                    context_down(e - 1)
                act.wait_ge(hidden_transposed, n + 1)
                nc.scalar.copy(hidh, ps[:, 2:4, :].rearrange("p b (k t) -> p (b k) t", k=4)).then_inc(hidden_high_done, 1)
                if last:
                    high(*following, 2)

            if l == 0:
                act.wait_ge(tile_stored[0], 16 * (NT // 2))
            else:
                act.wait_ge(tile_stored[0], 16 * (NT // 2 + TL // 2))
            if l == 0:
                act.wait_ge(ada_unit_used, 6 * KC)
            act.wait_ge(logits_done, NT if l == 0 else NT + TL)
            for j in range(3):
                high(0, 0, 0, 0, j)
            token_columns(n0, 0)
            token_high(n0, 0)
            moe_steps(act, step)
            high(2, NE - 1, NE // 2 - 1, 1, 3)
            if C:
                context_down(NE - 1)

        def dve_moe(dve, l):
            n0 = NE * l
            C = CAPC if l == 0 else 0

            def low(m, e, e2, odd, j):
                u, slot = first_unit(l, m, e, odd)
                dve.wait_ge(unit_high_done, u + j + 1)
                nc.vector.tensor_tensor(wlo[j], raw[slot + j], whi[j], ALU.subtract).then_inc(unit_low_done, 1)

            def token_columns(n, par):
                x = xT[par]
                dve.wait_ge(rows_transposed, n + 1)
                for k in range(KC // 2):
                    sc_, sh_ = columns(l, 1, k, 0)
                    ins = nc.vector.tensor_scalar(x[:, k, 0:P], ps[:, 4, (k % 4) * P:(k % 4 + 1) * P], sc_, sh_,
                                                  ALU.mult, ALU.add)
                for k in range(KC if C else 0):
                    sc_, sh_ = columns(l, 1, k, TL)
                    ins = nc.vector.tensor_scalar(x[:, k, P:P + C], ps[:, 7, k * C:(k + 1) * C], sc_, sh_,
                                                  ALU.mult, ALU.add)
                ins.then_inc(tokens_by_vector, 1)

            def token_low(n, par):
                dve.wait_ge(tokens_high_done, n + 1)
                x = xT[par][:, :, 0:P]
                nc.vector.tensor_tensor(xlo[par][:, :, 0:P], x, xhi[par], ALU.subtract).then_inc(tokens_low_done, 1)

            def result(e):
                n = n0 + e
                first = isinstance(e, int) and e == 0
                dve.wait_ge(expert_unit_used, units_done(l, 2, e))
                if C:
                    dve.wait_ge(context_down_half_copied, n + 1)
                    for c in range(2):
                        o = tmo[0:C, c * BANK:(c + 1) * BANK]
                        ins = nc.vector.tensor_tensor(o, o, ps[32 * c:32 * c + C, 6, :], ALU.add)
                    ins.then_inc(context_down_summed, 1)
                if not first:
                    dve.wait_ge(rows_scattered, n * 16)
                nc.vector.scalar_tensor_tensor(out=eout, in0=ps[:, 4:6, :].rearrange("p b n -> p (b n)"),
                                               scalar=gcolT[:, bass.ds(e, 1)], in1=bc[:, 2 * D:3 * D],
                                               op0=ALU.mult, op1=ALU.mult).then_inc(expert_rows_done, 1)
                if C:
                    dve.wait_ge(context_down_summed, n + 1)
                    if not first:
                        dve.wait_ge(context_rows_scattered, n * 16)
                    nc.vector.scalar_tensor_tensor(out=outc[0:C, :], in0=tmo[0:C, :],
                                                   scalar=gcolT[0:C, bass.ds(e + 32, 1)], in1=bc[0:C, 3 * D:4 * D],
                                                   op0=ALU.mult, op1=ALU.mult).then_inc(context_expert_rows_done, 1)

            def step(e2, odd):
                e = 2 * e2 + odd
                n = n0 + e
                known = isinstance(e2, int)
                first, last = known and e == 0, known and e == NE - 1
                order_ = matrix_order(e2, odd, l)
                up, down = order_[1], order_[2] if not first else None
                following = matrix_order(*((e2, 1) if odd == 0 else (e2 + 1, 0)), l)[0]
                low(*order_[0], 3)
                low(*up, 0)
                low(*up, 1)
                if not last:
                    token_columns(n + 1, 1 - odd)
                low(*up, 2)
                low(*up, 3)
                if C:
                    dve.wait_ge(context_gate_half_copied, n + 1)
                    nc.vector.tensor_tensor(silx[0:2 * C, :], tmc[0:2 * C, :], ps[0:2 * C, 6, :], ALU.add).then_inc(context_gate_summed, 1)
                if not last:
                    token_low(n + 1, 1 - odd)
                if not first:
                    for j in range(3):
                        low(*down, j)
                dve.wait_ge(expert_unit_used, units_done(l, 1, e))
                dve.wait_ge(silu_done, n + 1)
                if not first:
                    dve.wait_ge(hidden_transposed, n)
                nc.vector.tensor_tensor(hid, sil, ps[:, 2:4, :].rearrange("p b n -> p (b n)"), ALU.mult).then_inc(hidden_done, 1)
                if C:
                    dve.wait_ge(context_up_half_copied, n + 1)
                    nc.vector.tensor_tensor(tmc[0:2 * C, :], tmc[0:2 * C, :], ps[0:2 * C, 7, :], ALU.add).then_inc(context_up_summed, 1)
                    dve.wait_ge(context_up_summed, n + 1)
                    dve.wait_ge(context_silu_done, n + 1)
                    nc.vector.tensor_tensor(hidc[0:2 * C, :], tmc[0:2 * C, :], silx[0:2 * C, :], ALU.mult).then_inc(context_hidden_done, 1)
                if not first:
                    low(*down, 3)
                for j in range(2 if last else 3):
                    low(*following, j)
                if not first:
                    result(e - 1)
                dve.wait_ge(hidden_high_done, n + 1)
                ins = nc.vector.tensor_tensor(hidlo[:, :, 0:P],
                                              ps[:, 2:4, :].rearrange("p b (k t) -> p (b k) t", k=4), hidh, ALU.subtract)
                if C:
                    src = ps[:, 7, 0:8 * C].rearrange("p (k h t) -> p h k t", k=4, h=2)
                    for h in range(2):
                        ins = nc.vector.tensor_copy(hidT[:, 4 * h:4 * h + 4, P:P + C], src[:, h])
                ins.then_inc(hidden_low_done, 1)
                if last:
                    low(*following, 2)

            if l == 0:
                dve.wait_ge(tile_stored[1], 16 * (NT // 2))
                dve.wait_ge(normed_stored, 16 * NT)
            else:
                dve.wait_ge(tile_stored[1], 16 * (NT // 2 + TL // 2))
                dve.wait_ge(normed_stored, 16 * (NT + TL))
            low(0, 0, 0, 0, 0)
            low(0, 0, 0, 0, 1)
            token_columns(n0, 0)
            token_low(n0, 0)
            low(0, 0, 0, 0, 2)
            moe_steps(dve, step)
            low(2, NE - 1, NE // 2 - 1, 1, 3)
            result(NE - 1)

        def pool_moe(pool, l):
            n0 = NE * l
            C = CAPC if l == 0 else 0

            def gather(count, first):
                n, e = count - 1, count - 1 - n0
                if not first:
                    pool.wait_ge(rows_gathered, n * 16)
                    pool.wait_ge(rows_transposed, n)
                pool.tensor_copy(gidx[:, 0:1], icolT[:, bass.ds(e, 1)]).then_inc(gather_index_set, 1)
                if C:
                    if not first:
                        pool.wait_ge(context_rows_gathered, n * 16)
                    pool.tensor_copy(gidx[0:C, 1:2], icolT[0:C, bass.ds(e + 32, 1)]).then_inc(context_gather_index_set, 1)
                pool.wait_ge(tokens_chosen, l + 1)
                pool.wait_ge(gather_index_set, count)
                pool.indirect_dma_start(out=xg, out_offset=None, in_=xnd,
                                        in_offset=bass.IndirectOffsetOnAxis(ap=gidx[:, 0:1], axis=0)).then_inc(rows_gathered, 16)
                if C:
                    pool.wait_ge(tokens_chosen, l + 1)
                    pool.wait_ge(context_gather_index_set, count)
                    pool.indirect_dma_start(out=xgc[0:C, :], out_offset=None, in_=xnd,
                                            in_offset=bass.IndirectOffsetOnAxis(ap=gidx[0:C, 1:2], axis=0)).then_inc(context_rows_gathered, 16)

            def scatter(count, first):
                n, e = count - 1, count - 1 - n0
                pool.wait_ge(expert_rows_done, count)
                if not first:
                    pool.wait_ge(rows_scattered, n * 16)
                    if C:
                        pool.wait_ge(context_rows_scattered, n * 16)
                pool.tensor_copy(gidx[:, 2:3], icolT[:, bass.ds(e, 1)]).then_inc(scatter_index_set, 1)
                if C:
                    pool.tensor_copy(gidx[0:C, 3:4], icolT[0:C, bass.ds(e + 32, 1)]).then_inc(context_scatter_index_set, 1)
                pool.wait_ge(tokens_chosen, l + 1)
                pool.wait_ge(scatter_index_set, count)
                pool.indirect_dma_start(out=xres, out_offset=bass.IndirectOffsetOnAxis(ap=gidx[:, 2:3], axis=0),
                                        in_=eout, in_offset=None, compute_op=ALU.add).then_inc(rows_scattered, 16)
                if C:
                    pool.wait_ge(tokens_chosen, l + 1)
                    pool.wait_ge(context_scatter_index_set, count)
                    pool.wait_ge(context_expert_rows_done, count)
                    pool.indirect_dma_start(out=xres, out_offset=bass.IndirectOffsetOnAxis(ap=gidx[0:C, 3:4], axis=0),
                                            in_=outc[0:C, :], in_offset=None, compute_op=ALU.add).then_inc(context_rows_scattered, 16)

            pool.wait_ge(tokens_chosen, l + 1)
            pool.wait_ge(normed_stored, 16 * (NT if l == 0 else NT + TL))
            for b in range(2):
                pool.wait_ge(tile_stored[b], 16 * (NT // 2 if l == 0 else NT // 2 + TL // 2))
            gather(n0 + 1, True)
            gather(n0 + 2, False)
            gather(n0 + 3, False)
            gather(n0 + 4, False)
            scatter(n0 + 1, True)
            with pool.Fori(n0 + 5, n0 + NE + 1) as count:
                gather(count, False)
                scatter(count - 3, False)
            scatter(n0 + NE - 2, False)
            scatter(n0 + NE - 1, False)
            scatter(n0 + NE, False)

        def sp_final(sp):
            sp.wait_ge(rows_scattered, 16 * 2 * NE)
            sp.wait_ge(expert_rows_done, 2 * NE)
            for t in range(TL):
                sp.dma_start(FB[t], xres[t * P:(t + 1) * P, :]).then_inc(final_tile_loaded[t], 16)
            for t in range(TL):
                sp.wait_ge(final_tile_done, t + 1)
                sp.dma_start(out.rearrange("b t d -> (b t) d")[t * P:(t + 1) * P, :], FB[t]).then_inc(final_tile_stored, 16)
            sp.wait_ge(final_tile_stored, 16 * TL)
            for b in range(2):
                sp.wait_ge(tile_stored[b], 16 * max(xst_count[n] for n in xst_count if n % 2 == b))

        def act_final(act):
            n0 = norm0["final"]
            act.wait_ge(rows_scattered, 16 * 2 * NE)
            for t in range(TL):
                q = 32 + 4 * t
                act.wait_ge(final_tile_loaded[t], 16)
                nc.scalar.activation(XN, FB[t], ACT.Square, accum_out=st[:, q:q + 1]).then_inc(squares_summed, 1)
                act.wait_ge(squares_summed, n0 + t + 1)
                nc.scalar.activation(st[:, q + 1:q + 2], st[:, q:q + 1], ACT.Sqrt, bias=epsc[:, 0:1],
                                     scale=1.0 / D).then_inc(root_taken, 1)

        def dve_final(dve, own):
            dve.wait_ge(final_gain_loaded, 16)
            for t in range(TL):
                q = 32 + 4 * t
                dve.wait_ge(root_taken, norm0["final"] + t + 1)
                own.do(nc.vector.reciprocal(st[:, q + 2:q + 3], st[:, q + 1:q + 2]))
                nc.vector.scalar_tensor_tensor(out=FB[t], in0=FB[t], scalar=st[:, q + 2:q + 3], in1=bc[:, 3 * D:4 * D],
                                               op0=ALU.mult, op1=ALU.mult).then_inc(final_tile_done, 1)

        def pe_odd(pe):
            n0 = norm0["mix1"]
            for t in range(NT):
                norm_transposes(pe, n0 + t, 2 * (t % 2), n0 + t - 2 if t >= 2 else None)
            pe.wait_ge(odd_weights_loaded, 64)
            for g in range(4):
                ins = pe.transpose(ps[:, 7, g * P:(g + 1) * P], sgw[:, g, :], ident[:, :])
            ins.then_inc(spatial_weights_transposed, 1)
            pe.wait_ge(h_written_by_vector, n0 + NT)
            pe.wait_ge(h_written_by_scalar, n0 + NT)
            j = n_even_jobs
            for kind, b in odd_order:
                if kind in ("ga", "gx"):
                    c, d = b // 2, b % 2
                    banks_free(pe, j)
                    pe.wait_ge(odd_conv_done, c + 1)
                    m = (8 if kind == "gx" else 0) + 4 * d + c
                    for c0, cn in SPLIT:
                        ins = pe.matmul(wide(j % 2, T)[:, c0:c0 + cn], gatew[:, m, :], XC[:, c, c0:c0 + cn],
                                        start=True, stop=True)
                    ins.then_inc(job_done, 1)
                    j += 1
                elif kind == "v":
                    if b == 0:
                        pe.wait_ge(spatial_weights_copied, 1)
                        unit_in(pe, index[("w0",)])
                        unit_in(pe, index[("w1",)])
                    if b >= 2:
                        pe.wait_ge(v_gelu_done, b - 1)
                    v_tile(pe, b, index[("w0",)])
                else:
                    job(pe, j, index[(f"{kind}{b // 2}",)], b % 2)
                    j += 1
            pe.wait_ge(v_normed, TL)
            for t in range(TL):
                if t >= 2:
                    pe.wait_ge(spatial_gate_applied, t - 1)
                for g in range(4):
                    ins = pe.matmul(ps[:, 6 + t % 2, g * P:(g + 1) * P], vln[:, t, g * P:(g + 1) * P], sgwT[:, g, :],
                                    start=True, stop=True)
                ins.then_inc(spatial_mixed, 1)

        groups = {0: (0, 3), 1: (3, 6), 2: (6, 8)}

        def act_odd(act, own):
            n0 = norm0["mix1"]
            for t in range(NT + 1):
                if t < NT:
                    n = n0 + t
                    act.wait_ge(tile_loaded[n % 2], 16 * xl_count[n])
                    act_square(act, n)
                    act_root(act, n)
                if t >= 1:
                    act_blocks(act, n0 + t - 1, 1, 0, t - 1, 2 * ((t - 1) % 2))
            act.wait_ge(spatial_weights_transposed, 1)
            nc.scalar.copy(sgwT.rearrange("p g n -> p (g n)"), ps[:, 7, :]).then_inc(spatial_weights_copied, 1)
            j = n_even_jobs
            for kind, b in odd_order:
                if kind == "v":
                    act.wait_ge(v_tile_done, NT + b + 1)
                    nc.scalar.activation(vln[:, b, :], ps[:, 6 + b % 2, :], ACT.Gelu_apprx_tanh).then_inc(v_gelu_done, 1)
                    for i, (a, z) in groups.items():
                        if b == z - 1:
                            act.wait_ge(v_statistics_done, i + 1)
                            nc.scalar.activation(vsd[:, a:z], vmv[:, :].rearrange("p (t m) -> p t m", m=2)[:, a:z, 1],
                                                 ACT.Sqrt, bias=epsc[:, 0:1]).then_inc(v_deviation_done, 1)
                    continue
                act.wait_ge(job_done, j + 1)
                w = wide(j % 2, jobs[j][2])
                if kind == "xb":
                    nc.scalar.copy(TMP[b], w).then_inc(job_emptied_by_scalar, 1)
                elif kind in ("gb", "u"):
                    nc.scalar.activation(cat1[:, b + (4 if kind == "u" else 0), :], w, ACT.Gelu_apprx_tanh).then_inc(job_emptied_by_scalar, 1)
                else:
                    c, d = b // 2, b % 2
                    x = 1 if kind == "gx" else 0
                    v0 = VEC["gate_x_b" if x else "gate_a_b"] + 4 * d + c
                    if b >= 1:
                        act.wait_ge(lru_item_done, b)
                    else:
                        act.wait_ge(odd_conv_done, 4)
                    nc.scalar.activation(TMP[x], w, ACT.Sigmoid, bias=vcol[:, v0:v0 + 1]).then_inc(job_emptied_by_scalar, 1)
                    if x:
                        m = 4 * d + c
                        act.wait_ge(job_emptied_by_scalar, emptied["act"][j + 1])
                        act.wait_ge(lru_constants_done, 1)
                        nc.scalar.activation(TMP[2], TMP[0], ACT.Tanh, scale=lruc[:, m:m + 1])
                        nc.scalar.activation(TMP[0], TMP[0], ACT.Exp, scale=lruc[:, 16 + m:17 + m]).then_inc(lru_a_done, 1)
                        act.wait_ge(lru_square_done, b + 1)
                        nc.scalar.activation(TMP[2], TMP[2], ACT.Sqrt).then_inc(lru_root_done, 1)
                j += 1

        def dve_odd(dve, own):
            n0 = norm0["mix1"]
            for t in range(NT + 1):
                if t < NT:
                    dve_norm(dve, own, n0 + t)
                if t >= 1:
                    dve_blocks(dve, n0 + t - 1, 1, 0, t - 1, 2 * ((t - 1) % 2))
            j = n_even_jobs
            for kind, b in odd_order:
                if kind == "v":
                    for i, (a, z) in groups.items():
                        if b == z - 1:
                            for t in range(a, z):
                                dve.wait_ge(v_gelu_done, t + 1)
                                ins = nc.vector.bn_stats(vst[:, 6 * t:6 * t + 6], vln[:, t, :])
                            own.do(ins)
                            for t in range(a, z):
                                ins = nc.vector.bn_aggr(vmv[:, 2 * t:2 * t + 2], vst[:, 6 * t:6 * t + 6])
                            ins.then_inc(v_statistics_done, 1)
                            dve.wait_ge(v_deviation_done, i + 1)
                            own.do(nc.vector.reciprocal(vsd[:, 8 + a:8 + z], vsd[:, a:z]))
                            for t in range(a, z):
                                nc.vector.tensor_scalar(vln[:, t, :], vln[:, t, :], vmv[:, 2 * t:2 * t + 1],
                                                        vsd[:, 8 + t:9 + t], ALU.subtract, ALU.mult).then_inc(v_normed, 1)
                    continue
                if kind == "xb":
                    dve.wait_ge(job_emptied_by_scalar, emptied["act"][j + 1])
                    w0 = VEC["od_conv_w"] + b
                    tap = [vcol[:, w0 + 4 * i:w0 + 4 * i + 1] for i in range(4)]
                    own.do(nc.vector.tensor_scalar(XC[:, b, :], TMP[b], tap[2],
                                                   vcol[:, VEC["od_conv_b"] + b:VEC["od_conv_b"] + b + 1],
                                                   ALU.mult, ALU.add))
                    for i, off in ((0, -2), (1, -1), (3, 1)):
                        for s0, sn in ((0, LAT), (LAT, CTX)):
                            d0, x0 = (s0 - off, s0) if off < 0 else (s0, s0 + off)
                            ln = sn - abs(off)
                            ins = nc.vector.scalar_tensor_tensor(out=XC[:, b, d0:d0 + ln], in0=TMP[b][:, x0:x0 + ln],
                                                                 scalar=tap[i], in1=XC[:, b, d0:d0 + ln],
                                                                 op0=ALU.mult, op1=ALU.add)
                        if i < 3:
                            own.do(ins)
                        else:
                            ins.then_inc(odd_conv_done, 1)
                elif kind == "gx":
                    c, d = b // 2, b % 2
                    dve.wait_ge(job_emptied_by_scalar, emptied["act"][j + 1])
                    nc.vector.tensor_tensor(TMP[1], TMP[1], XC[:, c, :], ALU.mult)
                    dve.wait_ge(lru_a_done, b + 1)
                    own.do(nc.vector.tensor_tensor(TMP[3], TMP[0], TMP[0], ALU.mult))
                    own.do(nc.vector.scalar_tensor_tensor(out=TMP[2], in0=TMP[3], scalar=1.0, in1=TMP[2],
                                                          op0=ALU.add, op1=ALU.mult))
                    nc.vector.tensor_scalar(TMP[2], TMP[2], 2e-35, None, ALU.max).then_inc(lru_square_done, 1)
                    dve.wait_ge(lru_root_done, b + 1)
                    own.do(nc.vector.tensor_tensor(TMP[1], TMP[1], TMP[2], ALU.mult))
                    h = TMP[3]
                    if d == 0:
                        own.do(nc.vector.tensor_tensor_scan(h[:, LAT:T], TMP[0][:, LAT:T], TMP[1][:, LAT:T], 0.0,
                                                            ALU.mult, ALU.add))
                        nc.vector.tensor_tensor_scan(HL[:, c, :], TMP[0][:, 0:LAT], TMP[1][:, 0:LAT], h[:, T - 1:T],
                                                     ALU.mult, ALU.add).then_inc(lru_item_done, 1)
                    else:
                        rev = slice(None, None, -1)
                        own.do(nc.vector.tensor_tensor_scan(h[:, LAT:T][:, rev], TMP[0][:, LAT:T][:, rev],
                                                            TMP[1][:, LAT:T][:, rev], 0.0, ALU.mult, ALU.add))
                        own.do(nc.vector.tensor_tensor_scan(h[:, 0:LAT][:, rev], TMP[0][:, 0:LAT][:, rev],
                                                            TMP[1][:, 0:LAT][:, rev], h[:, LAT:LAT + 1],
                                                            ALU.mult, ALU.add))
                        nc.vector.tensor_tensor(HL[:, c, :], HL[:, c, :], h[:, 0:LAT], ALU.add).then_inc(lru_item_done, 1)
                j += 1
            dve.wait_ge(lru_item_done, 8)
            dve.wait_ge(job_emptied_by_scalar, emptied["act"][len(jobs)])
            for c in range(4):
                ins = nc.vector.tensor_tensor(cat1[:, c, :], cat1[:, c, :], HL[:, c, :], ALU.mult)
            ins.then_inc(recurrent_part_done, 1)
            for t in range(TL):
                dve.wait_ge(spatial_mixed, t + 1)
                for g in range(4):
                    o = ps[:, 6 + t % 2, g * P:(g + 1) * P]
                    v0 = VEC["sg_norm_g"] + g
                    ins = nc.vector.scalar_tensor_tensor(out=o, in0=o, scalar=vcol[:, v0:v0 + 1], in1=sgb[:, g, :],
                                                         op0=ALU.mult, op1=ALU.add)
                own.do(ins)
                o = cat1[:, 4:8, t * P:(t + 1) * P]
                nc.vector.tensor_tensor(o, o, ps[:, 6 + t % 2, :].rearrange("p (g t) -> p g t", g=4),
                                        ALU.mult).then_inc(spatial_gate_applied, 1)

        @block.gpsimd
        def _(pool):
            own = Chain(pool, pool_own)
            own.do(pool.memset(ident[:, :], 0.0))
            pool.affine_select(out=ident[:, :], in_=ident[:, :], compare_op=ALU.not_equal, fill=1.0, base=0,
                               pattern=[[-1, P]], channel_multiplier=1).then_inc(constants_made, 1)
            pool.memset(decup[0:32, :], 0.0).then_inc(zeros_made, 1)
            pool.memset(rowtmp, 0.0).then_inc(zeros_made, 1)
            own.do(pool.memset(maskf[:, :], 1.0))
            own.do(pool.memset(maskb[:, :], 1.0))
            own.do(pool.memset(chunk0[:, :], 1.0))
            pool.memset(epsc[:, :], EPS)
            pool.memset(ones[:, :], 1.0).then_inc(constants_made, 1)
            own.do(pool.affine_select(out=maskf, in_=maskf, compare_op=ALU.is_ge, fill=0.0, base=0,
                                      pattern=[[1, P]], channel_multiplier=-1))
            pool.affine_select(out=maskf[:, CHUNK:P], in_=maskf[:, CHUNK:P], compare_op=ALU.is_ge, fill=0.0,
                               base=-CHUNK, pattern=[[0, CHUNK]], channel_multiplier=1).then_inc(constants_made, 1)
            own.do(pool.affine_select(out=maskb, in_=maskb, compare_op=ALU.is_ge, fill=0.0, base=0,
                                      pattern=[[-1, P]], channel_multiplier=1))
            pool.affine_select(out=maskb[:, 0:CHUNK], in_=maskb[:, 0:CHUNK], compare_op=ALU.is_ge, fill=0.0,
                               base=CHUNK - 1, pattern=[[0, CHUNK]], channel_multiplier=-1).then_inc(constants_made, 1)
            pool.memset(chunk0[:, :].rearrange("p (c i) -> p c i", i=CHUNK)[:, :, 0:1], 0.0).then_inc(constants_made, 1)
            pool_moe(pool, 0)
            pool_moe(pool, 1)

        @block.sync
        def _(sp):
            def load_unit(i):
                if before[i] is not None:
                    sp.wait_ge(*used_when[before[i]])
                dst = ring[slot_of[i]]
                if stream[i][0][0] != "ada":
                    dst = dst.rearrange("p (k n) -> p k n", k=KC)
                sp.dma_start(dst, stream[i][1]).then_inc(unit_loaded[slot_of[i]], 16)

            def load_x(n, t, src_lat, src_ctx):
                if n >= 2:
                    sp.wait_ge(tile_normed, n - 1)
                sp.dma_start(XB[n % 2], tok_tile(src_lat, src_ctx, t)).then_inc(tile_loaded[n % 2], 16)

            for i in range(3):
                load_unit(i)
            for name, src, rows in small:
                sp.dma_start(vrow[VEC[name]:VEC[name] + rows, :],
                             flat(src).rearrange("(r n) -> r n", n=P)).then_inc(small_vectors_loaded, 16)
            sp.dma_start(adab_row[0:96, :], flat(I["ada_b"]).rearrange("(r n) -> r n", n=P)).then_inc(small_vectors_loaded, 16)
            for i in range(3, 8):
                load_unit(i)
            load_x(0, 0, x_rows, c_rows)
            load_x(1, 1, x_rows, c_rows)
            sp.dma_start(wlr[:, :].rearrange("p (k n) -> p k n", k=KC), ev_in[:, :, E_LR:E_LR + 2 * RANK]).then_inc(lowrank_weights_loaded, 16)
            sp.wait_ge(zeros_made, 1)
            for d in range(2):
                sp.dma_start(decup[RANK * d:RANK * (d + 1), 256 * d:256 * (d + 1)], I["ev_decay_up"][0, d]).then_inc(lowrank_weights_loaded, 16)
            for t in range(2, NT):
                load_x(t, t, x_rows, c_rows)
            for i in range(8, n_even):
                load_unit(i)
            sp_wout(sp, 0)
            sp.wait_ge(projected, NT)
            for i in range(n_even, n_late):
                load_unit(i)
            sp_moe(sp, 0)
            sp.wait_ge(expert_unit_used, 12 * NE)
            for i in range(n_late, n_late + 3):
                if i != index[("w0",)]:
                    load_unit(i)
            sp.wait_ge(rows_scattered, 16 * NE)
            sp.wait_ge(context_rows_scattered, 16 * NE)
            for t in range(4):
                load_x(norm0["mix1"] + t, t, xres, xres[LAT:T, :])
            sp.dma_start(gatew[:, 0:8, :], I["od_gate_a_w"].rearrange("l d h i j -> i (l d h) j")).then_inc(odd_weights_loaded, 16)
            sp.dma_start(gatew[:, 8:16, :], I["od_gate_x_w"].rearrange("l d h i j -> i (l d h) j")).then_inc(odd_weights_loaded, 16)
            sp.dma_start(sgw, I["od_sg_w"].rearrange("l g i j -> i (l g) j")).then_inc(odd_weights_loaded, 16)
            sp.dma_start(sgb, I["od_sg_b"].rearrange("l g i -> (l g) i").partition_broadcast(P)).then_inc(odd_weights_loaded, 16)
            for t in range(4, NT):
                load_x(norm0["mix1"] + t, t, xres, xres[LAT:T, :])
            for i in range(n_late + 2, len(stream)):
                load_unit(i)
            sp_wout(sp, 1)
            sp_moe(sp, 1)
            sp_final(sp)
        @block.tensor
        def _(pe):
            pe_start(pe)
            pe_even(pe)
            pe_gla(pe)
            pe_wout(pe, 0)
            pe_moe(pe, 0)
            pe_odd(pe)
            pe_wout(pe, 1)
            pe_moe(pe, 1)

        @block.scalar
        def _(act):
            own = Chain(act, scalar_own)
            act.wait_ge(vectors_copied, 1)
            s3 = silc[:, :].rearrange("p (k w) -> p k w", w=2)
            for w, name in enumerate(("c", "c_ctx")):
                nc.scalar.activation(s3[:, :, w], vcol[:, VEC[name]:VEC[name] + KC], ACT.Silu).then_inc(cond_silu_done, 1)
            act.wait_ge(lambda_abs_done, 1)
            own.do(nc.scalar.activation(lruc[:, 8:16], lruc[:, 8:16], ACT.Exp, scale=-1.0))
            nc.scalar.activation(lruc[:, 8:16], lruc[:, 8:16], ACT.Ln, bias=1.0).then_inc(lambda_log_done, 1)
            act.wait_ge(constants_made, 2)
            for t in range(NT + 1):
                if t < NT:
                    act.wait_ge(tile_loaded[t % 2], 16 * xl_count[t])
                    act_square(act, t)
                    act_root(act, t)
                if t >= 1:
                    if t == 1:
                        act.wait_ge(scales_done, 1)
                    act_blocks(act, t - 1, 0, 0, t - 1, 2 * ((t - 1) % 2))
            for j in range(n_even_jobs):
                if jobs[j][3] == "act":
                    act_even_job(act, own, j)
                elif jobs[j][0] == "dec":
                    act_decay(act, own, jobs[j][1])
            act_gla(act, own)
            act_wout(act, own, 0)
            act_moe(act, 0)
            act_odd(act, own)
            act_wout(act, own, 1)
            act_moe(act, 1)
            act_final(act)

        @block.vector
        def _(dve):
            own = Chain(dve, vector_own)
            dve.wait_ge(vectors_transposed, 1)
            nc.vector.tensor_copy(vcol[:, 0:NVEC], ps[:, 7, 0:NVEC]).then_inc(vectors_copied, 1)
            nc.vector.tensor_copy(adab[:, :], ps[:, 7, P:P + 96]).then_inc(vectors_copied, 1)
            dve.wait_ge(vectors_copied, 2)
            lam = vcol[:, VEC["lam"]:VEC["lam"] + 8]
            nc.vector.scalar_tensor_tensor(out=lruc[:, 8:16], in0=lam, scalar=-1.0, in1=lam,
                                           op0=ALU.mult, op1=ALU.max).then_inc(lambda_abs_done, 1)
            own.do(nc.vector.tensor_scalar(lruc[:, 0:8], lam, -1.0, 0.0, ALU.mult, ALU.max))
            dve.wait_ge(lambda_log_done, 1)
            own.do(nc.vector.tensor_tensor(lruc[:, 0:8], lruc[:, 0:8], lruc[:, 8:16], ALU.add))
            nc.vector.tensor_scalar(lruc[:, 16:24], lruc[:, 0:8], -LRU_C, None, ALU.mult)
            nc.vector.tensor_scalar(lruc[:, 0:8], lruc[:, 0:8], LRU_C, None, ALU.mult).then_inc(lru_constants_done, 1)
            dve_norm(dve, own, 0)
            dve_ada_rows(dve, 0)
            dve_ada_columns(dve, 0)
            dve.wait_ge(scales_done, 1)
            for t in range(NT + 1):
                if 1 <= t < NT:
                    dve_norm(dve, own, t)
                if t >= 1:
                    dve_blocks(dve, t - 1, 0, 0, t - 1, 2 * ((t - 1) % 2))
            for pd in range(4):
                dve_decay_in(dve, pd)
                if pd >= 1:
                    dve_decay_out(dve, own, pd - 1)
            dve_decay_out(dve, own, 3)
            for t in range(NT):
                dve.wait_ge(v_tile_done, t + 1)
                nc.vector.tensor_copy(vtok[:, t, :], ps[:, 6 + t % 2, :]).then_inc(v_tile_copied, 1)
            for what, *at in even_order:
                if what == "copy":
                    dve_ada_rows(dve, at[0])
                elif what == "rows":
                    dve_ada_columns(dve, at[0])
                elif what == "job" and jobs[at[0]][3] == "dve":
                    dve_even_job(dve, own, at[0])
            dve_gla(dve, own)
            dve_wout(dve, own, 0)
            dve_moe(dve, 0)
            dve_odd(dve, own)
            dve_wout(dve, own, 1)
            dve_moe(dve, 1)
            dve_final(dve, own)


_INS = ["x", "c", "ctx", "c_ctx", "ada_w", "ada_b", "norm_mix_g", "norm_ffn_g", "norm_final_g",
        "ev_w_in", "ev_conv_w", "ev_conv_b", "ev_decay_up", "ev_decay_b", "ev_norm_g", "ev_w_out",
        "od_w_in", "od_conv_w", "od_conv_b", "od_gate_a_w", "od_gate_a_b", "od_gate_x_w", "od_gate_x_b",
        "od_lambda", "od_sg_norm_g", "od_sg_w", "od_sg_b", "od_w_out",
        "moe_router", "moe_w_gate", "moe_w_up", "moe_w_down"]


def kernel(**inputs):
    import numpy as np
    import concourse.bacc as bacc
    from concourse.bass_utils import run_bass_kernel_spmd

    nc = bacc.Bacc("TRN2", target_bir_lowering=False, num_devices=1)
    arrays, aps = {}, {}
    for name in _INS:
        a = np.ascontiguousarray(inputs[name])
        arrays[f"in_{name}"] = a
        aps[name] = nc.dram_tensor(f"in_{name}", a.shape, mybir.dt.from_np(a.dtype), kind="ExternalInput").ap()
    out = nc.dram_tensor("out_0", (1, LAT, D), F32, kind="ExternalOutput").ap()
    build(nc, aps, out)
    return run_bass_kernel_spmd(nc, [arrays], core_ids=[0]).results[0]["out_0"]
```
